# Optimizing a Trainium2 kernel written in Bass

```python
import jax
import jax.numpy as jnp
from jax import lax
import numpy as np
import math
import jax, jax.numpy as jnp

D_MODEL = 1024
BATCH = 1
SEQ = 512
DEPTH = 2

HEAD_DIM = 64
A_WIDTH = D_MODEL // 2
A_HEADS = A_WIDTH // HEAD_DIM
CHUNK = 128
B_WIDTH = D_MODEL // 2
CONV_WIDTH = 31
IN_WIDTH = 2 * A_WIDTH + 2 * B_WIDTH
ATTN_HEADS = D_MODEL // HEAD_DIM
DILATED_PATTERNS = ((128, 1), (512, 4), (2048, 16))
BLOCK = 128
ROPE_THETA = 10000.0
D_FF = 2816
FFN_CONV_WIDTH = 3
EPS = 1e-6
NEG = -1e30


def rms_norm(x, g):
    xf = x.astype(jnp.float32)
    y = xf * lax.rsqrt(jnp.mean(xf * xf, axis=-1, keepdims=True) + EPS)
    return (y * g.astype(jnp.float32)).astype(x.dtype)

def layer_norm(x, g, b):
    xf = x.astype(jnp.float32)
    mu = jnp.mean(xf, axis=-1, keepdims=True)
    var = jnp.mean(jnp.square(xf - mu), axis=-1, keepdims=True)
    y = (xf - mu) * lax.rsqrt(var + EPS)
    return (y * g.astype(jnp.float32) + b.astype(jnp.float32)).astype(x.dtype)

def causal_dwconv(x, w, b):
    k = w.shape[0]
    y = lax.conv_general_dilated(
        x, w[:, None, :].astype(x.dtype), window_strides=(1,),
        padding=[(k - 1, 0)], dimension_numbers=('NWC', 'WIO', 'NWC'),
        feature_group_count=x.shape[-1])
    return y + b.astype(x.dtype)

def rotary(x, pos):
    half = x.shape[-1] // 2
    inv = ROPE_THETA ** (-jnp.arange(half, dtype=jnp.float32) / half)
    ang = pos.astype(jnp.float32)[:, None] * inv[None, :]
    cos = jnp.cos(ang)[None, :, None, :]
    sin = jnp.sin(ang)[None, :, None, :]
    xf = x.astype(jnp.float32)
    x1, x2 = xf[..., :half], xf[..., half:]
    out = jnp.concatenate([x1 * cos - x2 * sin, x2 * cos + x1 * sin], axis=-1)
    return out.astype(x.dtype)

def chunked_spatial_gating(z, ln_g, ln_b, w_s, b_s):
    u, v = jnp.split(z, 2, axis=-1)
    v = layer_norm(v, ln_g, ln_b)
    bn, s, _ = v.shape
    v = v.reshape(bn, s // CHUNK, CHUNK, A_HEADS, HEAD_DIM)
    causal = jnp.tril(jnp.ones((CHUNK, CHUNK), dtype=bool))
    w = jnp.where(causal, w_s, jnp.zeros_like(w_s))
    mixed = jnp.einsum('hts,bcshd->bcthd', w, v) + b_s.T[None, None, :, :, None]
    return u * mixed.reshape(bn, s, A_WIDTH)

def conformer_conv(z, conv_w, conv_b, ln_g, ln_b):
    a, g = jnp.split(z, 2, axis=-1)
    h = a * jax.nn.sigmoid(g)
    h = causal_dwconv(h, conv_w, conv_b)
    h = layer_norm(h, ln_g, ln_b)
    return jax.nn.silu(h)

def dilated_branch(q, k, v, window, dilation):
    bn, s, h, dh = q.shape
    span = dilation * BLOCK
    s_pad = -(-s // span) * span
    seq_len = s_pad // dilation
    nb = seq_len // BLOCK
    reach = window // dilation

    def strided(t):
        t = jnp.pad(t, [(0, 0), (0, s_pad - s), (0, 0), (0, 0)])
        t = t.reshape(bn, seq_len, dilation, h, dh).transpose(0, 2, 1, 3, 4)
        return t.reshape(bn, dilation, nb, BLOCK, h, dh)

    def with_prev(t):
        prev = jnp.pad(t, [(0, 0), (0, 0), (1, 0), (0, 0), (0, 0), (0, 0)])[:, :, :-1]
        return jnp.concatenate([prev, t], axis=3)

    qs = strided(q)
    kw = with_prev(strided(k))
    vw = with_prev(strided(v))
    qi = jnp.arange(BLOCK)[:, None]
    kj = jnp.arange(2 * BLOCK)[None, :]
    dist = BLOCK + qi - kj
    band = (dist >= 0) & (dist <= reach)
    blk = jnp.arange(nb)[:, None, None]
    valid = band[None] & ((blk > 0) | (kj[None] >= BLOCK))

    scores = jnp.einsum('brnqhd,brnkhd->brnhqk', qs, kw).astype(jnp.float32)
    scores = scores * (HEAD_DIM ** -0.5)
    scores = jnp.where(valid[None, None, :, None], scores, NEG)
    m = jnp.max(scores, axis=-1, keepdims=True)
    p = jnp.exp(scores - m)
    l = jnp.sum(p, axis=-1, keepdims=True)
    o = jnp.einsum('brnhqk,brnkhd->brnqhd', p / l, vw.astype(jnp.float32))
    lse = (m + jnp.log(l))[..., 0]

    o = o.reshape(bn, dilation, seq_len, h, dh).transpose(0, 2, 1, 3, 4)
    o = o.reshape(bn, s_pad, h, dh)[:, :s]
    lse = lse.transpose(0, 1, 2, 4, 3).reshape(bn, dilation, seq_len, h)
    lse = lse.transpose(0, 2, 1, 3).reshape(bn, s_pad, h)[:, :s]
    return o, lse

def dilated_attention(q, k, v):
    outs, lses = [], []
    for window, dilation in DILATED_PATTERNS:
        o, lse = dilated_branch(q, k, v, window, dilation)
        outs.append(o)
        lses.append(lse)
    wts = jax.nn.softmax(jnp.stack(lses, axis=0), axis=0)
    return jnp.einsum('pbsh,pbshd->bshd', wts, jnp.stack(outs, axis=0))

def conv_ffn(x, norm_g, w_up, conv_w, conv_b, w_down):
    h = rms_norm(x, norm_g)
    u = causal_dwconv(h @ w_up, conv_w, conv_b)
    gate, val = jnp.split(u, 2, axis=-1)
    return x + (jax.nn.silu(gate) * val) @ w_down

def first_inputs(seed: int = 0) -> dict:
    key = jax.random.key(seed)
    keys = iter(jax.random.split(key, 32))
    n_even = (DEPTH + 1) // 2
    n_odd = DEPTH // 2
    f32 = jnp.float32

    def nrm(shape, scale):
        return jax.random.normal(next(keys), shape, f32) * scale

    def gain(shape):
        return 1.0 + nrm(shape, 0.02)

    return {
        'x': nrm((BATCH, SEQ, D_MODEL), 1.0),
        'even_norm_g': gain((n_even, D_MODEL)),
        'even_w_in': nrm((n_even, D_MODEL, IN_WIDTH), D_MODEL ** -0.5),
        'even_b_in': nrm((n_even, IN_WIDTH), 0.02),
        'even_v_ln_g': gain((n_even, A_WIDTH)),
        'even_v_ln_b': nrm((n_even, A_WIDTH), 0.02),
        'even_w_s': nrm((n_even, A_HEADS, CHUNK, CHUNK), CHUNK ** -0.5),
        'even_b_s': gain((n_even, A_HEADS, CHUNK)),
        'even_conv_w': nrm((n_even, CONV_WIDTH, B_WIDTH), CONV_WIDTH ** -0.5),
        'even_conv_b': nrm((n_even, B_WIDTH), 0.02),
        'even_conv_ln_g': gain((n_even, B_WIDTH)),
        'even_conv_ln_b': nrm((n_even, B_WIDTH), 0.02),
        'even_w_out': nrm((n_even, A_WIDTH + B_WIDTH, D_MODEL), (A_WIDTH + B_WIDTH) ** -0.5),
        'odd_norm_g': gain((n_odd, D_MODEL)),
        'odd_w_qkv': nrm((n_odd, D_MODEL, 3 * D_MODEL), D_MODEL ** -0.5),
        'odd_w_o': nrm((n_odd, D_MODEL, D_MODEL), D_MODEL ** -0.5),
        'ffn_norm_g': gain((DEPTH, D_MODEL)),
        'ffn_w_up': nrm((DEPTH, D_MODEL, 2 * D_FF), D_MODEL ** -0.5),
        'ffn_conv_w': nrm((DEPTH, FFN_CONV_WIDTH, 2 * D_FF), FFN_CONV_WIDTH ** -0.5),
        'ffn_conv_b': nrm((DEPTH, 2 * D_FF), 0.02),
        'ffn_w_down': nrm((DEPTH, D_FF, D_MODEL), D_FF ** -0.5),
        'final_norm_g': gain((D_MODEL,)),
    }

def first_block(x, even_norm_g, even_w_in, even_b_in, even_v_ln_g, even_v_ln_b,
              even_w_s, even_b_s, even_conv_w, even_conv_b, even_conv_ln_g,
              even_conv_ln_b, even_w_out, odd_norm_g, odd_w_qkv, odd_w_o,
              ffn_norm_g, ffn_w_up, ffn_conv_w, ffn_conv_b, ffn_w_down,
              final_norm_g):
    bn, s, _ = x.shape
    pos = jnp.arange(s)
    for i in range(DEPTH):
        j = i // 2
        if i % 2 == 0:
            h = rms_norm(x, even_norm_g[j])
            z = h @ even_w_in[j] + even_b_in[j]
            za = jax.nn.gelu(z[..., :2 * A_WIDTH])
            zb = z[..., 2 * A_WIDTH:]
            ya = chunked_spatial_gating(za, even_v_ln_g[j], even_v_ln_b[j],
                                        even_w_s[j], even_b_s[j])
            yb = conformer_conv(zb, even_conv_w[j], even_conv_b[j],
                                even_conv_ln_g[j], even_conv_ln_b[j])
            x = x + jnp.concatenate([ya, yb], axis=-1) @ even_w_out[j]
        else:
            h = rms_norm(x, odd_norm_g[j])
            qkv = (h @ odd_w_qkv[j]).reshape(bn, s, 3, ATTN_HEADS, HEAD_DIM)
            q = rotary(qkv[:, :, 0], pos)
            k = rotary(qkv[:, :, 1], pos)
            v = qkv[:, :, 2]
            o = dilated_attention(q, k, v).astype(x.dtype).reshape(bn, s, D_MODEL)
            x = x + o @ odd_w_o[j]
        x = conv_ffn(x, ffn_norm_g[i], ffn_w_up[i], ffn_conv_w[i], ffn_conv_b[i],
                     ffn_w_down[i])
    return rms_norm(x, final_norm_g)


NSA_Q_HEADS = 6
NSA_KV_HEADS = 2
NSA_HPG = NSA_Q_HEADS // NSA_KV_HEADS
NSA_WIDTH = NSA_Q_HEADS * HEAD_DIM
N_BRANCH = 3
NSA_KV_COLS = N_BRANCH * 2 * NSA_KV_HEADS * HEAD_DIM
CMP_BLOCK = 32
CMP_STRIDE = 16
CMP_HIDDEN = 64
SEL_BLOCK = 64
SEL_TOP_N = 16
WINDOW = 512
FORCE_SCORE = 1.0e4
GLA_HEADS = 6
GLA_DK = 32
GLA_DV = 64
GLA_WIDTH = GLA_HEADS * GLA_DV
GLA_GATE_RANK = 16
GLA_GATE_NORM = 16.0
GLA_CHUNK = 64
POOL_WINDOWS = (2, 4, 8, 16)
POOL_GROUPS = 4
POOL_GROUP = 64
POOL_WIDTH = POOL_GROUPS * POOL_GROUP
MIX_WIDTH = NSA_WIDTH + GLA_WIDTH + POOL_WIDTH
SPLIT_SIZES = (NSA_WIDTH, NSA_KV_COLS, NSA_Q_HEADS * N_BRANCH,
               GLA_HEADS * GLA_DK, GLA_HEADS * GLA_DK, GLA_WIDTH, GLA_GATE_RANK, GLA_WIDTH,
               POOL_WIDTH)
P_IN = sum(SPLIT_SIZES)
D_FF_2 = 4 * D_MODEL
ROPE_THETA_2 = 500000.0
ROPE_DIM = HEAD_DIM // 4
Q_BLOCK = 128
SEL_Q_BLOCK = 32
LN_EPS = 1e-5
RMS_EPS = 1e-6
DEEPNORM_ALPHA = (2 * DEPTH) ** 0.25
DEEPNORM_BETA = (8 * DEPTH) ** -0.25


def partial_rope(x, pos):
    half = ROPE_DIM // 2
    inv = ROPE_THETA_2 ** (-jnp.arange(half, dtype=jnp.float32) * 2.0 / ROPE_DIM)
    ang = pos.astype(jnp.float32)[:, None] * inv[None, :]
    cos = jnp.cos(ang).astype(x.dtype)
    sin = jnp.sin(ang).astype(x.dtype)
    x1, x2, xp = x[..., :half], x[..., half:ROPE_DIM], x[..., ROPE_DIM:]
    return jnp.concatenate([x1 * cos - x2 * sin, x1 * sin + x2 * cos, xp], axis=-1)

def layer_norm_2(x, g, b):
    xf = x.astype(jnp.float32)
    mu = jnp.mean(xf, -1, keepdims=True)
    var = jnp.mean(jnp.square(xf - mu), -1, keepdims=True)
    return ((xf - mu) * lax.rsqrt(var + LN_EPS)).astype(x.dtype) * g + b

def masked_softmax(s, mask):
    s = jnp.where(mask, s.astype(jnp.float32), -jnp.inf)
    m = jnp.max(s, -1, keepdims=True)
    m = jnp.where(jnp.isfinite(m), m, 0.0)
    e = jnp.exp(s - m)
    return e / jnp.maximum(jnp.sum(e, -1, keepdims=True), 1e-30)

def nsa_mixer(q, kv, gates, cmp_pos, cmp_w1, cmp_w2):
    B, S, _ = q.shape
    G, H, Dh = NSA_KV_HEADS, NSA_HPG, HEAD_DIM
    pos = jnp.arange(S)
    q = q.reshape(B, S, G, H, Dh).transpose(0, 2, 3, 1, 4)
    q = partial_rope(q, pos) * (Dh ** -0.5)
    kv = kv.reshape(B, S, N_BRANCH, 2, G, Dh).transpose(2, 3, 0, 4, 1, 5)

    n_cmp = (S - CMP_BLOCK) // CMP_STRIDE + 1
    blk_idx = CMP_STRIDE * jnp.arange(n_cmp)[:, None] + jnp.arange(CMP_BLOCK)[None, :]

    def compress(t, p, w1, w2):
        tb = t[:, :, blk_idx] + p
        hid = jax.nn.gelu(tb.reshape(B, G, n_cmp, CMP_BLOCK * Dh) @ w1)
        return hid @ w2

    kc = compress(partial_rope(kv[0, 0], pos), cmp_pos[0], cmp_w1[0], cmp_w2[0])
    vc = compress(kv[0, 1], cmp_pos[1], cmp_w1[1], cmp_w2[1])
    s_cmp = jnp.einsum('bghsd,bgnd->bghsn', q, kc)
    cmp_mask = blk_idx[:, -1][None, :] <= pos[:, None]
    p_cmp = masked_softmax(s_cmp, cmp_mask)
    o_cmp = jnp.einsum('bghsn,bgnd->bghsd', p_cmp.astype(vc.dtype), vc)

    n_sel = S // SEL_BLOCK
    n_top = min(SEL_TOP_N, n_sel)
    c_lo = blk_idx[:, 0:1]
    s_lo = (SEL_BLOCK * jnp.arange(n_sel))[None, :]
    overlap = jnp.clip(jnp.minimum(c_lo + CMP_BLOCK, s_lo + SEL_BLOCK) - jnp.maximum(c_lo, s_lo), 0, None)
    cmp_to_sel = overlap.astype(jnp.float32) / CMP_BLOCK
    imp = jnp.einsum('bghsn,nj->bgsj', p_cmp, cmp_to_sel)
    cur = (pos // SEL_BLOCK)[:, None]
    jb = jnp.arange(n_sel)[None, :]
    imp = jnp.where((jb == 0) | (jb == cur) | (jb == cur - 1), FORCE_SCORE, imp)
    imp = jnp.where(jb > cur, -FORCE_SCORE, imp)
    _, sel_idx = lax.top_k(imp, n_top)

    k_slc = partial_rope(kv[1, 0], pos).reshape(B, G, n_sel, SEL_BLOCK, Dh)
    v_slc = kv[1, 1].reshape(B, G, n_sel, SEL_BLOCK, Dh)
    nqb = S // SEL_Q_BLOCK
    q_blk = q.reshape(B, G, H, nqb, SEL_Q_BLOCK, Dh).transpose(3, 0, 1, 2, 4, 5)
    idx_blk = sel_idx.reshape(B, G, nqb, SEL_Q_BLOCK, n_top).transpose(2, 0, 1, 3, 4)
    t_blk = pos.reshape(nqb, SEL_Q_BLOCK)
    bi = jnp.arange(B)[:, None, None, None]
    gi = jnp.arange(G)[None, :, None, None]

    def sel_block(args):
        qb, ib, tb = args
        kb = k_slc[bi, gi, ib]
        vb = v_slc[bi, gi, ib]
        s = jnp.einsum('bghqd,bgqnkd->bghqnk', qb, kb)
        kpos = ib[..., None] * SEL_BLOCK + jnp.arange(SEL_BLOCK)
        m = (kpos <= tb[None, None, :, None, None])[:, :, None]
        s = s.reshape(B, G, H, SEL_Q_BLOCK, n_top * SEL_BLOCK)
        m = m.reshape(B, G, 1, SEL_Q_BLOCK, n_top * SEL_BLOCK)
        p = masked_softmax(s, m).reshape(B, G, H, SEL_Q_BLOCK, n_top, SEL_BLOCK)
        return jnp.einsum('bghqnk,bgqnkd->bghqd', p.astype(vb.dtype), vb)

    o_slc = lax.map(sel_block, (q_blk, idx_blk, t_blk))
    o_slc = o_slc.transpose(1, 2, 3, 0, 4, 5).reshape(B, G, H, S, Dh)

    pad = ((0, 0), (0, 0), (WINDOW, 0), (0, 0))
    k_win = jnp.pad(partial_rope(kv[2, 0], pos), pad)
    v_win = jnp.pad(kv[2, 1], pad)
    nwb = S // Q_BLOCK
    span = WINDOW + Q_BLOCK
    q_wb = q.reshape(B, G, H, nwb, Q_BLOCK, Dh).transpose(3, 0, 1, 2, 4, 5)
    starts = jnp.arange(nwb) * Q_BLOCK

    def win_block(args):
        qb, s0 = args
        kb = lax.dynamic_slice_in_dim(k_win, s0, span, axis=2)
        vb = lax.dynamic_slice_in_dim(v_win, s0, span, axis=2)
        s = jnp.einsum('bghqd,bgkd->bghqk', qb, kb)
        tq = s0 + jnp.arange(Q_BLOCK)
        tk = s0 - WINDOW + jnp.arange(span)
        diff = tq[:, None] - tk[None, :]
        m = (diff >= 0) & (diff < WINDOW) & (tk[None, :] >= 0)
        p = masked_softmax(s, m)
        return jnp.einsum('bghqk,bgkd->bghqd', p.astype(vb.dtype), vb)

    o_win = lax.map(win_block, (q_wb, starts))
    o_win = o_win.transpose(1, 2, 3, 0, 4, 5).reshape(B, G, H, S, Dh)

    gt = jax.nn.sigmoid(gates.reshape(B, S, G, H, N_BRANCH).transpose(0, 2, 3, 1, 4))
    o = gt[..., 0:1] * o_cmp + gt[..., 1:2] * o_slc + gt[..., 2:3] * o_win
    return o.transpose(0, 3, 1, 2, 4).reshape(B, S, NSA_WIDTH)

def gla_mixer(q, k, v, g_lr, og, w_gate2, b_gate, norm_g):
    B, S, _ = q.shape
    Hh, dk, dv, C = GLA_HEADS, GLA_DK, GLA_DV, GLA_CHUNK
    N = S // C
    f32 = jnp.float32
    gk = jax.nn.log_sigmoid((g_lr @ w_gate2 + b_gate).astype(f32)) / GLA_GATE_NORM

    def chunks(t, d):
        return t.astype(f32).reshape(B, N, C, Hh, d).transpose(0, 3, 1, 2, 4)

    qc = chunks(q, dk) * (dk ** -0.5)
    kc = chunks(k, dk)
    vc = chunks(v, dv)
    bcum = jnp.cumsum(chunks(gk, dk), axis=3)
    blast = bcum[:, :, :, -1:]
    q_dec = qc * jnp.exp(bcum)
    k_inv = kc * jnp.exp(-bcum)
    k_end = kc * jnp.exp(blast - bcum)
    causal = jnp.tril(jnp.ones((C, C), bool))
    a = jnp.where(causal, jnp.einsum('bhnid,bhnjd->bhnij', q_dec, k_inv), 0.0)
    o_intra = jnp.einsum('bhnij,bhnjv->bhniv', a, vc)
    d_state = jnp.einsum('bhncd,bhncv->bhndv', k_end, vc)
    decay = jnp.exp(blast[:, :, :, 0])

    def step(s_prev, inp):
        dcy, ds = inp
        return s_prev * dcy[..., None] + ds, s_prev

    _, s_in = lax.scan(step, jnp.zeros((B, Hh, dk, dv), f32),
                       (decay.transpose(2, 0, 1, 3), d_state.transpose(2, 0, 1, 3, 4)))
    s_in = s_in.transpose(1, 2, 0, 3, 4)
    o = o_intra + jnp.einsum('bhncd,bhndv->bhncv', q_dec, s_in)
    o = o * lax.rsqrt(jnp.mean(o * o, -1, keepdims=True) + RMS_EPS)
    o = o.transpose(0, 2, 3, 1, 4).reshape(B, S, GLA_WIDTH).astype(og.dtype)
    return o * norm_g * jax.nn.silu(og)

def pool_mixer(u, w_pool, scale):
    B, S, Cw = u.shape
    uf = u.astype(jnp.float32)
    cs = jnp.pad(jnp.cumsum(uf, axis=1), ((0, 0), (1, 0), (0, 0)))
    win = jnp.repeat(jnp.array(POOL_WINDOWS, jnp.int32), POOL_GROUP)
    t = jnp.arange(S)[:, None]
    lo = jnp.maximum(t + 1 - win[None, :], 0)
    cnt = jnp.minimum(t + 1, win[None, :]).astype(jnp.float32)
    lo_sum = jnp.take_along_axis(cs, jnp.broadcast_to(lo[None], (B, S, Cw)), axis=1)
    pooled = (cs[:, 1:] - lo_sum) / cnt - uf
    y = jnp.einsum('bsgc,gcd->bsgd', pooled.reshape(B, S, POOL_GROUPS, POOL_GROUP).astype(u.dtype), w_pool)
    return y.reshape(B, S, POOL_WIDTH) * scale

def second_inputs(seed: int = 0) -> dict:
    key = jax.random.key(seed)
    ks = jax.random.split(key, 20)
    L, D = DEPTH, D_MODEL
    nrm = lambda k, shape, s: jax.random.normal(k, shape, jnp.float32) * s
    return {
        "x": nrm(ks[0], (BATCH, SEQ, D), 1.0),
        "w_in": nrm(ks[1], (L, D, P_IN), D ** -0.5),
        "cmp_pos": nrm(ks[2], (L, 2, CMP_BLOCK, HEAD_DIM), 0.1),
        "cmp_w1": nrm(ks[3], (L, 2, CMP_BLOCK * HEAD_DIM, CMP_HIDDEN), (CMP_BLOCK * HEAD_DIM) ** -0.5),
        "cmp_w2": nrm(ks[4], (L, 2, CMP_HIDDEN, HEAD_DIM), CMP_HIDDEN ** -0.5),
        "gla_w_gate2": nrm(ks[5], (L, GLA_GATE_RANK, GLA_HEADS * GLA_DK), GLA_GATE_RANK ** -0.5),
        "gla_b_gate": nrm(ks[6], (L, GLA_HEADS * GLA_DK), 0.01),
        "gla_norm_g": 1.0 + nrm(ks[7], (L, GLA_WIDTH), 0.02),
        "pool_w": nrm(ks[8], (L, POOL_GROUPS, POOL_GROUP, POOL_GROUP), POOL_GROUP ** -0.5),
        "pool_scale": 1.0 + nrm(ks[9], (L, POOL_WIDTH), 0.02),
        "w_out": nrm(ks[10], (L, MIX_WIDTH, D), MIX_WIDTH ** -0.5 * DEEPNORM_BETA),
        "ln1_g": 1.0 + nrm(ks[11], (L, D), 0.02),
        "ln1_b": nrm(ks[12], (L, D), 0.02),
        "w_up": nrm(ks[13], (L, D, D_FF_2), D ** -0.5),
        "w_down": nrm(ks[14], (L, D_FF_2, D), D_FF_2 ** -0.5 * DEEPNORM_BETA),
        "ln2_g": 1.0 + nrm(ks[15], (L, D), 0.02),
        "ln2_b": nrm(ks[16], (L, D), 0.02),
    }

def second_block(x, w_in, cmp_pos, cmp_w1, cmp_w2, gla_w_gate2, gla_b_gate, gla_norm_g, pool_w, pool_scale,
              w_out, ln1_g, ln1_b, w_up, w_down, ln2_g, ln2_b):
    split_points = []
    acc = 0
    for sz in SPLIT_SIZES[:-1]:
        acc += sz
        split_points.append(acc)
    h = x
    for l in range(DEPTH):
        proj = h @ w_in[l]
        nq, nkv, ngate, gq, gk, gv, glr, gog, pu = jnp.split(proj, split_points, axis=-1)
        mixed = jnp.concatenate([
            nsa_mixer(nq, nkv, ngate, cmp_pos[l], cmp_w1[l], cmp_w2[l]),
            gla_mixer(gq, gk, gv, glr, gog, gla_w_gate2[l], gla_b_gate[l], gla_norm_g[l]),
            pool_mixer(pu, pool_w[l], pool_scale[l]),
        ], axis=-1)
        h = layer_norm_2(DEEPNORM_ALPHA * h + mixed @ w_out[l], ln1_g[l], ln1_b[l])
        ff = jnp.square(jax.nn.relu(h @ w_up[l])) @ w_down[l]
        h = layer_norm_2(DEEPNORM_ALPHA * h + ff, ln2_g[l], ln2_b[l])
    return h


def setup_inputs(seed=0):
    out = dict(first_inputs(seed))
    for name, value in second_inputs(seed + 1).items():
        if name != "x":
            out[name + "_2"] = value
    return out


def reference(
    x, even_norm_g, even_w_in, even_b_in, even_v_ln_g, even_v_ln_b, even_w_s, even_b_s,
    even_conv_w, even_conv_b, even_conv_ln_g, even_conv_ln_b, even_w_out, odd_norm_g, odd_w_qkv,
    odd_w_o, ffn_norm_g, ffn_w_up, ffn_conv_w, ffn_conv_b, ffn_w_down, final_norm_g, w_in_2,
    cmp_pos_2, cmp_w1_2, cmp_w2_2, gla_w_gate2_2, gla_b_gate_2, gla_norm_g_2, pool_w_2,
    pool_scale_2, w_out_2, ln1_g_2, ln1_b_2, w_up_2, w_down_2, ln2_g_2, ln2_b_2,
):
    x = first_block(
        x, even_norm_g, even_w_in, even_b_in, even_v_ln_g, even_v_ln_b, even_w_s, even_b_s,
        even_conv_w, even_conv_b, even_conv_ln_g, even_conv_ln_b, even_w_out, odd_norm_g,
        odd_w_qkv, odd_w_o, ffn_norm_g, ffn_w_up, ffn_conv_w, ffn_conv_b, ffn_w_down,
        final_norm_g,
    )
    return second_block(
        x, w_in_2, cmp_pos_2, cmp_w1_2, cmp_w2_2, gla_w_gate2_2, gla_b_gate_2, gla_norm_g_2,
        pool_w_2, pool_scale_2, w_out_2, ln1_g_2, ln1_b_2, w_up_2, w_down_2, ln2_g_2, ln2_b_2,
    )


_drawn_inputs = setup_inputs


def setup_inputs(seed=0):
    import zlib

    import numpy as np

    out = dict(_drawn_inputs(seed))
    spreads = {}
    factors = {'even_norm_g': 2.928,
     'even_b_in': 2.966,
     'even_v_ln_g': 8.0,
     'even_v_ln_b': 8.0,
     'even_b_s': 5.792,
     'even_conv_ln_g': 4.707,
     'even_conv_ln_b': 5.315,
     'odd_norm_g': 8.0,
     'ffn_norm_g': 2.909,
     'ffn_conv_b': 2.888,
     'cmp_pos_2': 22.687,
     'gla_b_gate_2': 8.0,
     'gla_norm_g_2': 23.32,
     'pool_scale_2': 22.406,
     'cmp_w1_2': 2.687}
    for name, (base, spread) in spreads.items():
        noise = np.random.default_rng([zlib.crc32(name.encode()), seed]).standard_normal(out[name].shape)
        drawn = base * np.exp(spread * noise) if base else spread * noise
        out[name] = jnp.asarray(drawn.astype(out[name].dtype))
    for name, factor in factors.items():
        out[name] = (out[name] * factor).astype(out[name].dtype)
    return out
```

```python
from contextlib import ExitStack

import numpy as np

import concourse.bass as bass
from concourse import mybir

F32 = mybir.dt.float32
F32R = mybir.dt.float32r
I32 = mybir.dt.int32
ALU = mybir.AluOpType
ACT = mybir.ActivationFunctionType
AX = mybir.AxisListType

P = 128
T = 512
TT = T // P
D = 1024
DC = D // P
HALF = D // 2
HC = HALF // P
TAPS = 31
PAD = TAPS - 1
FF = 2816
FC = FF // P
FF2 = 4096
F2C = FF2 // P
F2H = F2C // 2
HD = 64
PAIRS = D // P
NSA_PAIRS = 3
N_CMP = 31
CMP_BLOCK, CMP_STRIDE = 32, 16
GLA_CHUNK = 64
GLA_CHUNKS = T // GLA_CHUNK
DEPTH2 = 2
EPS = 1e-6
LN_EPS = 1e-5
ALPHA = float((2 * DEPTH2) ** 0.25)
BIG = 1.0e30
SCORE_SCALE = HD ** -0.5

(Z_GATE, Z_KC, Z_VC, Z_KS, Z_VS, Z_KW, Z_VW, Z_Q, Z_GV, Z_GK, Z_GQ, Z_PU, Z_OG) = (
    0, 1, 2, 3, 4, 5, 6, 7, 10, 13, 15, 17, 19)
Z_TILES = 22
RANK = 16
GLA_DK, GLA_DV = 32, 64
GK = 3 * GLA_DK
POOL_PAD = 16
GATE_ROW = 32

E_IN = 0
E_OUT = E_IN + 16
F_UP = [E_OUT + DC, 0]
F_DOWN = [F_UP[0] + 2 * FC, 0]
O_QKV = F_DOWN[0] + FC
O_OUT = O_QKV + 3 * PAIRS
F_UP[1] = O_OUT + DC
F_DOWN[1] = F_UP[1] + 2 * FC
L_IN = [F_DOWN[1] + FC, 0]
L_SLOTS = Z_TILES + DC + 2 * F2C
L_IN[1] = L_IN[0] + L_SLOTS
SLOTS = L_IN[1] + L_SLOTS

VECS = [("even_norm_g", DC), ("even_b_in", 16), ("even_v_ln_g", HC), ("even_v_ln_b", HC),
        ("even_conv_w", HC * TAPS), ("even_conv_b", HC), ("even_conv_ln_g", HC), ("even_conv_ln_b", HC),
        ("odd_norm_g", DC), ("final_norm_g", DC)]
for _l in range(2):
    VECS += [(f"ffn_norm_g{_l}", DC), (f"ffn_conv{_l}", 2 * FC * 4)]
for _l in range(DEPTH2):
    VECS += [(f"gla_norm_g{_l}", 3), (f"pool_scale{_l}", 2), (f"ln1_g{_l}", DC), (f"ln1_b{_l}", DC),
             (f"ln2_g{_l}", DC), (f"ln2_b{_l}", DC)]
VEC_AT = {}
VEC_COLS = 0
for _n, _w in VECS:
    VEC_AT[_n] = VEC_COLS
    VEC_COLS += _w

TABLES = [("identity", P), ("ones", P), ("swap", P), ("swap2", P), ("cumulate", P), ("head_mean", P),
          ("dilated", T), ("causal", T), ("cos", T), ("sin", T), ("cos2", T), ("sin2", T),
          ("cmp_mask", TT * N_CMP), ("inv_count", 2 * POOL_PAD),
          ("inv_window", 2), ("bias_row", 1), ("gla_mask", P)]
TAB_AT = {}
TAB_COLS = 0
for _n, _w in TABLES:
    TAB_AT[_n] = (TAB_COLS, _w)
    TAB_COLS += _w

UNIT0 = [PAIRS, PAIRS + 2 * NSA_PAIRS]
UNITS = 2 * NSA_PAIRS

ADD = {n: 2 * HC + DC * i for i, n in enumerate(f"ln{a}_{l}" for l in range(DEPTH2) for a in (1, 2))}
ORDER = (2, 3, 4, 5, 6, 7, 0, 1)
NORM, _at = {}, 0
for _i, (_n, _w) in enumerate([("even", DC), ("v", HC), ("conv", HC), ("f0", DC), ("odd", DC), ("f1", DC), ("final", DC)]
                              + [(f"ln{a}_{l}", DC) for l in range(DEPTH2) for a in (1, 2)]):
    NORM[_n] = (_at, _i)
    _at += _w
ROWS, _at = {}, 0
for _n, _w in [("v", HC), ("conv", HC), ("final", DC)] + [(f"ln{a}_{l}", DC) for l in range(DEPTH2) for a in (1, 2)]:
    ROWS[_n] = _at
    _at += _w
H_FILL = {n: DC * i for i, n in enumerate(
    ["even", "even_out", "f0", "odd", "f1"] + [f"{a}{l}" for l in range(DEPTH2) for a in ("in", "out", "up")])}
XR = {n: DC * i for i, n in enumerate(["f0", "odd", "f1", "final"] + [f"{a}{l}" for l in range(DEPTH2) for a in ("ln1_", "half", "ln2_")])}


def make_tables():
    t = {}
    i = np.arange(P)
    t["identity"] = np.eye(P)
    t["ones"] = np.ones((P, P))
    swap = np.zeros((P, P))
    swap2 = np.zeros((P, P))
    half, half2 = HD // 2, 8
    for base in (0, HD):
        for d in range(half):
            swap[base + half + d, base + d] = -1.0
            swap[base + d, base + half + d] = 1.0
        for d in range(half2):
            swap2[base + half2 + d, base + d] = -1.0
            swap2[base + d, base + half2 + d] = 1.0
    t["swap"], t["swap2"] = swap, swap2
    pos = np.arange(T, dtype=np.float32)
    inv = (np.float32(10000.0) ** (-np.arange(half, dtype=np.float32) / np.float32(half))).astype(np.float32)
    ang = (pos[None, :] * inv[:, None]).astype(np.float32)
    t["cos"] = np.tile(np.cos(ang), (4, 1))
    t["sin"] = np.tile(np.sin(ang), (4, 1))
    inv2 = (np.float32(500000.0) ** (-np.arange(half2, dtype=np.float32) * np.float32(2.0) / np.float32(16))).astype(np.float32)
    ang2 = (pos[None, :] * inv2[:, None]).astype(np.float32)
    cos2, sin2 = np.ones((HD, T)), np.zeros((HD, T))
    cos2[:half2], cos2[half2:2 * half2] = np.cos(ang2), np.cos(ang2)
    sin2[:half2], sin2[half2:2 * half2] = np.sin(ang2), np.sin(ang2)
    t["cos2"], t["sin2"] = np.tile(cos2, (2, 1)), np.tile(sin2, (2, 1))
    same = (i[:, None] // GLA_CHUNK) == (i[None, :] // GLA_CHUNK)
    t["cumulate"] = same & (i[:, None] <= i[None, :])
    t["gla_mask"] = same & (i[:, None] <= i[None, :])
    t["head_mean"] = ((i[:, None] // HD) == (i[None, :] // HD)) / HD
    dist = P * (3 - np.arange(T)[None, :] // P) + i[:, None] - np.arange(T)[None, :] % P
    count = (dist <= 128) * 1 + (dist % 4 == 0) + (dist % 16 == 0)
    count = np.where(dist >= 0, count, 0)
    t["dilated"] = np.where(count > 0, -np.log(np.maximum(count, 1)), BIG)
    t["causal"] = np.where(dist >= 0, 0.0, BIG)
    token = P * np.arange(TT)[None, :, None] + i[:, None, None]
    last = CMP_STRIDE * np.arange(N_CMP)[None, None, :] + CMP_BLOCK - 1
    t["cmp_mask"] = np.where(last <= token, 0.0, BIG).reshape(P, TT * N_CMP)
    count, window = np.zeros((P, 2, POOL_PAD)), np.zeros((P, 2))
    for g, w in enumerate((2, 4, 8, 16)):
        rows = slice(HD * (g % 2), HD * (g % 2) + HD)
        count[rows, g // 2, :] = 1.0 / np.minimum(np.arange(POOL_PAD) + 1, w)
        window[rows, g // 2] = 1.0 / w
    t["inv_count"], t["inv_window"] = count, window
    t["bias_row"] = (i == RANK) * 1.0
    return np.concatenate([np.asarray(t[n], np.float32).reshape(P, w) for n, w in TABLES], axis=1)


def program(nc, wstream, xt, vecs, tables, spatial_w, spatial_b, gate_w, pool_w, cmp_w1, cmp_w2, cmp_p, out):
    with ExitStack() as ctx:
        def sb(name, shape, dt=F32, scope=ctx):
            return scope.enter_context(nc.sbuf_tensor(name, shape, dt))

        def sem(name):
            return ctx.enter_context(nc.semaphore(name))

        PS = ctx.enter_context(nc.psum_tensor("PS", [P, 8, T], F32))
        X = sb("X", [P, DC, T])
        HH = sb("HH", [P, DC, T], F32R)
        HL = sb("HL", [P, DC, T], F32R)
        RAW = sb("RAW", [P, 2, D])
        WH = sb("WH", [P, 2, D], F32R)
        WL = sb("WL", [P, 2, D], F32R)
        VEC = sb("VEC", [P, VEC_COLS])
        TAB = sb("TAB", [P, TAB_COLS])
        MU = sb("MU", [P, T])
        VAR = sb("VAR", [P, T])
        RSTD = sb("RSTD", [P, T])

        def vec(name, j=0):
            return VEC[:, VEC_AT[name] + j:VEC_AT[name] + j + 1]

        def tab(name):
            at, w = TAB_AT[name]
            return TAB[:, at:at + w]

        with ExitStack() as even:
            NB = sb("NB", [P, DC, T], scope=even)
            CB = sb("CB", [P, HC, PAD + T], scope=even)
            CONV = sb("CONV", [P, HC, T], scope=even)
            SIG = sb("SIG", [P, T], scope=even)
            U = sb("U", [P, HC, T], scope=even)
            V = sb("V", [P, HC, T], scope=even)
            VTOK = sb("VTOK", [P, TT, HALF], scope=even)
            WS = sb("WS", [P, 2 * HC, P], scope=even)
            BS = sb("BS", [P, HC, P], scope=even)
            MIX = sb("MIX", [P, 2, T], scope=even)
            Y = sb("Y", [P, DC, T], scope=even)
            ZE = sb("ZE", [P, 2, T], scope=even)
            RSTDV = sb("RSTDV", [P, T], scope=even)
        with ExitStack() as ffn:
            NBF = sb("NBF", [P, DC, T], scope=ffn)
            MH = sb("MH", [P, FC, T], F32R, scope=ffn)
            ML = sb("ML", [P, FC, T], F32R, scope=ffn)
        ACCS = NBF[:, 0:2, :]
        SG = NBF[:, 2, :]
        MID = NBF[:, 3, :]
        ZF = NBF[:, 4:6, :]
        with ExitStack() as odd:
            NBO = sb("NBO", [P, DC, T], scope=odd)
            COSR, SINR = NBO[:, 0, :], NBO[:, 1, :]
            QRAW = sb("QRAW", [P, T], scope=odd)
            KRAW = sb("KRAW", [P, T], scope=odd)
            VRAW = sb("VRAW", [P, T], scope=odd)
            QR = sb("QR", [P, T], scope=odd)
            KR = sb("KR", [P, T], scope=odd)
            RT = sb("RT", [P, 2, T], scope=odd)
            VT = sb("VT", [P, TT, P], scope=odd)
            PB = sb("PB", [P, 2, 1280], scope=odd)
            PT = sb("PT", [P, 2, 1280], scope=odd)
            NEGMAX = sb("NEGMAX", [P, 8], scope=odd)
            SUM = sb("SUM", [P, 8], scope=odd)
            RCP = sb("RCP", [P, 8], scope=odd)
            OH = sb("OH", [P, PAIRS, T], F32R, scope=odd)
            OL = sb("OL", [P, PAIRS, T], F32R, scope=odd)

        with ExitStack() as mixer:
            ZT = sb("ZT", [P, Z_TILES, T], scope=mixer)
            GW = sb("GW", [RANK + 1, 2 * GK], scope=mixer)
            PW = sb("PW", [P, 2, P], scope=mixer)
            W2 = sb("W2", [P, 2, P], scope=mixer)
            CP = sb("CP", [P, 2, CMP_BLOCK], scope=mixer)
            GT = sb("GT", [P, TT, 3 * 2 * NSA_PAIRS], scope=mixer)
            VTS = sb("VTS", [P, 2, TT, P], scope=mixer)
            HID = sb("HID", [P, 2, N_CMP], scope=mixer)
            KCS = sb("KCS", [P, N_CMP], scope=mixer)
            VCS = sb("VCS", [N_CMP, P], scope=mixer)
            PC = sb("PC", [P, 8, N_CMP], scope=mixer)
            CM = sb("CM", [P, 8], scope=mixer)
            CS = sb("CS", [P, 8], scope=mixer)
            NEGMAX2 = sb("NEGMAX2", [P, 8], scope=mixer)
            SUM2 = sb("SUM2", [P, 8], scope=mixer)
            RCP2 = sb("RCP2", [P, 8], scope=mixer)
            GVTOK = sb("GVTOK", [P, TT, 6 * GLA_DV], scope=mixer)
            LS = sb("LS", [P, TT, 2 * GK], scope=mixer)
            BC = sb("BC", [GK, 2, T], scope=mixer)
            GA = sb("GA", [GK, 2, T], scope=mixer)
            GB = sb("GB", [GK, 2, T], scope=mixer)
            DEC = sb("DEC", [GK, 2, GLA_CHUNKS], scope=mixer)
            ST = sb("ST", [GK, 2, GLA_CHUNKS, GLA_DV], scope=mixer)
            AT = sb("AT", [P, 2, T], scope=mixer)
            PU = sb("PU", [P, 2, POOL_PAD + T], scope=mixer)
            PA = sb("PA", [P, POOL_PAD + T], scope=mixer)
            PD = sb("PD", [P, POOL_PAD + T], scope=mixer)
            with ExitStack() as compress:
                W1 = sb("W1", [P, 2, CMP_BLOCK, HD], scope=compress)
                TB = sb("TB", [P, CMP_BLOCK, N_CMP], scope=compress)
            with ExitStack() as attend:
                PB2 = sb("PB2", [P, 2, 1280], scope=attend)
                PT2 = sb("PT2", [P, 2, 1280], scope=attend)
        KTOK = LS
        PTC = ZT[0:N_CMP, Z_GATE:Z_GATE + 2, :]
        NSA_OUT = (Z_VC, Z_VS, Z_VW)
        with ExitStack() as ffn2:
            NB2 = sb("NB2", [P, DC, T], scope=ffn2)
            RB = sb("RB", [P, 2, T], scope=ffn2)
            SB = sb("SB", [P, 2, T], scope=ffn2)
            MH2 = sb("MH2", [P, F2H, T], F32R, scope=ffn2)
            ML2 = sb("ML2", [P, F2H, T], F32R, scope=ffn2)

        w_loaded = [sem("w_loaded0"), sem("w_loaded1")]
        w_hi = sem("w_hi")
        w_lo = sem("w_lo")
        tile_done = sem("tile_done")
        x_loaded = sem("x_loaded")
        c_loaded = sem("c_loaded")
        s_loaded = sem("s_loaded")
        out_stored = sem("out_stored")
        y_done = sem("y_done")
        x_ready = sem("x_ready")
        h_hi = sem("h_hi")
        h_lo = sem("h_lo")
        n_sq = sem("n_sq")
        n_sum = sem("n_sum")
        n_add = sem("n_add")
        n_cent = sem("n_cent")
        n_var = sem("n_var")
        n_std = sem("n_std")
        n_row = sem("n_row")
        e_pad = sem("e_pad")
        e_mask = sem("e_mask")
        e_z = sem("e_z")
        e_sig = sem("e_sig")
        e_glu = sem("e_glu")
        e_gelu = sem("e_gelu")
        e_conv = sem("e_conv")
        e_vaff = sem("e_vaff")
        e_vt = sem("e_vt")
        e_vtok = sem("e_vtok")
        e_mix = sem("e_mix")
        e_y = sem("e_y")
        f_z = sem("f_z")
        f_acc = sem("f_acc")
        f_conv = sem("f_conv")
        f_silu = sem("f_silu")
        f_mid = sem("f_mid")
        f_mhi = sem("f_mhi")
        f_mlo = sem("f_mlo")
        o_raw = sem("o_raw")
        o_v = sem("o_v")
        o_perm = sem("o_perm")
        o_rope = sem("o_rope")
        o_vt = sem("o_vt")
        o_hi = sem("o_hi")
        o_lo = sem("o_lo")
        at_s = sem("at_s")
        at_max = sem("at_max")
        at_exp = sem("at_exp")
        at_p = sem("at_p")
        at_pt = sem("at_pt")
        at_ptc = sem("at_ptc")
        at_o = sem("at_o")

        m_loaded = sem("m_loaded")
        m_zero = sem("m_zero")
        z_kept = sem("z_kept")
        x_new = sem("x_new")
        g_logit = sem("g_logit")
        g_gate = sem("g_gate")
        g_sig = sem("g_sig")
        g_soft = sem("g_soft")
        g_ls = sem("g_ls")
        g_cum = sem("g_cum")
        g_grow = sem("g_grow")
        g_diff = sem("g_diff")
        g_end = sem("g_end")
        g_q = sem("g_q")
        g_inv = sem("g_inv")
        g_ke = sem("g_ke")
        g_ki = sem("g_ki")
        g_kt = sem("g_kt")
        g_vt = sem("g_vt")
        g_ktok = sem("g_ktok")
        g_vtok = sem("g_vtok")
        g_ds = sem("g_ds")
        g_st = sem("g_st")
        g_at = sem("g_at")
        g_am = sem("g_am")
        g_o = sem("g_o")
        g_ok = sem("g_ok")
        g_ms = sem("g_ms")
        g_var = sem("g_var")
        g_sd = sem("g_sd")
        g_sil = sem("g_sil")
        g_y = sem("g_y")
        r_swap = sem("r_swap")
        r_done = sem("r_done")
        v_turn = sem("v_turn")
        v_kept = sem("v_kept")
        c_tb = sem("c_tb")
        c_hid = sem("c_hid")
        c_gelu = sem("c_gelu")
        c_kv = sem("c_kv")
        c_kept = sem("c_kept")
        c_s = sem("c_s")
        c_sm = sem("c_sm")
        c_x = sem("c_x")
        c_p = sem("c_p")
        c_t = sem("c_t")
        c_ptc = sem("c_ptc")
        c_v = sem("c_v")
        c_acc = sem("c_acc")
        u_acc = sem("u_acc")
        p_sum = sem("p_sum")
        p_lin = sem("p_lin")
        p_y = sem("p_y")
        q_relu = sem("q_relu")
        q_sq = sem("q_sq")
        q_hi = sem("q_hi")
        q_lo = sem("q_lo")

        ROW_AT = {3: 0, 2: 512, 0: 896, 1: 1024}
        COL_AT = {0: 0, 1: 512, 3: 896, 2: 1024}

        def head_banks(e):
            return PS[:, 2 + 3 * e:5 + 3 * e, :].rearrange("p a b -> p (a b)")

        block = ctx.enter_context(nc.Block())

        @block.sync
        def _(sp):
            sp.dma_start(X[:, 0:4, :], xt[:, 0:4, :]).then_inc(x_loaded, 16)
            sp.dma_start(X[:, 4:8, :], xt[:, 4:8, :]).then_inc(x_loaded, 16)
            sp.dma_start(VEC[:], vecs).then_inc(c_loaded, 16)
            for b in range(2):
                sp.dma_start(RAW[:, b, :], wstream[b * P:(b + 1) * P, :]).then_inc(w_loaded[b], 16)
            sp.dma_start(TAB[:], tables).then_inc(c_loaded, 16)
            sp.dma_start(WS[:], spatial_w).then_inc(s_loaded, 16)
            sp.dma_start(BS[:], spatial_b).then_inc(s_loaded, 16)
            with sp.Fori(1, SLOTS // 2) as i:
                for b in range(2):
                    sp.wait_ge(w_lo, 2 * i + b - 1)
                    sp.dma_start(RAW[:, b, :], wstream[bass.ds((2 * i + b) * P, P), :]).then_inc(w_loaded[b], 16)
            sp.wait_ge(x_new, DC * 2 * DEPTH2)
            sp.dma_start(out, X[:]).then_inc(out_stored, 16)
            sp.wait_ge(out_stored, 16)

        @block.gpsimd
        def _(pool):
            pool.memset(CB[:, :, 0:PAD], 0.0).then_inc(e_pad, 1)
            pool.wait_ge(s_loaded, 32)
            pool.affine_select(out=WS[:], in_=WS[:], pattern=[[0, 2 * HC], [1, P]], base=0, channel_multiplier=-1,
                               compare_op=ALU.is_ge, fill=0.0).then_inc(e_mask, 1)

            for l in range(DEPTH2):
                pool.wait_ge(h_lo, H_FILL[f"in{l}"] + DC)
                for dst, src in ((GW, gate_w), (PW, pool_w), (W2, cmp_w2), (CP, cmp_p), (W1, cmp_w1)):
                    pool.dma_start(dst[:], src[l]).then_inc(m_loaded, 16)
                pool.memset(PU[:, :, 0:POOL_PAD], 0.0)
                pool.memset(AT[:], 0.0).then_inc(m_zero, 1)
                for n in range(2):
                    pool.wait_ge(z_kept, Z_TILES * l + Z_PU + n + 1)
                    if n:
                        pool.drain()
                    src, width = PU[:, n, :], 1
                    for dst in (PA, PD) if n == 0 else (PA, PD, PA, PD):
                        first = 2 * width - 1
                        pool.tensor_tensor(dst[:, first:], src[:, first:], src[:, first - width:POOL_PAD + T - width], ALU.add)
                        pool.drain()
                        src, width = dst, 2 * width
                    for half, win in ((0, PA), (1, PD)):
                        rows = slice(half * HD, (half + 1) * HD)
                        early = tab("inv_count")[rows, n * POOL_PAD:(n + 1) * POOL_PAD]
                        pool.tensor_tensor(win[rows, 0:POOL_PAD], win[rows, POOL_PAD:2 * POOL_PAD], early, ALU.mult)
                        pool.drain()
                        pool.tensor_scalar(win[rows, 2 * POOL_PAD:], win[rows, 2 * POOL_PAD:],
                                           tab("inv_window")[rows, n:n + 1], None, ALU.mult)
                        pool.drain()
                        u = PU[rows, n, :]
                        pool.tensor_tensor(u[:, POOL_PAD:2 * POOL_PAD], win[rows, 0:POOL_PAD], u[:, POOL_PAD:2 * POOL_PAD],
                                           ALU.subtract)
                        last = pool.tensor_tensor(u[:, 2 * POOL_PAD:], win[rows, 2 * POOL_PAD:], u[:, 2 * POOL_PAD:],
                                                  ALU.subtract)
                    last.then_inc(p_sum, 1)

        @block.scalar
        def _(act):
            def split_hi(i, c, first=False):
                b = c % 2
                act.wait_ge(w_loaded[b], 16 * (i + c // 2 + 1))
                if not first:
                    act.wait_ge(tile_done, 2 * i + c - 1)
                act.activation(WH[:, b, :], RAW[:, b, :], ACT.Copy).then_inc(w_hi, 1)

            def squares(buf, src, order, ready, base):
                for q, n in enumerate(order):
                    act.wait_ge(ready, base + q + 1)
                    act.activation(buf[:, n, :], src[:, n, :], ACT.Square).then_inc(n_sq, 1)

            def root(inst):
                act.wait_ge(n_var, inst + 1)
                act.activation(VAR[:], VAR[:], ACT.Sqrt).then_inc(n_std, 1)

            def rows_hi(buf, base):
                for n in range(DC):
                    act.wait_ge(n_row, base + n + 1)
                    act.activation(HH[:, n, :], buf[:, n, :], ACT.Copy).then_inc(h_hi, 1)

            def fill_scaled(buf, gain, ready, counts):
                for n in range(DC):
                    act.wait_ge(ready, counts[n])
                    act.activation(HH[:, n, :], X[:, n, :], ACT.Identity, scale=vec(gain, n)).then_inc(h_hi, 1)
                    act.activation(buf[:, n, :], X[:, n, :], ACT.Square).then_inc(n_sq, 1)

            split_hi(0, 0, first=True)
            split_hi(0, 1, first=True)
            act.wait_ge(c_loaded, 16)
            fill_scaled(NB, "even_norm_g", x_loaded, [16] * (DC // 2) + [32] * (DC // 2))
            root(NORM["even"][1])
            for j in range(HC):
                split_hi(0, 2 * j + 2)
                split_hi(0, 2 * j + 3)
                act.wait_ge(e_z, 2 * j + 2)
                if j:
                    act.wait_ge(e_glu, j)
                act.activation(SIG[:], ZE[:, 1, :], ACT.Sigmoid, bias=vec("even_b_in", 12 + j)).then_inc(e_sig, 1)
            for j in range(2 * HC):
                s = 2 * HC + j
                split_hi(0, s + 2)
                if j == 6:
                    root(NORM["v"][1])
                act.wait_ge(e_z, s + 1)
                dst = V[:, j, :] if j < HC else U[:, j - HC, :]
                act.activation(dst, ZE[:, s % 2, :], ACT.Gelu_apprx_tanh,
                               bias=vec("even_b_in", 4 + j if j < HC else j - HC)).then_inc(e_gelu, 1)
                if j == 5:
                    squares(NB, V, range(HC), n_cent, 0)
            for n in range(HC):
                act.wait_ge(n_row, ROWS["v"] + n + 1)
                act.activation(V[:, n, :], NB[:, n, :], ACT.Identity, scale=vec("even_v_ln_g", n),
                               bias=vec("even_v_ln_b", n)).then_inc(e_vaff, 1)
            for t in range(TT):
                act.wait_ge(e_vt, t + 1)
                act.activation(VTOK[:, t, :], PS[:, 4 + t, :], ACT.Copy).then_inc(e_vtok, 1)
            for n in range(HC):
                act.wait_ge(e_y, n + 1)
                act.activation(HH[:, n, :], Y[:, n, :], ACT.Copy).then_inc(h_hi, 1)
            squares(NB, CONV, range(HC), n_cent, HC)
            root(NORM["conv"][1])
            for n in range(HC):
                act.wait_ge(n_row, ROWS["conv"] + n + 1)
                act.activation(Y[:, HC + n, :], NB[:, n, :], ACT.Silu, scale=vec("even_conv_ln_g", n),
                               bias=vec("even_conv_ln_b", n))
                act.drain()
                act.activation(HH[:, HC + n, :], Y[:, HC + n, :], ACT.Copy).then_inc(h_hi, 1)
            for k in range(2, DC + 1):
                split_hi(0, E_OUT + k)

            def conv_ffn(l):
                base = F_UP[l] // 2
                cv = f"ffn_conv{l}"
                fill_scaled(NBF, f"ffn_norm_g{l}", x_ready, range(XR[f"f{l}"] + 1, XR[f"f{l}"] + DC + 1))
                split_hi(base, 1)
                root(NORM[f"f{l}"][1])

                def last_tap(i, b, first=False):
                    if b == 0 and not first:
                        act.wait_ge(f_silu, FC * l + i)
                    w = VEC[:, bass.ds(VEC_AT[cv] + 8 * i + 4 * b, 4)]
                    act.wait_ge(f_z, 2 * FC * l + 2 * i + b + 1)
                    act.activation(ACCS[:, b, :], ZF[:, b, :], ACT.Identity, scale=w[:, 2:3], bias=w[:, 3:4]).then_inc(f_acc, 1)

                def gate(i):
                    act.wait_ge(f_conv, 2 * FC * l + 2 * i + 1)
                    act.activation(SG[:], ACCS[:, 0, :], ACT.Silu).then_inc(f_silu, 1)

                def high(i):
                    act.wait_ge(f_mid, FC * l + i + 1)
                    act.activation(MH[:, bass.ds(i, 1), :], MID[:], ACT.Copy).then_inc(f_mhi, 1)

                split_hi(base, 2)
                last_tap(0, 0, first=True)
                split_hi(base, 3)
                last_tap(0, 1)
                gate(0)
                with act.Fori(1, FC) as i:
                    split_hi(base + i, 2)
                    last_tap(i, 0)
                    high(i - 1)
                    split_hi(base + i, 3)
                    last_tap(i, 1)
                    gate(i)
                high(FC - 1)
                down = F_DOWN[l] // 2
                with act.Fori(1, FC // 2) as i:
                    for b in range(2):
                        split_hi(down + i, b)
                split_hi(down + FC // 2, 0)

            conv_ffn(0)

            def exps(u, PB=PB, NEGMAX=NEGMAX, SUM=SUM):
                for e in range(2):
                    for i in range(TT):
                        w = (i + 1) * P
                        act.wait_ge(at_max, 8 * u + 4 * e + i + 1)
                        row = PB[:, e, ROW_AT[i]:ROW_AT[i] + w]
                        act.activation(row, row, ACT.Exp, scale=-1.0, bias=NEGMAX[:, 4 * e + i:4 * e + i + 1],
                                       accum_out=SUM[:, 4 * e + i:4 * e + i + 1]).then_inc(at_exp, 1)

            def keep_pt(u, PT=PT):
                for e in range(2):
                    act.wait_ge(at_pt, 2 * u + e + 1)
                    act.activation(PT[:, e, :], head_banks(e)[:, 0:1280], ACT.Copy).then_inc(at_ptc, 1)

            fill_scaled(NBO, "odd_norm_g", x_ready, range(XR["odd"] + 1, XR["odd"] + DC + 1))

            def raw_q(m, c, b):
                act.wait_ge(tile_done, O_QKV + 6 * m + c + 1)
                act.activation(QRAW[:], PS[:, b, :], ACT.Copy, scale=-SCORE_SCALE).then_inc(o_raw, 1)

            def raw_k(m, c, b):
                act.wait_ge(tile_done, O_QKV + 6 * m + c + 1)
                act.activation(KRAW[:], PS[:, b, :], ACT.Copy).then_inc(o_raw, 1)

            def keep_vt(j):
                act.wait_ge(o_perm, 3 * j + 3)
                act.activation(VT[:], PS[:, 7, :].rearrange("p (a b) -> p a b", a=TT), ACT.Copy).then_inc(o_vt, 1)

            def heads_out(j):
                act.wait_ge(at_o, j + 1)
                act.activation(OH[:, bass.ds(j, 1), :], PS[:, 2, :], ACT.Copy).then_inc(o_hi, 1)

            base = O_QKV // 2
            split_hi(base, 1)
            raw_q(0, 0, 0)
            root(NORM["odd"][1])
            split_hi(base, 2)
            raw_k(0, 1, 1)
            split_hi(base, 3)
            keep_vt(0)

            def pair_step(m, r):
                j = 2 * m + r
                c = 3 * (r + 1)
                split_hi(base + 3 * m, c + 1)
                exps(j)
                raw_q(m, c, c % 2)
                keep_pt(j)
                split_hi(base + 3 * m, c + 2)
                raw_k(m, c + 1, (c + 1) % 2)
                heads_out(j)
                split_hi(base + 3 * m, c + 3)
                keep_vt(j + 1)

            with act.Fori(0, PAIRS // 2 - 1) as m:
                for r in range(2):
                    pair_step(m, r)
            pair_step(PAIRS // 2 - 1, 0)
            exps(PAIRS - 1)
            keep_pt(PAIRS - 1)
            heads_out(PAIRS - 1)
            for k in range(DC):
                split_hi(0, O_OUT + k + 1)
            conv_ffn(1)

            squares(NBF, X, range(DC), x_ready, XR["final"])
            root(NORM["final"][1])
            rows_hi(X, ROWS["final"])

            def layer_norm(nm, fill):
                squares(NB2, X, range(DC), n_cent, ADD[nm])
                root(NORM[nm][1])
                bias = nm.replace("_", "_b")
                for n in range(DC):
                    act.wait_ge(n_row, ROWS[nm] + n + 1)
                    act.activation(X[:, n, :], NB2[:, n, :], ACT.Identity, bias=vec(bias, n)).then_inc(x_new, 1)
                    if fill is not None:
                        act.activation(HH[:, n, :], NB2[:, n, :], ACT.Identity, bias=vec(bias, n)).then_inc(h_hi, 1)

            def mix_layer(l):
                z0 = L_IN[l]

                def keep(s):
                    split_hi(0, z0 + s + 1)
                    act.wait_ge(tile_done, z0 + s + 1)
                    ps = PS[:, (z0 + s) % 2, :]
                    if s == Z_GATE:
                        ins = act.activation(ZT[:, s, :], ps, ACT.Identity, bias=tab("bias_row"))
                    elif Z_PU <= s < Z_PU + 2:
                        act.wait_ge(m_zero, l + 1)
                        ins = act.activation(PU[:, s - Z_PU, POOL_PAD:], ps, ACT.Copy)
                    else:
                        scale = -SCORE_SCALE if Z_Q <= s < Z_Q + NSA_PAIRS else 1.0
                        ins = act.activation(ZT[:, s, :], ps, ACT.Copy, scale=scale)
                    ins.then_inc(z_kept, 1)

                def gate_logs():
                    act.wait_ge(g_logit, l + 1)
                    ls = LS[:].rearrange("p (a b) c -> p a (b c)", a=2)
                    act.activation(ls, PS[:, 2:4, 0:4 * GK], ACT.Abs)
                    act.drain()
                    act.activation(LS[:], LS[:], ACT.Exp, scale=-1.0)
                    act.drain()
                    act.activation(LS[:], LS[:], ACT.Ln, bias=1.0).then_inc(g_soft, 1)

                def branch_gates():
                    act.wait_ge(g_gate, l + 1)
                    gates = PS[:, 6, :].rearrange("p (a b) -> p a b", a=TT)[:, :, GATE_ROW:GATE_ROW + 6 * NSA_PAIRS]
                    act.activation(GT[:], gates, ACT.Sigmoid).then_inc(g_sig, 1)

                def growth():
                    act.wait_ge(g_cum, l + 1)
                    act.activation(BC[:], PS[0:GK, 4:6, :], ACT.Copy, scale=1.0 / 16)
                    act.drain()
                    act.activation(GA[:], BC[:], ACT.Exp)
                    ends = BC[:].rearrange("p a (c t) -> p a c t", t=GLA_CHUNK)[:, :, :, GLA_CHUNK - 1]
                    act.activation(DEC[:], ends, ACT.Exp).then_inc(g_grow, 1)

                def to_end():
                    act.wait_ge(g_diff, l + 1)
                    act.activation(GB[:], GB[:], ACT.Exp).then_inc(g_end, 1)

                def inverse():
                    act.wait_ge(g_q, l + 1)
                    act.activation(GA[:], BC[:], ACT.Exp, scale=-1.0).then_inc(g_inv, 1)

                def hidden(kv):
                    act.wait_ge(c_hid, 2 * l + kv + 1)
                    act.activation(HID[:, kv, :], PS[:, 2 + kv, 0:N_CMP], ACT.Gelu_apprx_tanh).then_inc(c_gelu, 1)

                def keep_values(b):
                    act.wait_ge(v_turn, 2 * l + b + 1)
                    act.activation(VTS[:, b, :, :], PS[:, 6, :].rearrange("p (a b) -> p a b", a=TT), ACT.Copy).then_inc(v_kept, 1)

                def keep_compressed():
                    act.wait_ge(c_kv, l + 1)
                    act.activation(KCS[:], PS[:, 4, 0:N_CMP], ACT.Copy)
                    act.activation(VCS[:], PS[0:N_CMP, 5, 0:P], ACT.Copy).then_inc(c_kept, 1)

                def cmp_exp(jj):
                    act.wait_ge(c_sm, 2 * (NSA_PAIRS * l + jj) + 2)
                    act.activation(PC[:], PC[:], ACT.Exp, scale=-1.0).then_inc(c_x, 1)

                def cmp_keep(jj):
                    act.wait_ge(c_t, NSA_PAIRS * l + jj + 1)
                    act.activation(PTC, PS[0:N_CMP, 5:7, :], ACT.Copy).then_inc(c_ptc, 1)

                def unit(k):
                    exps(UNIT0[l] + k, PB2, NEGMAX2, SUM2)

                def unit_keep(k):
                    keep_pt(UNIT0[l] + k, PT2)

                def keep_gla_keys():
                    act.wait_ge(g_kt, l + 1)
                    view = KTOK[:].rearrange("p (a b) c -> p a (b c)", a=2)
                    act.activation(view[:, 0, :], PS[:, 4, 0:4 * GK], ACT.Copy)
                    act.activation(view[:, 1, :], PS[:, 7, 0:4 * GK], ACT.Copy).then_inc(g_ktok, 1)

                def keep_gla_values():
                    act.wait_ge(g_vt, l + 1)
                    for n in range(3):
                        ins = act.activation(GVTOK[:, :, n * P:(n + 1) * P],
                                             PS[:, 4 + n, :].rearrange("p (a b) -> p a b", a=TT), ACT.Copy)
                    ins.then_inc(g_vtok, 1)

                def gla_out(n):
                    act.wait_ge(g_o, 3 * l + n + 1)
                    act.activation(ZT[:, Z_GV + n, :], PS[:, 7, :], ACT.Copy)
                    if n:
                        act.wait_ge(g_ms, 3 * l + n)
                    act.activation(SQ, PS[:, 7, :], ACT.Square).then_inc(g_ok, 1)

                def gla_root(n):
                    act.wait_ge(g_var, 3 * l + n + 1)
                    act.activation(VAR[:], VAR[:], ACT.Sqrt).then_inc(g_sd, 1)

                SQ = ZT[:, Z_GATE, :]
                keep(0)
                keep(1)
                gate_logs()
                branch_gates()
                keep(2)
                keep(3)
                growth()
                keep(4)
                to_end()
                hidden(0)
                keep(5)
                keep_values(0)
                keep(6)
                hidden(1)
                keep(7)
                keep_values(1)
                keep_compressed()
                keep(8)
                keep(9)
                keep(10)
                unit(0)
                cmp_exp(0)
                keep(11)
                unit_keep(0)
                keep(12)
                cmp_keep(0)
                cmp_exp(1)
                unit(1)
                keep(13)
                unit_keep(1)
                keep(14)
                cmp_keep(1)
                cmp_exp(2)
                unit(2)
                keep(15)
                unit_keep(2)
                keep(16)
                cmp_keep(2)
                inverse()
                keep_gla_keys()
                unit(3)
                keep(17)
                unit_keep(3)
                keep(18)
                keep_gla_values()
                unit(4)
                keep(19)
                unit_keep(4)
                keep(20)
                unit(5)
                keep(21)
                unit_keep(5)
                act.wait_ge(z_kept, Z_TILES * (l + 1))
                for n in range(3):
                    og = ZT[:, Z_OG + n, :]
                    ins = act.activation(og, og, ACT.Silu)
                ins.then_inc(g_sil, 1)
                for n in range(3):
                    gla_out(n)
                    gla_root(n)
                order = [(g_y, 3 * l + n + 1, ZT[:, Z_GV + n, :]) for n in range(3)]
                order += [(p_y, 2 * l + n + 1, PU[:, n, POOL_PAD:]) for n in range(2)]
                order += [(c_acc, 3 * l + 3, None)] + [(u_acc, UNITS * (l + 1), None)]
                for n, (s, v, src) in enumerate(order[:5]):
                    act.wait_ge(s, v)
                    act.activation(HH[:, n, :], src, ACT.Copy).then_inc(h_hi, 1)
                act.wait_ge(c_acc, 3 * l + 3)
                act.wait_ge(u_acc, UNITS * (l + 1))
                for n in range(3):
                    act.activation(HH[:, 5 + n, :], ZT[:, NSA_OUT[n], :], ACT.Copy).then_inc(h_hi, 1)
                for k in range(DC):
                    split_hi(0, z0 + Z_TILES + k + 1)

            def square_ffn(l):
                for half in range(2):
                    up = L_IN[l] + Z_TILES + DC + half * 2 * F2H
                    done = F2C * l + F2H * half
                    with act.Fori(0, F2H // 2) as i:
                        for b in range(2):
                            split_hi(up // 2 + i, b + 1)
                            act.wait_ge(tile_done, up + 2 * i + b + 1)
                            act.activation(RB[:, b, :], PS[:, b, :], ACT.Relu).then_inc(q_relu, 1)
                            act.wait_ge(q_sq, done + 2 * i + b + 1)
                            act.activation(MH2[:, bass.ds(2 * i + b, 1), :], SB[:, b, :], ACT.Copy).then_inc(q_hi, 1)
                    last = l == DEPTH2 - 1 and half == 1
                    with act.Fori(0, F2H // 2 - (1 if last else 0)) as i:
                        for b in range(2):
                            split_hi((up + F2H) // 2 + i, b + 1)
                    if last:
                        split_hi(0, SLOTS - 1)

            for l in range(DEPTH2):
                mix_layer(l)
                layer_norm(f"ln1_{l}", H_FILL[f"up{l}"])
                square_ffn(l)
                layer_norm(f"ln2_{l}", None if l == DEPTH2 - 1 else H_FILL[f"in{l + 1}"])

        @block.tensor
        def _(pe):
            def project(i, c):
                b = c % 2
                pe.wait_ge(w_lo, 2 * i + c + 1)
                for k in range(DC):
                    w = slice(k * P, (k + 1) * P)
                    pe.matmul(PS[:, b, :], WH[:, b, w], HH[:, k, :], start=(k == 0), stop=False)
                    pe.matmul(PS[:, b, :], WH[:, b, w], HL[:, k, :], start=False, stop=False)
                    last = pe.matmul(PS[:, b, :], WL[:, b, w], HH[:, k, :], start=False, stop=(k == DC - 1))
                last.then_inc(tile_done, 1)

            def add_rows(i, c, rh, rl, first, final, frees=None):
                b = c % 2
                pe.wait_ge(w_lo, 2 * i + c + 1)
                for n in ORDER if first else range(DC):
                    if frees and n in frees:
                        pe.wait_ge(*frees[n])
                    w = slice(n * P, (n + 1) * P)
                    pe.matmul(PS[:, n, :], WH[:, b, w], rh, start=first, stop=False)
                    pe.matmul(PS[:, n, :], WH[:, b, w], rl, start=False, stop=False)
                    last = pe.matmul(PS[:, n, :], WL[:, b, w], rh, start=False, stop=final)
                    if final and n != DC - 1:
                        last.then_inc(y_done, 1)
                last.then_inc(tile_done, 1)

            def sum_rows(buf, order, bank, ready, base, done, free=0):
                for q, n in enumerate(order):
                    pe.wait_ge(ready, base + max(q, free) + 1)
                    pe.matmul(PS[:, bank, :], tab("ones"), buf[:, n, :], start=(q == 0),
                              stop=(q == len(order) - 1)).then_inc(done, 1)

            def first_tile(i, buf, nm, fill):
                pe.wait_ge(w_lo, 2 * i + 1)
                for k in range(DC + 2):
                    if k < DC:
                        w = slice(k * P, (k + 1) * P)
                        pe.wait_ge(h_lo, fill + k + 1)
                        pe.matmul(PS[:, 0, :], WH[:, 0, w], HH[:, k, :], start=(k == 0), stop=False)
                        pe.matmul(PS[:, 0, :], WH[:, 0, w], HL[:, k, :], start=False, stop=False)
                        last = pe.matmul(PS[:, 0, :], WL[:, 0, w], HH[:, k, :], start=False, stop=(k == DC - 1))
                        if k == DC - 1:
                            last.then_inc(tile_done, 1)
                    if k >= 2:
                        n = k - 2
                        pe.wait_ge(n_sq, NORM[nm][0] + n + 1)
                        pe.matmul(PS[:, 2, :], tab("ones"), buf[:, n, :], start=(n == 0), stop=(n == DC - 1)).then_inc(n_sum, 1)

            pe.wait_ge(c_loaded, 32)
            first_tile(0, NB, "even", H_FILL["even"])
            for s in range(1, 16):
                if s >= 2:
                    pe.wait_ge(e_z, s - 1)
                if s == 12:
                    sum_rows(V, range(HC), 2, e_gelu, 0, n_add)
                if s == 14:
                    sum_rows(NB, range(HC), 3, n_sq, NORM["v"][0], n_sum)
                project(0, s)
            for t in range(TT):
                for n in range(HC):
                    pe.wait_ge(e_vaff, n + 1)
                    last = pe.transpose(PS[:, 4 + t, n * P:(n + 1) * P], V[:, n, t * P:(t + 1) * P], tab("identity"))
                last.then_inc(e_vt, 1)
            pe.wait_ge(e_mask, 1)
            pe.wait_ge(e_z, 16)
            for n in range(HC):
                for t in range(TT):
                    pe.wait_ge(e_vtok, t + 1)
                    for e in range(2):
                        h = 2 * n + e
                        last = pe.matmul(PS[e * HD:(e + 1) * HD, n, t * P:(t + 1) * P],
                                         VTOK[:, t, h * HD:(h + 1) * HD], WS[:, h, :], start=True, stop=True)
                last.then_inc(e_mix, 1)
            sum_rows(CONV, range(HC), 4, e_conv, HC * TAPS - HC, n_add)
            sum_rows(NB, range(HC), 5, n_sq, NORM["conv"][0], n_sum)
            pe.wait_ge(n_var, NORM["conv"][1] + 1)
            for k in range(DC):
                pe.wait_ge(h_lo, H_FILL["even_out"] + k + 1)
                add_rows(0, E_OUT + k, HH[:, k, :], HL[:, k, :], k == 0, k == DC - 1)

            def conv_ffn(l):
                base = F_UP[l] // 2
                first_tile(base, NBF, f"f{l}", H_FILL[f"f{l}"])
                project(base, 1)
                with pe.Fori(1, FC) as i:
                    for b in range(2):
                        pe.wait_ge(f_z, 2 * FC * l + 2 * i + b - 1)
                        project(base + i, b)
                down = F_DOWN[l] // 2
                done = 2 * FC * (l + 1)
                for b in range(2):
                    pe.wait_ge(f_mlo, FC * l + b + 1)
                    add_rows(down, b, MH[:, b, :], ML[:, b, :], b == 0, False,
                             {0: (f_z, done - 1), 1: (f_z, done)} if b == 0 else None)
                with pe.Fori(1, FC // 2 - 1) as i:
                    for b in range(2):
                        k = 2 * i + b
                        pe.wait_ge(f_mlo, FC * l + 2 * i + b + 1)
                        add_rows(down + i, b, MH[:, bass.ds(k, 1), :], ML[:, bass.ds(k, 1), :], False, False)
                for b in range(2):
                    k = FC - 2 + b
                    pe.wait_ge(f_mlo, FC * l + k + 1)
                    add_rows(down + FC // 2 - 1, b, MH[:, k, :], ML[:, k, :], False, b == 1)

            conv_ffn(0)

            def scores(e, q, k):
                for i in (3, 2, 0, 1):
                    w = (i + 1) * P
                    last = pe.matmul(head_banks(e)[:, ROW_AT[i]:ROW_AT[i] + w], q[e * HD:(e + 1) * HD, i * P:(i + 1) * P],
                                     k[e * HD:(e + 1) * HD, 0:w], start=True, stop=True)
                last.then_inc(at_s, 1)

            def turn_p(u, PB=PB):
                for e in range(2):
                    pe.wait_ge(at_p, 2 * u + e + 1)
                    for i in range(TT):
                        for k in range(i + 1):
                            at = COL_AT[k] + (i - k) * P
                            last = pe.transpose(head_banks(e)[:, at:at + P],
                                                PB[:, e, ROW_AT[i] + k * P:ROW_AT[i] + (k + 1) * P], tab("identity"))
                    last.then_inc(at_pt, 1)

            def values(u, vt, PT=PT):
                for e in range(2):
                    pe.wait_ge(at_ptc, 2 * u + e + 1)
                    for k in range(TT):
                        last = pe.matmul(PS[e * HD:(e + 1) * HD, 2, k * P:T], vt[:, k, e * HD:(e + 1) * HD],
                                         PT[:, e, COL_AT[k]:COL_AT[k] + (TT - k) * P], start=(k == 0), stop=(k == TT - 1))
                last.then_inc(at_o, 1)

            base = O_QKV // 2

            def swap_q(j):
                pe.wait_ge(o_raw, 2 * j + 1)
                pe.matmul(PS[:, 5, :], tab("swap"), QRAW[:], start=True, stop=True).then_inc(o_perm, 1)

            def swap_k(j):
                pe.wait_ge(o_raw, 2 * j + 2)
                pe.matmul(PS[:, 6, :], tab("swap"), KRAW[:], start=True, stop=True).then_inc(o_perm, 1)

            def turn_v(j):
                pe.wait_ge(o_v, j + 1)
                for t in range(TT):
                    last = pe.transpose(PS[:, 7, t * P:(t + 1) * P], VRAW[:, t * P:(t + 1) * P], tab("identity"))
                last.then_inc(o_perm, 1)

            def pair_scores(j):
                pe.wait_ge(o_rope, 2 * j + 2)
                scores(0, QR, KR)
                pe.wait_ge(o_vt, j + 1)
                scores(1, QR, KR)

            first_tile(base, NBO, "odd", H_FILL["odd"])
            project(base, 1)
            swap_q(0)
            swap_k(0)
            pe.wait_ge(o_raw, 1)
            project(base, 2)
            turn_v(0)
            pair_scores(0)

            def pair_step(m, r):
                j = 2 * m + r
                c = 3 * (r + 1)
                pe.wait_ge(o_raw, 2 * j + 2)
                project(base + 3 * m, c)
                turn_p(j)
                pe.wait_ge(o_v, j + 1)
                project(base + 3 * m, c + 1)
                values(j, VT)
                swap_q(j + 1)
                swap_k(j + 1)
                project(base + 3 * m, c + 2)
                turn_v(j + 1)
                pe.wait_ge(o_lo, j + 1)
                pair_scores(j + 1)

            with pe.Fori(0, PAIRS // 2 - 1) as m:
                for r in range(2):
                    pair_step(m, r)
            pair_step(PAIRS // 2 - 1, 0)
            turn_p(PAIRS - 1)
            values(PAIRS - 1, VT)
            for k in range(DC):
                pe.wait_ge(o_lo, k + 1)
                if k == 0:
                    pe.wait_ge(o_lo, DC)
                add_rows(0, O_OUT + k, OH[:, k, :], OL[:, k, :], k == 0, k == DC - 1)
            conv_ffn(1)

            sum_rows(NBF, range(DC), 2, n_sq, NORM["final"][0], n_sum, free=2)

            def layer_norm(nm):
                sum_rows(X, range(DC), 2, x_ready, XR[nm], n_add, free=2)
                sum_rows(NB2, range(DC), 3, n_sq, NORM[nm][0], n_sum)

            def mix_layer(l):
                z0 = L_IN[l]

                def tile(s):
                    if s == 0:
                        pe.wait_ge(h_lo, H_FILL[f"in{l}"] + DC)
                    if s >= 2:
                        pe.wait_ge(z_kept, Z_TILES * l + s - 1)
                    project(0, z0 + s)

                def kept(s):
                    pe.wait_ge(z_kept, Z_TILES * l + s + 1)

                def gate_logits():
                    kept(Z_GATE)
                    for t in range(TT):
                        last = pe.transpose(PS[:, 6, t * P:(t + 1) * P], ZT[:, Z_GATE, t * P:(t + 1) * P], tab("identity"))
                    last.then_inc(g_gate, 1)
                    pe.wait_ge(m_loaded, 80 * (l + 1))
                    for t in range(TT):
                        last = pe.matmul(PS[:, 2 + t // 2, (t % 2) * 2 * GK:(t % 2 + 1) * 2 * GK],
                                         ZT[0:RANK + 1, Z_GATE, t * P:(t + 1) * P], GW[:], start=True, stop=True)
                    last.then_inc(g_logit, 1)

                def cumulate():
                    pe.wait_ge(g_ls, l + 1)
                    for a in range(2):
                        for t in range(TT):
                            last = pe.matmul(PS[0:GK, 4 + a, t * P:(t + 1) * P], LS[:, t, a * GK:(a + 1) * GK], tab("cumulate"),
                                             start=True, stop=True)
                    last.then_inc(g_cum, 1)

                swaps = [Z_KC, Z_KS, Z_KW] + [Z_Q + n for n in range(NSA_PAIRS)]

                def swap(q):
                    kept(swaps[q])
                    if q:
                        pe.wait_ge(r_done, 6 * l + q)
                    pe.matmul(PS[:, 7, :], tab("swap2"), ZT[:, swaps[q], :], start=True, stop=True).then_inc(r_swap, 1)

                def hidden(kv):
                    pe.wait_ge(c_tb, 2 * l + kv + 1)
                    for g in range(2):
                        rows = slice(g * HD, (g + 1) * HD)
                        for t in range(CMP_BLOCK):
                            last = pe.matmul(PS[rows, 2 + kv, 0:N_CMP], W1[rows, kv, t, :], TB[rows, t, :], start=(t == 0),
                                             stop=(t == CMP_BLOCK - 1))
                    last.then_inc(c_hid, 1)

                def turn_values(b):
                    kept((Z_VS, Z_VW)[b])
                    if b == 0:
                        pe.wait_ge(g_sig, l + 1)
                    else:
                        pe.wait_ge(v_kept, 2 * l + 1)
                    for t in range(TT):
                        last = pe.transpose(PS[:, 6, t * P:(t + 1) * P], ZT[:, (Z_VS, Z_VW)[b], t * P:(t + 1) * P], tab("identity"))
                    last.then_inc(v_turn, 1)

                def compressed():
                    pe.wait_ge(c_gelu, 2 * l + 2)
                    pe.wait_ge(g_grow, l + 1)
                    pe.matmul(PS[:, 4, 0:N_CMP], W2[:, 0, :], HID[:, 0, :], start=True, stop=True)
                    pe.matmul(PS[0:N_CMP, 5, 0:P], HID[:, 1, :], W2[:, 1, :], start=True, stop=True).then_inc(c_kv, 1)

                def cmp_scores(jj):
                    pe.wait_ge(c_kept, l + 1)
                    pe.wait_ge(r_done, 6 * l + 4 + jj)
                    for e in range(2):
                        rows = slice(e * HD, (e + 1) * HD)
                        for i in range(TT):
                            last = pe.matmul(PS[:, (7 if jj else 3, 4)[e], i * N_CMP:(i + 1) * N_CMP], ZT[rows, Z_Q + jj, i * P:(i + 1) * P], KCS[rows, :],
                                             start=True, stop=True)
                    last.then_inc(c_s, 1)

                def cmp_turn(jj):
                    pe.wait_ge(c_p, NSA_PAIRS * l + jj + 1)
                    for q in range(8):
                        last = pe.transpose(PS[0:N_CMP, 5 + q // TT, (q % TT) * P:(q % TT + 1) * P], PC[:, q, :], tab("identity"))
                    last.then_inc(c_t, 1)

                def cmp_values(jj):
                    pe.wait_ge(c_ptc, NSA_PAIRS * l + jj + 1)
                    for e in range(2):
                        last = pe.matmul(PS[e * HD:(e + 1) * HD, 3, :], VCS[:, e * HD:(e + 1) * HD], PTC[:, e, :],
                                         start=True, stop=True)
                    last.then_inc(c_v, 1)

                def unit_scores(k):
                    jj, b = divmod(k, 2)
                    pe.wait_ge(r_done, 6 * l + 6)
                    if k:
                        pe.wait_ge(u_acc, UNITS * l + k)
                    for e in range(2):
                        scores(e, ZT[:, Z_Q + jj, :], ZT[:, (Z_KS, Z_KW)[b], :])

                def unit_values(k):
                    turn_p(UNIT0[l] + k, PB2)
                    values(UNIT0[l] + k, VTS[:, k % 2, :, :], PT2)

                def turn_gla_keys():
                    pe.wait_ge(g_ke, l + 1)
                    for t in range(TT):
                        for a in range(2):
                            at = (t % 2) * 2 * GK + a * GK
                            last = pe.transpose(PS[:, 4 if t < 2 else 7, at:at + GK], GB[:, a, t * P:(t + 1) * P],
                                                tab("identity")[0:GK, 0:GK])
                    last.then_inc(g_kt, 1)

                def turn_gla_values():
                    kept(Z_GV + 2)
                    for n in range(3):
                        for t in range(TT):
                            last = pe.transpose(PS[:, 4 + n, t * P:(t + 1) * P], ZT[:, Z_GV + n, t * P:(t + 1) * P],
                                                tab("identity"))
                    last.then_inc(g_vt, 1)

                def chunk_states():
                    pe.wait_ge(g_ktok, l + 1)
                    pe.wait_ge(g_vtok, l + 1)
                    for a in range(2):
                        for c in range(GLA_CHUNKS - 1):
                            rows = slice((c % 2) * GLA_CHUNK, (c % 2 + 1) * GLA_CHUNK)
                            for h in range(3):
                                k = a * GK + h * GLA_DK
                                v = (3 * a + h) * GLA_DV
                                at = (4 * a + c // 2) * GLA_DV
                                last = pe.matmul(PS[h * GLA_DK:(h + 1) * GLA_DK, 3 + c % 2, at:at + GLA_DV],
                                                 KTOK[rows, c // 2, k:k + GLA_DK], GVTOK[rows, c // 2, v:v + GLA_DV],
                                                 start=True, stop=True)
                    last.then_inc(g_ds, 1)

                def within(n):
                    pe.wait_ge(g_ki, l + 1)
                    if n:
                        pe.wait_ge(g_am, 3 * l + n)
                    for e in range(2):
                        a, h = divmod(2 * n + e, 3)
                        rows = slice(h * GLA_DK, (h + 1) * GLA_DK)
                        for t in range(TT):
                            cols = slice(t * P, (t + 1) * P)
                            last = pe.matmul(PS[:, 5 + e, cols], ZT[rows, Z_GK + a, cols], ZT[rows, Z_GQ + a, cols],
                                             start=True, stop=True)
                    last.then_inc(g_at, 1)

                def gla_values(n):
                    pe.wait_ge(g_am, 3 * l + n + 1)
                    pe.wait_ge(g_st, l + 1)
                    if n:
                        pe.wait_ge(g_ok, 3 * l + n)
                    for e in range(2):
                        a, h = divmod(2 * n + e, 3)
                        rows = slice(h * GLA_DK, (h + 1) * GLA_DK)
                        v = (2 * n + e) * GLA_DV
                        for t in range(TT):
                            pe.matmul(PS[e * HD:(e + 1) * HD, 7, t * P:(t + 1) * P], GVTOK[:, t, v:v + GLA_DV],
                                      AT[:, e, t * P:(t + 1) * P], start=True, stop=False)
                            for c in (2 * t, 2 * t + 1):
                                if c:
                                    cols = slice(c * GLA_CHUNK, (c + 1) * GLA_CHUNK)
                                    last = pe.matmul(PS[e * HD:(e + 1) * HD, 7, cols], ST[rows, a, c, :], ZT[rows, Z_GQ + a, cols],
                                                     start=False, stop=(c == 2 * t + 1))
                    last.then_inc(g_o, 1)

                def gla_squares(n):
                    pe.wait_ge(g_ok, 3 * l + n + 1)
                    if n:
                        pe.wait_ge(g_var, 3 * l + n)
                    pe.matmul(PS[:, 4, :], tab("head_mean"), ZT[:, Z_GATE, :], start=True, stop=True).then_inc(g_ms, 1)

                def pool_mix(n):
                    pe.wait_ge(p_sum, 2 * l + n + 1)
                    pe.matmul(PS[:, (3, 6)[n], :], PW[:, n, :], PU[:, n, POOL_PAD:], start=True, stop=True).then_inc(p_lin, 1)

                tile(0)
                tile(1)
                gate_logits()
                tile(2)
                swap(0)
                tile(3)
                cumulate()
                tile(4)
                swap(1)
                hidden(0)
                tile(5)
                turn_values(0)
                tile(6)
                swap(2)
                hidden(1)
                tile(7)
                turn_values(1)
                compressed()
                tile(8)
                swap(3)
                tile(9)
                swap(4)
                tile(10)
                swap(5)
                cmp_scores(0)
                pe.wait_ge(v_kept, 2 * l + 2)
                pe.wait_ge(c_sm, 6 * l + 1)
                unit_scores(0)
                tile(11)
                unit_values(0)
                cmp_turn(0)
                cmp_scores(1)
                tile(12)
                pe.wait_ge(c_ptc, 3 * l + 1)
                pe.wait_ge(c_sm, 6 * l + 3)
                unit_scores(1)
                tile(13)
                unit_values(1)
                cmp_values(0)
                cmp_turn(1)
                cmp_scores(2)
                tile(14)
                pe.wait_ge(c_acc, 3 * l + 1)
                pe.wait_ge(c_ptc, 3 * l + 2)
                pe.wait_ge(c_sm, 6 * l + 5)
                unit_scores(2)
                tile(15)
                unit_values(2)
                cmp_values(1)
                cmp_turn(2)
                turn_gla_keys()
                tile(16)
                pe.wait_ge(c_acc, 3 * l + 2)
                pe.wait_ge(c_ptc, 3 * l + 3)
                pe.wait_ge(g_ktok, l + 1)
                unit_scores(3)
                tile(17)
                unit_values(3)
                cmp_values(2)
                turn_gla_values()
                tile(18)
                pe.wait_ge(c_acc, 3 * l + 3)
                pe.wait_ge(g_vtok, l + 1)
                unit_scores(4)
                tile(19)
                unit_values(4)
                chunk_states()
                within(0)
                tile(20)
                pe.wait_ge(g_st, l + 1)
                pe.wait_ge(g_am, 3 * l + 1)
                unit_scores(5)
                tile(21)
                unit_values(5)
                gla_values(0)
                within(1)
                gla_squares(0)
                gla_values(1)
                within(2)
                gla_squares(1)
                gla_values(2)
                gla_squares(2)
                pool_mix(0)
                pe.wait_ge(g_am, 3 * l + 3)
                pool_mix(1)
                pe.wait_ge(p_y, 2 * l + 2)
                pe.wait_ge(g_var, 3 * l + 3)
                pe.wait_ge(u_acc, UNITS * (l + 1))
                for k in range(DC):
                    pe.wait_ge(h_lo, H_FILL[f"out{l}"] + k + 1)
                    add_rows(0, z0 + Z_TILES + k, HH[:, k, :], HL[:, k, :], k == 0, k == DC - 1)

            def square_ffn(l):
                pe.wait_ge(h_lo, H_FILL[f"up{l}"] + DC)
                for half in range(2):
                    up = L_IN[l] + Z_TILES + DC + half * 2 * F2H
                    done = F2C * l + F2H * half
                    if half:
                        pe.wait_ge(x_ready, XR[f"half{l}"] + DC)
                    for b in range(2):
                        project(up // 2, b)
                    with pe.Fori(1, F2H // 2) as i:
                        for b in range(2):
                            pe.wait_ge(q_relu, done + 2 * i + b - 1)
                            project(up // 2 + i, b)
                    down = (up + F2H) // 2
                    for b in range(2):
                        pe.wait_ge(q_lo, done + b + 1)
                        add_rows(down, b, MH2[:, b, :], ML2[:, b, :], b == 0, False,
                                 {0: (q_relu, done + F2H - 1), 1: (q_relu, done + F2H)} if b == 0 else None)
                    with pe.Fori(1, F2H // 2 - 1) as i:
                        for b in range(2):
                            k = 2 * i + b
                            pe.wait_ge(q_lo, done + 2 * i + b + 1)
                            add_rows(down + i, b, MH2[:, bass.ds(k, 1), :], ML2[:, bass.ds(k, 1), :], False, False)
                    for b in range(2):
                        k = F2H - 2 + b
                        pe.wait_ge(q_lo, done + k + 1)
                        add_rows(down + F2H // 2 - 1, b, MH2[:, k, :], ML2[:, k, :], False, b == 1)

            for l in range(DEPTH2):
                mix_layer(l)
                layer_norm(f"ln1_{l}")
                square_ffn(l)
                layer_norm(f"ln2_{l}")

        @block.vector
        def _(dve):
            def split_lo(i, c):
                b = c % 2
                dve.wait_ge(w_hi, 2 * i + c + 1)
                dve.tensor_tensor(WL[:, b, :], RAW[:, b, :], WH[:, b, :].bitcast(F32), ALU.subtract).then_inc(w_lo, 1)

            def mean(bank, width, ready, count):
                dve.wait_ge(ready, count)
                dve.tensor_scalar(MU[:], PS[:, bank, :], 1.0 / width, None, ALU.mult)
                dve.drain()

            def centre(buf, order):
                for n in order:
                    dve.tensor_tensor(buf[:, n, :], buf[:, n, :], MU[:], ALU.subtract).then_inc(n_cent, 1)

            def spread(bank, width, eps, nm, chunks, meanwhile=None, rstd=RSTD):
                base, inst = NORM[nm]
                dve.wait_ge(n_sum, base + chunks)
                dve.tensor_scalar(VAR[:], PS[:, bank, :], 1.0 / width, eps, ALU.mult, ALU.add).then_inc(n_var, 1)
                if meanwhile:
                    meanwhile()
                dve.wait_ge(n_std, inst + 1)
                dve.reciprocal(rstd[:], VAR[:])
                dve.drain()

            def rows(buf, src, gain, fill):
                for n in range(DC + 1):
                    if n < DC:
                        dve.scalar_tensor_tensor(buf[:, n, :], src[:, n, :], vec(gain, n), RSTD[:], ALU.mult, ALU.mult)\
                           .then_inc(n_row, 1)
                    if n:
                        low(buf, n - 1, fill)

            def low(buf, n, fill):
                dve.wait_ge(h_hi, fill + n + 1)
                dve.tensor_tensor(HL[:, n, :], buf[:, n, :], HH[:, n, :].bitcast(F32), ALU.subtract).then_inc(h_lo, 1)

            def low_scaled(n, gain, fill):
                dve.wait_ge(h_hi, fill + n + 1)
                dve.scalar_tensor_tensor(HL[:, n, :], X[:, n, :], vec(gain, n), HH[:, n, :].bitcast(F32), ALU.mult,
                                         ALU.subtract).then_inc(h_lo, 1)

            def add_out(out_no, last_slot, scale=None, gain=None, fill=None):
                for n in range(DC):
                    if n < DC - 1:
                        dve.wait_ge(y_done, (DC - 1) * out_no + n + 1)
                    else:
                        dve.wait_ge(tile_done, last_slot + 1)
                    if scale is None:
                        dve.tensor_tensor(X[:, n, :], X[:, n, :], PS[:, n, :], ALU.add).then_inc(x_ready, 1)
                    else:
                        dve.scalar_tensor_tensor(X[:, n, :], X[:, n, :], scale, PS[:, n, :], ALU.mult, ALU.add)\
                           .then_inc(x_ready, 1)
                    if gain and n:
                        low_scaled(n - 1, gain, fill)
                if gain:
                    low_scaled(DC - 1, gain, fill)

            split_lo(0, 0)
            split_lo(0, 1)
            for n in range(DC):
                low_scaled(n, "even_norm_g", H_FILL["even"])
            spread(2, D, EPS, "even", DC)

            def normed(s):
                dve.wait_ge(tile_done, s + 1)
                if s >= 10:
                    dve.wait_ge(e_gelu, s - 9)
                elif s >= 2:
                    dve.wait_ge(e_glu, s // 2)
                dve.tensor_tensor(ZE[:, s % 2, :], PS[:, s % 2, :], RSTD[:], ALU.mult).then_inc(e_z, 1)

            def glu(j):
                dve.wait_ge(e_sig, j + 1)
                if j == 0:
                    dve.wait_ge(e_pad, 1)
                dve.scalar_tensor_tensor(CB[:, j, PAD:], ZE[:, 0, :], vec("even_b_in", 8 + j), SIG[:], ALU.add, ALU.mult)\
                   .then_inc(e_glu, 1)

            def conv_taps(first, last):
                for q in range(first, last):
                    side, k = divmod(q, TAPS)
                    if k == 0:
                        dve.wait_ge(e_glu, 2 * side + 2)
                    for n in (2 * side, 2 * side + 1):
                        src = CB[:, n, k:k + T]
                        w = vec("even_conv_w", n * TAPS + k)
                        if k == 0:
                            ins = dve.tensor_scalar(CONV[:, n, :], src, w, vec("even_conv_b", n), ALU.mult, ALU.add)
                        else:
                            dve.wait_ge(e_conv, 2 * q + n % 2 - 1)
                            ins = dve.scalar_tensor_tensor(CONV[:, n, :], src, w, CONV[:, n, :], ALU.mult, ALU.add)
                        ins.then_inc(e_conv, 1)

            for s in range(4):
                normed(s)
                split_lo(0, s + 2)
                if s % 2:
                    glu(s // 2)
            for s in range(4, 16):
                normed(s)
                split_lo(0, s + 2)
                if s in (5, 7):
                    glu(s // 2)
                if s == 12:
                    mean(2, HALF, n_add, HC)
                    centre(V, range(HC))
                if s == 14:
                    spread(3, HALF, EPS, "v", HC, rstd=RSTDV)
                if s == 15:
                    for n in range(HC):
                        dve.tensor_tensor(NB[:, n, :], V[:, n, :], RSTDV[:], ALU.mult).then_inc(n_row, 1)
                conv_taps(5 * (s - 4), 5 * (s - 3))
            conv_taps(60, 2 * TAPS)
            dve.wait_ge(s_loaded, 32)
            for n in range(HC + 1):
                if n < HC:
                    dve.wait_ge(e_mix, n + 1)
                    dve.tensor_tensor(MIX[:, n % 2, :].rearrange("p (a b) -> p a b", a=TT),
                                      PS[:, n, :].rearrange("p (a b) -> p a b", a=TT),
                                      BS[:, n:n + 1, :].to_broadcast([P, TT, P]), ALU.add)
                    dve.drain()
                    dve.tensor_tensor(Y[:, n, :], MIX[:, n % 2, :], U[:, n, :], ALU.mult).then_inc(e_y, 1)
                if n:
                    low(Y, n - 1, H_FILL["even_out"])
            mean(4, HALF, n_add, 2 * HC)
            centre(CONV, range(HC))
            spread(5, HALF, EPS, "conv", HC, rstd=RSTDV)
            for n in range(HC):
                dve.tensor_tensor(NB[:, n, :], CONV[:, n, :], RSTDV[:], ALU.mult).then_inc(n_row, 1)
            for n in range(HC, DC):
                low(Y, n, H_FILL["even_out"])
            for k in range(2, DC + 1):
                split_lo(0, E_OUT + k)
            add_out(0, E_OUT + DC - 1, gain="ffn_norm_g0", fill=H_FILL["f0"])

            def conv_ffn(l, out_no, gain, fill):
                base = F_UP[l] // 2
                cv = f"ffn_conv{l}"
                split_lo(base, 1)
                spread(2, D, EPS, f"f{l}", DC)

                def normed(i, b, first=False):
                    if not first:
                        dve.wait_ge(f_conv, 2 * FC * l + 2 * i + b - 1)
                    dve.wait_ge(tile_done, 2 * (base + i) + b + 1)
                    dve.tensor_tensor(ZF[:, b, :], PS[:, b, :], RSTD[:], ALU.mult).then_inc(f_z, 1)

                def taps(i, b):
                    w = VEC[:, bass.ds(VEC_AT[cv] + 8 * i + 4 * b, 4)]
                    dve.wait_ge(f_acc, 2 * FC * l + 2 * i + b + 1)
                    for back in (1, 2):
                        acc = ACCS[:, b, back:T]
                        ins = dve.scalar_tensor_tensor(acc, ZF[:, b, 0:T - back], w[:, 2 - back:3 - back], acc, ALU.mult, ALU.add)
                        if back == 1:
                            dve.drain()
                    ins.then_inc(f_conv, 1)

                def gated(i, first=False):
                    if not first:
                        dve.wait_ge(f_mlo, FC * l + i)
                    dve.wait_ge(f_conv, 2 * FC * l + 2 * i + 2)
                    dve.wait_ge(f_silu, FC * l + i + 1)
                    dve.tensor_tensor(MID[:], SG[:], ACCS[:, 1, :], ALU.mult).then_inc(f_mid, 1)

                def gated_low(i):
                    dve.wait_ge(f_mhi, FC * l + i + 1)
                    dve.tensor_tensor(ML[:, bass.ds(i, 1), :], MID[:], MH[:, bass.ds(i, 1), :].bitcast(F32), ALU.subtract)\
                       .then_inc(f_mlo, 1)

                for b in range(2):
                    normed(0, b, first=True)
                    split_lo(base, b + 2)
                    taps(0, b)
                def pair(i, first=False):
                    normed(i, 0)
                    split_lo(base + i, 2)
                    gated(i - 1, first)
                    taps(i, 0)
                    normed(i, 1)
                    split_lo(base + i, 3)
                    taps(i, 1)
                    gated_low(i - 1)

                pair(1, first=True)
                with dve.Fori(2, FC) as i:
                    pair(i)
                gated(FC - 1)
                gated_low(FC - 1)
                down = F_DOWN[l] // 2
                with dve.Fori(1, FC // 2) as i:
                    for b in range(2):
                        split_lo(down + i, b)
                split_lo(down + FC // 2, 0)
                add_out(out_no, F_DOWN[l] + FC - 1, gain=gain, fill=fill)

            conv_ffn(0, 1, "odd_norm_g", H_FILL["odd"])

            def maxima(u, mask, PB=PB, NEGMAX=NEGMAX, SUM=SUM):
                for e in range(2):
                    dve.wait_ge(at_s, 2 * u + e + 1)
                    dve.memset(SUM[:, 4 * e:4 * e + 4], 0.0)
                    for i in range(TT):
                        w = (i + 1) * P
                        row = slice(ROW_AT[i], ROW_AT[i] + w)
                        dve.tensor_tensor_reduce(PB[:, e, row], head_banks(e)[:, row], tab(mask)[:, T - w:T], 1.0, 3.0e38,
                                                 ALU.add, ALU.min, NEGMAX[:, 4 * e + i:4 * e + i + 1]).then_inc(at_max, 1)

            def divide(u, gates=None, PB=PB, SUM=SUM, RCP=RCP):
                for e in range(2):
                    dve.wait_ge(at_exp, 8 * u + 4 * e + 4)
                    dve.reciprocal(RCP[:, 4 * e:4 * e + 4], SUM[:, 4 * e:4 * e + 4])
                    dve.drain()
                    if gates is not None:
                        dve.tensor_tensor(RCP[:, 4 * e:4 * e + 4], RCP[:, 4 * e:4 * e + 4], gates(e), ALU.mult)
                        dve.drain()
                    for i in range(TT):
                        row = PB[:, e, ROW_AT[i]:ROW_AT[i] + (i + 1) * P]
                        ins = dve.tensor_scalar(row, row, RCP[:, 4 * e + i:4 * e + i + 1], None, ALU.mult)
                    ins.then_inc(at_p, 1)

            base = O_QKV // 2

            def rope(dst, src, bank, side):
                dve.tensor_tensor(dst, src, COSR, ALU.mult)
                dve.tensor_tensor(RT[:, side, :], PS[:, bank, :], SINR, ALU.mult)
                dve.drain()
                return dve.tensor_tensor(dst, dst, RT[:, side, :], ALU.add)

            def ropes(j):
                dve.wait_ge(o_perm, 3 * j + 1)
                rope(QR[:], QRAW[:], 5, 0).then_inc(o_rope, 1)
                dve.wait_ge(o_perm, 3 * j + 2)
                rope(KR[:], KRAW[:], 6, 1).then_inc(o_rope, 1)

            def normed_v(m, c, b):
                dve.wait_ge(tile_done, O_QKV + 6 * m + c + 1)
                dve.tensor_tensor(VRAW[:], PS[:, b, :], RSTD[:], ALU.mult).then_inc(o_v, 1)

            def heads_low(j):
                dve.wait_ge(o_hi, j + 1)
                dve.tensor_tensor(OL[:, bass.ds(j, 1), :], PS[:, 2, :], OH[:, bass.ds(j, 1), :].bitcast(F32), ALU.subtract)\
                   .then_inc(o_lo, 1)

            split_lo(base, 1)
            spread(2, D, EPS, "odd", DC, lambda: split_lo(base, 2))
            dve.tensor_tensor(COSR, tab("cos"), RSTD[:], ALU.mult)
            dve.tensor_tensor(SINR, tab("sin"), RSTD[:], ALU.mult)
            dve.drain()
            ropes(0)
            split_lo(base, 3)
            normed_v(0, 2, 0)

            def pair_step(m, r):
                j = 2 * m + r
                c = 3 * (r + 1)
                split_lo(base + 3 * m, c + 1)
                maxima(j, "dilated")
                divide(j)
                split_lo(base + 3 * m, c + 2)
                heads_low(j)
                ropes(j + 1)
                split_lo(base + 3 * m, c + 3)
                normed_v(m, c + 2, c % 2)

            with dve.Fori(0, PAIRS // 2 - 1) as m:
                for r in range(2):
                    pair_step(m, r)
            pair_step(PAIRS // 2 - 1, 0)
            maxima(PAIRS - 1, "dilated")
            divide(PAIRS - 1)
            heads_low(PAIRS - 1)
            for k in range(DC):
                split_lo(0, O_OUT + k + 1)
            add_out(2, O_OUT + DC - 1, gain="ffn_norm_g1", fill=H_FILL["f1"])
            conv_ffn(1, 3, None, None)

            spread(2, D, EPS, "final", DC)
            rows(X, X, "final_norm_g", H_FILL["in0"])

            def layer_norm(nm, fill):
                mean(2, D, n_add, ADD[nm] + DC)
                centre(X, range(DC))
                spread(3, D, LN_EPS, nm, DC)
                gain = nm.replace("_", "_g")
                for n in range(DC + 1):
                    if n < DC:
                        dve.scalar_tensor_tensor(NB2[:, n, :], X[:, n, :], vec(gain, n), RSTD[:], ALU.mult, ALU.mult)\
                           .then_inc(n_row, 1)
                    if n and fill is not None:
                        low(X, n - 1, fill)

            def mix_layer(l):
                z0 = L_IN[l]

                def lo(s):
                    split_lo(0, z0 + s)

                def kept(s):
                    dve.wait_ge(z_kept, Z_TILES * l + s + 1)

                def gate_logs():
                    dve.wait_ge(g_soft, l + 1)
                    ls = LS[:].rearrange("p (a b) c -> p a (b c)", a=2)
                    dve.scalar_tensor_tensor(ls, PS[:, 2:4, 0:4 * GK], 0.0, ls, ALU.min, ALU.subtract).then_inc(g_ls, 1)

                def chunked(x):
                    return x.rearrange("p a (c t) -> p a c t", t=GLA_CHUNK)

                def from_end():
                    dve.wait_ge(g_grow, l + 1)
                    for a in range(2):
                        bc = chunked(BC[:])[:, a]
                        ends = bc[:, :, GLA_CHUNK - 1:GLA_CHUNK].to_broadcast([GK, GLA_CHUNKS, GLA_CHUNK])
                        ins = dve.tensor_tensor(chunked(GB[:])[:, a], ends, bc, ALU.subtract)
                    ins.then_inc(g_diff, 1)

                def decay_queries():
                    kept(Z_GQ + 1)
                    q = ZT[0:GK, Z_GQ:Z_GQ + 2, :]
                    dve.scalar_tensor_tensor(q, q, GLA_DK ** -0.5, GA[:], ALU.mult, ALU.mult).then_inc(g_q, 1)

                def decay_keys():
                    kept(Z_GK + 1)
                    dve.wait_ge(g_end, l + 1)
                    dve.tensor_tensor(GB[:], ZT[0:GK, Z_GK:Z_GK + 2, :], GB[:], ALU.mult).then_inc(g_ke, 1)

                def inverse_keys():
                    dve.wait_ge(g_inv, l + 1)
                    k = ZT[0:GK, Z_GK:Z_GK + 2, :]
                    dve.tensor_tensor(k, k, GA[:], ALU.mult).then_inc(g_ki, 1)

                swaps = [Z_KC, Z_KS, Z_KW] + [Z_Q + n for n in range(NSA_PAIRS)]

                def turn(q):
                    dve.wait_ge(r_swap, 6 * l + q + 1)
                    z = ZT[:, swaps[q], :]
                    dve.tensor_tensor(z, z, tab("cos2"), ALU.mult)
                    dve.tensor_tensor(MU[:], PS[:, 7, :], tab("sin2"), ALU.mult)
                    dve.drain()
                    dve.tensor_tensor(z, z, MU[:], ALU.add).then_inc(r_done, 1)
                    dve.drain()

                def blocks(kv):
                    kept(Z_KC + kv)
                    dve.wait_ge(m_loaded, 80 * (l + 1))
                    if kv:
                        dve.wait_ge(c_hid, 2 * l + 1)
                    z = ZT[:, Z_KC + kv, :].rearrange("p (n s) -> p s n", s=CMP_STRIDE)
                    for part in range(2):
                        js = slice(part * CMP_STRIDE, (part + 1) * CMP_STRIDE)
                        pos = CP[:, kv, js].rearrange("p (s n) -> p s n", n=1).to_broadcast([P, CMP_STRIDE, N_CMP])
                        ins = dve.tensor_tensor(TB[:, js, :], z[:, :, part:part + N_CMP], pos, ALU.add)
                    ins.then_inc(c_tb, 1)

                def cmp_soft(jj):
                    u = NSA_PAIRS * l + jj
                    dve.wait_ge(c_s, u + 1)
                    if jj:
                        dve.wait_ge(c_t, u)
                    for e in range(2):
                        ins = dve.tensor_tensor(PC[:, e * TT:(e + 1) * TT, :].rearrange("p i n -> p (i n)"),
                                                PS[:, (7 if jj else 3, 4)[e], 0:TT * N_CMP], tab("cmp_mask"), ALU.add)
                    ins.then_inc(c_sm, 1)
                    dve.drain()
                    dve.tensor_reduce(CM[:], PC[:], AX.X, ALU.min)
                    dve.drain()
                    dve.tensor_scalar(CM[:], CM[:], 1.0e20, None, ALU.min)
                    dve.drain()
                    least = CM[:].rearrange("p (q n) -> p q n", n=1).to_broadcast([P, 8, N_CMP])
                    dve.tensor_tensor(PC[:], PC[:], least, ALU.subtract).then_inc(c_sm, 1)

                def gate(b, jj, e):
                    return GT[:, :, 3 * (NSA_PAIRS * e + jj) + b]

                def cmp_divide(jj):
                    u = NSA_PAIRS * l + jj
                    dve.wait_ge(c_x, u + 1)
                    dve.tensor_reduce(CS[:], PC[:], AX.X, ALU.add)
                    dve.drain()
                    dve.tensor_scalar(CS[:], CS[:], 1.0e-30, None, ALU.max)
                    dve.drain()
                    dve.reciprocal(CS[:], CS[:])
                    dve.drain()
                    dve.wait_ge(g_sig, l + 1)
                    for e in range(2):
                        dve.tensor_tensor(CS[:, TT * e:TT * e + TT], CS[:, TT * e:TT * e + TT], gate(0, jj, e), ALU.mult)
                    dve.drain()
                    share = CS[:].rearrange("p (q n) -> p q n", n=1).to_broadcast([P, 8, N_CMP])
                    dve.tensor_tensor(PC[:], PC[:], share, ALU.mult).then_inc(c_p, 1)

                def cmp_add(jj):
                    dve.wait_ge(c_v, NSA_PAIRS * l + jj + 1)
                    o = ZT[:, NSA_OUT[jj], :]
                    if jj == 2:
                        ins = dve.tensor_copy(o, PS[:, 3, :])
                    else:
                        ins = dve.tensor_tensor(o, o, PS[:, 3, :], ALU.add)
                    ins.then_inc(c_acc, 1)
                    dve.drain()

                def unit(k):
                    jj, b = divmod(k, 2)
                    maxima(UNIT0[l] + k, "causal", PB2, NEGMAX2, SUM2)
                    divide(UNIT0[l] + k, lambda e: gate(1 + b, jj, e), PB2, SUM2, RCP2)

                def unit_add(k):
                    jj, b = divmod(k, 2)
                    dve.wait_ge(at_o, UNIT0[l] + k + 1)
                    o = ZT[:, NSA_OUT[jj], :]
                    if b == 0 and jj < 2:
                        ins = dve.tensor_copy(o, PS[:, 2, :])
                    else:
                        ins = dve.tensor_tensor(o, o, PS[:, 2, :], ALU.add)
                    ins.then_inc(u_acc, 1)
                    dve.drain()

                def states():
                    dve.wait_ge(g_ds, l + 1)
                    for c in range(GLA_CHUNKS - 1):
                        for a in range(2):
                            ds = PS[0:GK, 3 + c % 2, (4 * a + c // 2) * GLA_DV:(4 * a + c // 2 + 1) * GLA_DV]
                            if c == 0:
                                ins = dve.tensor_copy(ST[:, a, 1, :], ds)
                            else:
                                ins = dve.scalar_tensor_tensor(ST[:, a, c + 1, :], ST[:, a, c, :], DEC[:, a, c:c + 1], ds,
                                                               ALU.mult, ALU.add)
                        if c < GLA_CHUNKS - 2:
                            dve.drain()
                    ins.then_inc(g_st, 1)

                def mask_within(n):
                    dve.wait_ge(g_at, 3 * l + n + 1)
                    dve.wait_ge(m_zero, l + 1)
                    if n:
                        dve.wait_ge(g_o, 3 * l + n)
                    mask = tab("gla_mask").bitcast(I32).rearrange("p (a t) -> p a t", a=1).to_broadcast([P, TT, P])
                    for e in range(2):
                        ins = dve.copy_predicated(AT[:, e, :].rearrange("p (a t) -> p a t", a=TT), mask,
                                                  PS[:, 5 + e, :].rearrange("p (a t) -> p a t", a=TT))
                    ins.then_inc(g_am, 1)

                def gla_norm(n):
                    dve.wait_ge(g_ms, 3 * l + n + 1)
                    dve.tensor_scalar(VAR[:], PS[:, 4, :], EPS, None, ALU.add).then_inc(g_var, 1)
                    dve.wait_ge(g_sd, 3 * l + n + 1)
                    dve.reciprocal(RSTD[:], VAR[:])
                    dve.drain()
                    o = ZT[:, Z_GV + n, :]
                    dve.scalar_tensor_tensor(o, o, vec(f"gla_norm_g{l}", n), RSTD[:], ALU.mult, ALU.mult)
                    dve.drain()
                    dve.wait_ge(g_sil, l + 1)
                    dve.tensor_tensor(o, o, ZT[:, Z_OG + n, :], ALU.mult).then_inc(g_y, 1)

                def pool_scale(n):
                    dve.wait_ge(p_lin, 2 * l + n + 1)
                    dve.tensor_scalar(PU[:, n, POOL_PAD:], PS[:, (3, 6)[n], :], vec(f"pool_scale{l}", n), None, ALU.mult)\
                       .then_inc(p_y, 1)

                lo(1)
                lo(2)
                gate_logs()
                lo(3)
                turn(0)
                blocks(0)
                lo(4)
                from_end()
                lo(5)
                turn(1)
                blocks(1)
                lo(6)
                lo(7)
                turn(2)
                lo(8)
                lo(9)
                turn(3)
                lo(10)
                turn(4)
                lo(11)
                turn(5)
                cmp_soft(0)
                unit(0)
                lo(12)
                cmp_divide(0)
                unit_add(0)
                lo(13)
                cmp_soft(1)
                unit(1)
                lo(14)
                cmp_divide(1)
                unit_add(1)
                cmp_add(0)
                lo(15)
                cmp_soft(2)
                decay_keys()
                unit(2)
                lo(16)
                cmp_divide(2)
                unit_add(2)
                cmp_add(1)
                lo(17)
                decay_queries()
                inverse_keys()
                unit(3)
                lo(18)
                unit_add(3)
                cmp_add(2)
                lo(19)
                unit(4)
                lo(20)
                unit_add(4)
                states()
                mask_within(0)
                lo(21)
                unit(5)
                lo(22)
                unit_add(5)
                for n in range(3):
                    if n < 2:
                        mask_within(n + 1)
                    gla_norm(n)
                for n in range(2):
                    pool_scale(n)
                fill = H_FILL[f"out{l}"]
                for n in range(3):
                    dve.wait_ge(h_hi, fill + n + 1)
                    dve.tensor_tensor(HL[:, n, :], ZT[:, Z_GV + n, :], HH[:, n, :].bitcast(F32), ALU.subtract).then_inc(h_lo, 1)
                for n in range(2):
                    dve.wait_ge(h_hi, fill + 3 + n + 1)
                    dve.tensor_tensor(HL[:, 3 + n, :], PU[:, n, POOL_PAD:], HH[:, 3 + n, :].bitcast(F32), ALU.subtract)\
                       .then_inc(h_lo, 1)
                for n in range(3):
                    dve.wait_ge(h_hi, fill + 5 + n + 1)
                    dve.tensor_tensor(HL[:, 5 + n, :], ZT[:, NSA_OUT[n], :], HH[:, 5 + n, :].bitcast(F32), ALU.subtract)\
                       .then_inc(h_lo, 1)
                for k in range(DC):
                    split_lo(0, z0 + Z_TILES + k + 1)
                add_out(4 + 3 * l, z0 + Z_TILES + DC - 1, ALPHA)

            def square_ffn(l):
                for half in range(2):
                    up = L_IN[l] + Z_TILES + DC + half * 2 * F2H
                    done = F2C * l + F2H * half
                    with dve.Fori(0, F2H // 2) as i:
                        for b in range(2):
                            split_lo(up // 2 + i, b + 1)
                            dve.wait_ge(q_relu, done + 2 * i + b + 1)
                            dve.tensor_tensor(SB[:, b, :], RB[:, b, :], RB[:, b, :], ALU.mult).then_inc(q_sq, 1)
                            dve.wait_ge(q_hi, done + 2 * i + b + 1)
                            dve.tensor_tensor(ML2[:, bass.ds(2 * i + b, 1), :], SB[:, b, :],
                                              MH2[:, bass.ds(2 * i + b, 1), :].bitcast(F32), ALU.subtract).then_inc(q_lo, 1)
                    last = l == DEPTH2 - 1 and half == 1
                    with dve.Fori(0, F2H // 2 - (1 if last else 0)) as i:
                        for b in range(2):
                            split_lo((up + F2H) // 2 + i, b + 1)
                    if last:
                        split_lo(0, SLOTS - 1)
                    add_out(5 + 3 * l + half, up + 2 * F2H - 1, None if half else ALPHA)

            for l in range(DEPTH2):
                mix_layer(l)
                layer_norm(f"ln1_{l}", H_FILL[f"up{l}"])
                square_ffn(l)
                layer_norm(f"ln2_{l}", None if l == DEPTH2 - 1 else H_FILL[f"in{l + 1}"])


def _columns(v):
    return np.asarray(v).reshape(-1, P).T


def _by_columns(w):
    k, n = w.shape
    return w.reshape(k // P, P, n // P, P).transpose(2, 1, 0, 3).reshape(-1, D)


def lay_out(a):
    w_in = a["even_w_in"][0]
    za, zb = w_in[:, :D], w_in[:, D:]
    pairs = [np.concatenate([zb[:, n * P:(n + 1) * P], zb[:, HALF + n * P:HALF + (n + 1) * P]], 1) for n in range(HC)]
    stream = [_by_columns(np.concatenate(pairs + [za[:, HALF:], za[:, :HALF]], 1)), a["even_w_out"][0]]

    def ffn(l):
        up = a["ffn_w_up"][l]
        both = np.stack([up[:, :FF].reshape(D, FC, P), up[:, FF:].reshape(D, FC, P)], 2).reshape(D, 2 * FF)
        return [_by_columns(both), a["ffn_w_down"][l]]

    stream += ffn(0)
    qkv = a["odd_w_qkv"][0].reshape(D, 3, PAIRS, P).transpose(0, 2, 1, 3).reshape(D, 3 * D)
    stream += [_by_columns(qkv), a["odd_w_o"][0]]
    stream += ffn(1)
    for l in range(DEPTH2):
        w = a["w_in_2"][l]
        at = np.cumsum([0, 384, 768, 18, 192, 192, 384, 16, 384, 256])
        q, kv, gates, gq, gk, gv, rank, og, pu = (w[:, at[n]:at[n + 1]] for n in range(9))
        none = np.zeros((D, P), np.float32)
        first = np.concatenate([rank, none[:, :GATE_ROW - RANK], gates, none[:, :P - GATE_ROW - gates.shape[1]]], 1)
        kv = kv.reshape(D, 6, P)
        heads = q.reshape(D, 2, NSA_PAIRS, HD).transpose(0, 2, 1, 3).reshape(D, -1)
        threes = [np.concatenate([g[:, n * GK:(n + 1) * GK], none[:, :P - GK]], 1) for g in (gk, gq) for n in range(2)]
        cols = np.concatenate([first, *(kv[:, n] for n in range(6)), heads, gv, *threes, pu, og], 1)
        w_out = a["w_out_2"][l]
        nsa = w_out[:384].reshape(2, NSA_PAIRS, HD, D).transpose(1, 0, 2, 3).reshape(-1, D)
        up, down = _by_columns(a["w_up_2"][l]), a["w_down_2"][l]
        half = F2H * P
        stream += [_by_columns(cols), w_out[384:], nsa, up[:half], down[:half], up[half:], down[half:]]
    vecs = [_columns(a["even_norm_g"][0]), _columns(a["even_b_in"][0]), _columns(a["even_v_ln_g"][0]),
            _columns(a["even_v_ln_b"][0]),
            a["even_conv_w"][0].reshape(TAPS, HC, P).transpose(2, 1, 0).reshape(P, -1),
            _columns(a["even_conv_b"][0]), _columns(a["even_conv_ln_g"][0]), _columns(a["even_conv_ln_b"][0]),
            _columns(a["odd_norm_g"][0]), _columns(a["final_norm_g"])]
    for l in range(2):
        taps = np.concatenate([a["ffn_conv_w"][l], a["ffn_conv_b"][l][None]], 0)
        vecs += [_columns(a["ffn_norm_g"][l]),
                 taps.reshape(4, 2, FC, P).transpose(3, 2, 1, 0).reshape(P, -1)]
    for l in range(DEPTH2):
        vecs += [_columns(a[n][l]) for n in ("gla_norm_g_2", "pool_scale_2", "ln1_g_2", "ln1_b_2", "ln2_g_2", "ln2_b_2")]
    feeds = {
        "wstream": np.concatenate(stream, 0),
        "xt": a["x"][0].T.reshape(DC, P, T).transpose(1, 0, 2),
        "vecs": np.concatenate(vecs, 1),
        "tables": make_tables(),
        "spatial_w": a["even_w_s"][0].transpose(2, 0, 1),
        "spatial_b": np.repeat(a["even_b_s"][0].reshape(HC, 2, P), HD, 1).transpose(1, 0, 2),
    }
    blocks = np.zeros((DEPTH2, P, 2, P), np.float32)
    second = np.zeros((DEPTH2, P, 2, P), np.float32)
    for g in range(2):
        r = slice(g * HD, (g + 1) * HD)
        for n in range(2):
            blocks[:, r, n, r] = a["pool_w_2"][:, 2 * n + g]
            second[:, r, n, r] = a["cmp_w2_2"][:, n]
    w1 = a["cmp_w1_2"].reshape(DEPTH2, 2, CMP_BLOCK, HD, HD).transpose(0, 3, 1, 2, 4)
    pos = a["cmp_pos_2"].transpose(0, 3, 1, 2)
    feeds |= {
        "gate_w": np.concatenate([a["gla_w_gate2_2"], a["gla_b_gate_2"][:, None]], 1),
        "pool_w": blocks, "cmp_w2": second,
        "cmp_w1": np.concatenate([w1, w1], 1), "cmp_p": np.concatenate([pos, pos], 1),
    }
    return {n: np.ascontiguousarray(v) for n, v in feeds.items()}


def kernel(**inputs):
    import concourse.bacc as bacc
    from concourse.bass_utils import run_bass_kernel_spmd

    feeds = lay_out({n: np.asarray(v) for n, v in inputs.items()})
    nc = bacc.Bacc("TRN2", target_bir_lowering=False, num_devices=1)
    aps = {n: nc.dram_tensor(n, v.shape, F32, kind="ExternalInput").ap() for n, v in feeds.items()}
    out = nc.dram_tensor("out", (P, DC, T), F32, kind="ExternalOutput").ap()
    program(nc, **aps, out=out)
    result = run_bass_kernel_spmd(nc, [feeds], core_ids=[0]).results[0]["out"]
    return result.transpose(1, 0, 2).reshape(D, T).T[None]
```

```python
from contextlib import ExitStack

import numpy as np

import concourse.bass as bass
from concourse import mybir

F32 = mybir.dt.float32
F32R = mybir.dt.float32r
I32 = mybir.dt.int32
ALU = mybir.AluOpType
ACT = mybir.ActivationFunctionType
AX = mybir.AxisListType

P = 128
T = 512
TT = T // P
D = 1024
DC = D // P
X_PARTS = 4
HALF = D // 2
HC = HALF // P
TAPS = 31
PAD = TAPS - 1
DIAG_PARTS = (0, 8, 16, 24, TAPS)
PE_PARTS = (0, 10, 20, TAPS)
FF = 2816
FC = FF // P
FF2 = 4096
F2C = FF2 // P
F2H = F2C // 2
HD = 64
PAIRS = D // P
NSA_PAIRS = 3
N_CMP = 31
CMP_BLOCK, CMP_STRIDE = 32, 16
GLA_CHUNK = 64
GLA_CHUNKS = T // GLA_CHUNK
DEPTH2 = 2
EPS = 1e-6
LN_EPS = 1e-5
ALPHA = float((2 * DEPTH2) ** 0.25)
BIG = 1.0e30
SCORE_SCALE = HD ** -0.5

Z_GATE, Z_KC, Z_VC, Z_GK, Z_GQ, Z_GV, Z_KS, Z_VS = 0, 1, 2, 3, 5, 7, 10, 11
Z_Q, Z_PU = (12, 13, 15), (14, 16)
Z_KW, Z_VW, Z_OG = 17, 18, 19
Z_TILES = 22
RANK = 16
GLA_DK, GLA_DV = 32, 64
GK = 3 * GLA_DK
POOL_PAD = 16
GATE_ROW = 32

SWAPS = ((Z_KC, 7), (Z_KS, 2), (Z_Q[0], 2), (Z_Q[1], 2), (Z_Q[2], 3), (Z_KW, 7))

E_IN = 0
E_OUT = E_IN + 16
F_UP = [E_OUT + DC, 0]
F_DOWN = [F_UP[0] + 2 * FC, 0]
O_QKV = F_DOWN[0] + FC
O_OUT = O_QKV + 3 * PAIRS
F_UP[1] = O_OUT + DC
F_DOWN[1] = F_UP[1] + 2 * FC
L_IN = [F_DOWN[1] + FC, 0]
L_SLOTS = Z_TILES + DC + 2 * F2C
L_IN[1] = L_IN[0] + L_SLOTS
SLOTS = L_IN[1] + L_SLOTS

VECS = [("even_norm_g", DC), ("even_b_in", 16), ("even_v_ln_g", HC), ("even_v_ln_b", HC),
        ("even_conv_w", HC * TAPS), ("even_conv_b", HC), ("even_conv_ln_g", HC), ("even_conv_ln_b", HC),
        ("odd_norm_g", DC), ("final_norm_g", DC)]
for _l in range(2):
    VECS += [(f"ffn_norm_g{_l}", DC), (f"ffn_conv{_l}", 2 * FC * 4)]
for _l in range(DEPTH2):
    VECS += [(f"gla_norm_g{_l}", 3), (f"pool_scale{_l}", 2), (f"ln1_g{_l}", DC), (f"ln1_b{_l}", DC),
             (f"ln2_g{_l}", DC), (f"ln2_b{_l}", DC)]
VEC_AT = {}
VEC_COLS = 0
for _n, _w in VECS:
    VEC_AT[_n] = VEC_COLS
    VEC_COLS += _w

VEC_EVEN = VEC_AT["odd_norm_g"]

TABLES = [("identity", P), ("ones", P), ("swap", P), ("swap2", P), ("cumulate", P), ("head_mean", P),
          ("dilated", T), ("causal", T), ("cos", T), ("sin", T), ("cos2", T), ("sin2", T),
          ("cmp_mask", TT * N_CMP), ("inv_count", 2 * POOL_PAD),
          ("inv_window", 2), ("bias_row", 1), ("gla_mask", P)]
TAB_AT = {}
TAB_COLS = 0
for _n, _w in TABLES:
    TAB_AT[_n] = (TAB_COLS, _w)
    TAB_COLS += _w
TAB_EVEN = TAB_AT["swap"][0]

UNIT0 = [PAIRS, PAIRS + 2 * NSA_PAIRS]
UNITS = 2 * NSA_PAIRS

ADD = {n: 2 * HC + DC * i for i, n in enumerate(f"ln{a}_{l}" for l in range(DEPTH2) for a in (1, 2))}
ORDER = (2, 3, 4, 5, 6, 7, 0, 1)
NORM, _at = {}, 0
for _i, (_n, _w) in enumerate([("even", DC), ("v", HC), ("conv", HC), ("f0", DC), ("odd", DC), ("f1", DC), ("final", DC)]
                              + [(f"ln{a}_{l}", DC) for l in range(DEPTH2) for a in (1, 2)]):
    NORM[_n] = (_at, _i)
    _at += _w
ROWS, _at = {}, 0
for _n, _w in [("v", HC), ("conv", HC), ("final", DC)] + [(f"ln{a}_{l}", DC) for l in range(DEPTH2) for a in (1, 2)]:
    ROWS[_n] = _at
    _at += _w
H_FILL = {n: DC * i for i, n in enumerate(
    ["even", "even_out", "f0", "odd", "f1"] + [f"{a}{l}" for l in range(DEPTH2) for a in ("in", "out", "up")])}
XR = {n: DC * i for i, n in enumerate(["f0", "odd", "f1", "final"] + [f"{a}{l}" for l in range(DEPTH2) for a in ("ln1_", "half", "ln2_")])}


def z_bank(s):
    return (s + (s >= Z_OG)) % 2


def make_tables():
    t = {}
    i = np.arange(P)
    t["identity"] = np.eye(P)
    t["ones"] = np.ones((P, P))
    swap = np.zeros((P, P))
    swap2 = np.zeros((P, P))
    half, half2 = HD // 2, 8
    for base in (0, HD):
        for d in range(half):
            swap[base + half + d, base + d] = -1.0
            swap[base + d, base + half + d] = 1.0
        for d in range(half2):
            swap2[base + half2 + d, base + d] = -1.0
            swap2[base + d, base + half2 + d] = 1.0
    t["swap"], t["swap2"] = swap, swap2
    pos = np.arange(T, dtype=np.float32)
    inv = (np.float32(10000.0) ** (-np.arange(half, dtype=np.float32) / np.float32(half))).astype(np.float32)
    ang = (pos[None, :] * inv[:, None]).astype(np.float32)
    t["cos"] = np.tile(np.cos(ang), (4, 1))
    t["sin"] = np.tile(np.sin(ang), (4, 1))
    inv2 = (np.float32(500000.0) ** (-np.arange(half2, dtype=np.float32) * np.float32(2.0) / np.float32(16))).astype(np.float32)
    ang2 = (pos[None, :] * inv2[:, None]).astype(np.float32)
    cos2, sin2 = np.ones((HD, T)), np.zeros((HD, T))
    cos2[:half2], cos2[half2:2 * half2] = np.cos(ang2), np.cos(ang2)
    sin2[:half2], sin2[half2:2 * half2] = np.sin(ang2), np.sin(ang2)
    t["cos2"], t["sin2"] = np.tile(cos2, (2, 1)), np.tile(sin2, (2, 1))
    same = (i[:, None] // GLA_CHUNK) == (i[None, :] // GLA_CHUNK)
    t["cumulate"] = same & (i[:, None] <= i[None, :])
    t["gla_mask"] = same & (i[:, None] <= i[None, :])
    t["head_mean"] = ((i[:, None] // HD) == (i[None, :] // HD)) / HD
    dist = P * (3 - np.arange(T)[None, :] // P) + i[:, None] - np.arange(T)[None, :] % P
    count = (dist <= 128) * 1 + (dist % 4 == 0) + (dist % 16 == 0)
    count = np.where(dist >= 0, count, 0)
    t["dilated"] = np.where(count > 0, -np.log(np.maximum(count, 1)), BIG)
    t["causal"] = np.where(dist >= 0, 0.0, BIG)
    token = P * np.arange(TT)[None, :, None] + i[:, None, None]
    last = CMP_STRIDE * np.arange(N_CMP)[None, None, :] + CMP_BLOCK - 1
    t["cmp_mask"] = np.where(last <= token, 0.0, BIG).reshape(P, TT * N_CMP)
    count, window = np.zeros((P, 2, POOL_PAD)), np.zeros((P, 2))
    for g, w in enumerate((2, 4, 8, 16)):
        rows = slice(HD * (g % 2), HD * (g % 2) + HD)
        count[rows, g // 2, :] = 1.0 / np.minimum(np.arange(POOL_PAD) + 1, w)
        window[rows, g // 2] = 1.0 / w
    t["inv_count"], t["inv_window"] = count, window
    t["bias_row"] = (i == RANK) * 1.0
    return np.concatenate([np.asarray(t[n], np.float32).reshape(P, w) for n, w in TABLES], axis=1)


def program(nc, wstream, xt, vecs, tables, spatial_w, spatial_b, gate_w, pool_w, cmp_w1, cmp_w2, cmp_p, out):
    with ExitStack() as ctx:
        def sb(name, shape, dt=F32, scope=ctx):
            return scope.enter_context(nc.sbuf_tensor(name, shape, dt))

        def sem(name):
            return ctx.enter_context(nc.semaphore(name))

        PS = ctx.enter_context(nc.psum_tensor("PS", [P, 8, T], F32))
        X = sb("X", [P, DC, T])
        HH = sb("HH", [P, DC, T], F32R)
        HL = sb("HL", [P, DC, T], F32R)
        RAW = sb("RAW", [P, 2, D])
        WH = sb("WH", [P, 2, D], F32R)
        WL = sb("WL", [P, 2, D], F32R)
        VEC = sb("VEC", [P, VEC_COLS])
        TAB = sb("TAB", [P, TAB_COLS])
        MU = sb("MU", [P, T])
        RSTD = sb("RSTD", [P, T])
        STD = sb("STD", [P, T])
        WARM = sb("WARM", [P, len(NORM)])

        def vec(name, j=0):
            return VEC[:, VEC_AT[name] + j:VEC_AT[name] + j + 1]

        def tab(name):
            at, w = TAB_AT[name]
            return TAB[:, at:at + w]

        with ExitStack() as even:
            NB = sb("NB", [P, DC, T], scope=even)
            CB = sb("CB", [P, HC, PAD + T], scope=even)
            CONV = sb("CONV", [P, HC, T], scope=even)
            SIG = sb("SIG", [P, T], scope=even)
            U = sb("U", [P, HC, T], scope=even)
            V = sb("V", [P, HC, T], scope=even)
            VTOK = sb("VTOK", [P, TT, HALF], scope=even)
            WS = sb("WS", [P, 2 * HC, P], scope=even)
            BS = sb("BS", [P, HC, P], scope=even)
            MIX = sb("MIX", [P, 2, T], scope=even)
            Y = sb("Y", [P, DC, T], scope=even)
            ZE = sb("ZE", [P, 2, T], scope=even)
            RSTDV = sb("RSTDV", [P, T], scope=even)
        TAPD = Y[:].rearrange("p a b -> p (a b)")[:, 0:TAPS * P].rearrange("p (k m) -> p k m", m=P)
        with ExitStack() as ffn:
            NBF = sb("NBF", [P, DC, T], scope=ffn)
            MH = sb("MH", [P, FC, T], F32R, scope=ffn)
            ML = sb("ML", [P, FC, T], F32R, scope=ffn)
        ACCS = NBF[:, 0:2, :]
        SG = NBF[:, 2, :]
        MID = NBF[:, 3, :]
        ZF = NBF[:, 4:6, :]
        with ExitStack() as odd:
            NBO = sb("NBO", [P, DC, T], scope=odd)
            COSR, SINR = NBO[:, 0, :], NBO[:, 1, :]
            QRAW = sb("QRAW", [P, T], scope=odd)
            KRAW = sb("KRAW", [P, T], scope=odd)
            VRAW = sb("VRAW", [P, T], scope=odd)
            QR = sb("QR", [P, T], scope=odd)
            KR = sb("KR", [P, T], scope=odd)
            RT = sb("RT", [P, 2, T], scope=odd)
            VT = sb("VT", [P, TT, P], scope=odd)
            PB = sb("PB", [P, 2, 1280], scope=odd)
            PT = sb("PT", [P, 2, 1280], scope=odd)
            NEGMAX = sb("NEGMAX", [P, 8], scope=odd)
            SUM = sb("SUM", [P, 8], scope=odd)
            RCP = sb("RCP", [P, 8], scope=odd)
            OH = sb("OH", [P, PAIRS, T], F32R, scope=odd)
            OL = sb("OL", [P, PAIRS, T], F32R, scope=odd)

        with ExitStack() as mixer:
            ZT = sb("ZT", [P, Z_TILES, T], scope=mixer)
            GW = sb("GW", [RANK + 1, 2 * GK], scope=mixer)
            PW = sb("PW", [P, 2, P], scope=mixer)
            W2 = sb("W2", [P, 2, P], scope=mixer)
            CP = sb("CP", [P, 2, CMP_BLOCK], scope=mixer)
            GT = sb("GT", [P, TT, 3 * 2 * NSA_PAIRS], scope=mixer)
            VTS = sb("VTS", [P, 2, TT, P], scope=mixer)
            HID = sb("HID", [P, 2, N_CMP], scope=mixer)
            KCS = sb("KCS", [P, N_CMP], scope=mixer)
            VCS = sb("VCS", [N_CMP, P], scope=mixer)
            PC = sb("PC", [P, 8, N_CMP], scope=mixer)
            CM = sb("CM", [P, 8], scope=mixer)
            CS = sb("CS", [P, 8], scope=mixer)
            NEGMAX2 = sb("NEGMAX2", [P, 8], scope=mixer)
            SUM2 = sb("SUM2", [P, 8], scope=mixer)
            RCP2 = sb("RCP2", [P, 8], scope=mixer)
            GVTOK = sb("GVTOK", [P, TT, 6 * GLA_DV], scope=mixer)
            LS = sb("LS", [P, TT, 2 * GK], scope=mixer)
            BC = sb("BC", [GK, 2, T], scope=mixer)
            GA = sb("GA", [GK, 2, T], scope=mixer)
            GB = sb("GB", [GK, 2, T], scope=mixer)
            DEC = sb("DEC", [GK, 2, GLA_CHUNKS], scope=mixer)
            ST = sb("ST", [GK, 2, GLA_CHUNKS, GLA_DV], scope=mixer)
            AT = sb("AT", [P, 2, T], scope=mixer)
            PU = sb("PU", [P, 2, POOL_PAD + T], scope=mixer)
            PA = sb("PA", [P, POOL_PAD + T], scope=mixer)
            PD = sb("PD", [P, POOL_PAD + T], scope=mixer)
            with ExitStack() as compress:
                W1 = sb("W1", [P, 2, CMP_BLOCK, HD], scope=compress)
                TB = sb("TB", [P, CMP_BLOCK, N_CMP], scope=compress)
            with ExitStack() as attend:
                PB2 = sb("PB2", [P, 2, 1280], scope=attend)
                PT2 = sb("PT2", [P, 2, 1280], scope=attend)
        KTOK = LS
        SQ = (Z_GATE, *Z_PU)
        PTC = ZT[0:N_CMP, Z_PU[0]:Z_PU[1] + 1:Z_PU[1] - Z_PU[0], :]
        NSA_OUT = (Z_KC, Z_VC, Z_VS)
        MIX_CHUNKS = [("nsa", 0), ("nsa", 1), ("pool", 0), ("pool", 1), ("nsa", 2), ("gla", 0), ("gla", 1), ("gla", 2)]

        def mixed(c):
            kind, n = MIX_CHUNKS[c]
            return PU[:, n, POOL_PAD:] if kind == "pool" else ZT[:, NSA_OUT[n] if kind == "nsa" else Z_GV + n, :]
        with ExitStack() as ffn2:
            NB2 = sb("NB2", [P, DC, T], scope=ffn2)
            RB = sb("RB", [P, 2, T], scope=ffn2)
            SB = sb("SB", [P, 2, T], scope=ffn2)
            MH2 = sb("MH2", [P, F2H, T], F32R, scope=ffn2)
            ML2 = sb("ML2", [P, F2H, T], F32R, scope=ffn2)

        w_loaded = [sem("w_loaded0"), sem("w_loaded1")]
        w_hi = sem("w_hi")
        w_lo = sem("w_lo")
        tile_done = sem("tile_done")
        x_loaded = [sem(f"x_loaded{n}") for n in range(X_PARTS)]
        c_loaded = sem("c_loaded")
        r_loaded = sem("r_loaded")
        s_loaded = sem("s_loaded")
        out_stored = sem("out_stored")
        y_done = sem("y_done")
        x_ready = sem("x_ready")
        h_hi = sem("h_hi")
        h_lo = sem("h_lo")
        n_sq = sem("n_sq")
        n_sum = sem("n_sum")
        n_add = sem("n_add")
        n_cent = sem("n_cent")
        n_var = sem("n_var")
        n_std = sem("n_std")
        n_row = sem("n_row")
        e_pad = sem("e_pad")
        e_mask = sem("e_mask")
        e_z = sem("e_z")
        e_sig = sem("e_sig")
        e_glu = sem("e_glu")
        e_gelu = sem("e_gelu")
        e_conv = sem("e_conv")
        e_diag = sem("e_diag")
        e_conv3 = sem("e_conv3")
        e_kept3 = sem("e_kept3")
        e_vaff = sem("e_vaff")
        e_vt = sem("e_vt")
        e_vtok = sem("e_vtok")
        e_mix = sem("e_mix")
        e_y = sem("e_y")
        f_z = sem("f_z")
        f_acc = sem("f_acc")
        f_conv = sem("f_conv")
        f_silu = sem("f_silu")
        f_mid = sem("f_mid")
        f_mhi = sem("f_mhi")
        f_mlo = sem("f_mlo")
        o_raw = sem("o_raw")
        o_v = sem("o_v")
        o_perm = sem("o_perm")
        o_rope = sem("o_rope")
        o_vt = sem("o_vt")
        o_hi = sem("o_hi")
        o_lo = sem("o_lo")
        at_s = [sem("at_s0"), sem("at_s1")]
        at_max = sem("at_max")
        at_exp = sem("at_exp")
        at_p = sem("at_p")
        at_pt = sem("at_pt")
        at_ptc = sem("at_ptc")
        at_o = sem("at_o")

        m_loaded = sem("m_loaded")
        m_zero = sem("m_zero")
        z_kept = sem("z_kept")
        x_new = sem("x_new")
        g_logit = sem("g_logit")
        g_gate = sem("g_gate")
        g_sig = sem("g_sig")
        g_soft = sem("g_soft")
        g_ls = sem("g_ls")
        g_cum = sem("g_cum")
        g_grow = sem("g_grow")
        g_diff = sem("g_diff")
        g_end = sem("g_end")
        g_q = sem("g_q")
        g_inv = sem("g_inv")
        g_ke = sem("g_ke")
        g_ki = sem("g_ki")
        g_kt = sem("g_kt")
        g_vt = sem("g_vt")
        g_ktok = sem("g_ktok")
        g_vtok = sem("g_vtok")
        g_ds = sem("g_ds")
        g_st = sem("g_st")
        g_at = sem("g_at")
        g_am = sem("g_am")
        g_o = sem("g_o")
        g_ok = sem("g_ok")
        g_ms = sem("g_ms")
        g_var = sem("g_var")
        g_sd = sem("g_sd")
        g_sil = sem("g_sil")
        g_y = sem("g_y")
        r_swap = sem("r_swap")
        r_done = sem("r_done")
        v_turn = sem("v_turn")
        v_kept = sem("v_kept")
        c_tb = sem("c_tb")
        c_hid = sem("c_hid")
        c_gelu = sem("c_gelu")
        c_kv = sem("c_kv")
        c_kept = sem("c_kept")
        c_s = sem("c_s")
        c_sm = sem("c_sm")
        c_x = sem("c_x")
        c_p = sem("c_p")
        c_t = sem("c_t")
        c_ptc = sem("c_ptc")
        c_v = sem("c_v")
        c_acc = sem("c_acc")
        u_acc = sem("u_acc")
        p_sum = sem("p_sum")
        p_lin = sem("p_lin")
        p_y = sem("p_y")
        q_relu = sem("q_relu")
        q_sq = sem("q_sq")
        q_hi = sem("q_hi")
        q_lo = sem("q_lo")

        ROW_AT = {3: 0, 2: 512, 0: 896, 1: 1024}
        ROW_ORDER = (3, 2, 0, 1)
        COL_AT = {0: 0, 1: 512, 3: 896, 2: 1024}

        def head_banks(e):
            return PS[:, 2 + 3 * e:5 + 3 * e, :].rearrange("p a b -> p (a b)")

        block = ctx.enter_context(nc.Block())

        @block.sync
        def _(sp):
            def load_x(n):
                w = DC // X_PARTS
                sp.dma_start(X[:, n * w:(n + 1) * w, :], xt[:, n * w:(n + 1) * w, :]).then_inc(x_loaded[n], 16)

            sp.dma_start(RAW[:, 0, :], wstream[0:P, :]).then_inc(w_loaded[0], 16)
            sp.dma_start(VEC[:, 0:VEC_EVEN], vecs[:, 0:VEC_EVEN]).then_inc(c_loaded, 16)
            load_x(0)
            sp.dma_start(TAB[:, 0:TAB_EVEN], tables[:, 0:TAB_EVEN]).then_inc(c_loaded, 16)
            for n in range(1, X_PARTS):
                load_x(n)
            sp.dma_start(RAW[:, 1, :], wstream[P:2 * P, :]).then_inc(w_loaded[1], 16)
            sp.dma_start(WS[:], spatial_w).then_inc(s_loaded, 16)
            sp.dma_start(BS[:], spatial_b).then_inc(s_loaded, 16)
            sp.dma_start(VEC[:, VEC_EVEN:], vecs[:, VEC_EVEN:]).then_inc(r_loaded, 16)
            sp.dma_start(TAB[:, TAB_EVEN:], tables[:, TAB_EVEN:]).then_inc(r_loaded, 16)
            with sp.Fori(1, SLOTS // 2) as i:
                for b in range(2):
                    sp.wait_ge(w_lo, 2 * i + b - 1)
                    sp.dma_start(RAW[:, b, :], wstream[bass.ds((2 * i + b) * P, P), :]).then_inc(w_loaded[b], 16)
            for n in range(DC):
                sp.wait_ge(x_new, DC * (2 * DEPTH2 - 1) + n + 1)
                sp.dma_start(out[:, n, :], X[:, n, :]).then_inc(out_stored, 16)
            sp.wait_ge(out_stored, 16 * DC)

        @block.gpsimd
        def _(pool):
            pool.memset(CB[:, :, 0:PAD], 0.0).then_inc(e_pad, 1)
            pool.wait_ge(s_loaded, 32)
            pool.affine_select(out=WS[:], in_=WS[:], pattern=[[0, 2 * HC], [1, P]], base=0, channel_multiplier=-1,
                               compare_op=ALU.is_ge, fill=0.0).then_inc(e_mask, 1)

            pool.wait_ge(r_loaded, 32)
            for l in range(DEPTH2):
                pool.wait_ge(h_lo, H_FILL[f"in{l}"] + DC)
                for dst, src in ((GW, gate_w), (PW, pool_w), (W2, cmp_w2), (CP, cmp_p), (W1, cmp_w1)):
                    pool.dma_start(dst[:], src[l]).then_inc(m_loaded, 16)
                pool.memset(PU[:, :, 0:POOL_PAD], 0.0)
                pool.memset(AT[:], 0.0).then_inc(m_zero, 1)
                for n in range(2):
                    pool.wait_ge(z_kept, Z_TILES * l + Z_PU[n] + 1)
                    if n:
                        pool.drain()
                    src, width = PU[:, n, :], 1
                    for dst in (PA, PD) if n == 0 else (PA, PD, PA, PD):
                        first = 2 * width - 1
                        pool.tensor_tensor(dst[:, first:], src[:, first:], src[:, first - width:POOL_PAD + T - width], ALU.add)
                        pool.drain()
                        src, width = dst, 2 * width
                    for half, win in ((0, PA), (1, PD)):
                        rows = slice(half * HD, (half + 1) * HD)
                        early = tab("inv_count")[rows, n * POOL_PAD:(n + 1) * POOL_PAD]
                        pool.tensor_tensor(win[rows, 0:POOL_PAD], win[rows, POOL_PAD:2 * POOL_PAD], early, ALU.mult)
                        pool.drain()
                        pool.tensor_scalar(win[rows, 2 * POOL_PAD:], win[rows, 2 * POOL_PAD:],
                                           tab("inv_window")[rows, n:n + 1], None, ALU.mult)
                        pool.drain()
                        u = PU[rows, n, :]
                        pool.tensor_tensor(u[:, POOL_PAD:2 * POOL_PAD], win[rows, 0:POOL_PAD], u[:, POOL_PAD:2 * POOL_PAD],
                                           ALU.subtract)
                        last = pool.tensor_tensor(u[:, 2 * POOL_PAD:], win[rows, 2 * POOL_PAD:], u[:, 2 * POOL_PAD:],
                                                  ALU.subtract)
                    last.then_inc(p_sum, 1)

        @block.scalar
        def _(act):
            def split_hi(i, c, first=False):
                b = c % 2
                act.wait_ge(w_loaded[b], 16 * (i + c // 2 + 1))
                if not first:
                    act.wait_ge(tile_done, 2 * i + c - 1)
                act.activation(WH[:, b, :], RAW[:, b, :], ACT.Copy).then_inc(w_hi, 1)

            def squares(buf, src, order, ready, base):
                for q, n in enumerate(order):
                    act.wait_ge(ready, base + q + 1)
                    act.activation(buf[:, n, :], src[:, n, :], ACT.Square).then_inc(n_sq, 1)

            def bring_root(nm):
                n = NORM[nm][1]
                act.activation(WARM[:, n:n + 1], tab("ones")[:, 0:1], ACT.Sqrt)

            def root(nm):
                act.wait_ge(n_var, NORM[nm][1] + 1)
                act.activation(STD[:], STD[:], ACT.Sqrt).then_inc(n_std, 1)

            def rows_hi(buf, base):
                for n in range(DC):
                    act.wait_ge(n_row, base + n + 1)
                    act.activation(HH[:, n, :], buf[:, n, :], ACT.Copy).then_inc(h_hi, 1)

            def fill_scaled(buf, gain, waits):
                for n in range(DC):
                    act.wait_ge(*waits[n])
                    act.activation(HH[:, n, :], X[:, n, :], ACT.Identity, scale=vec(gain, n)).then_inc(h_hi, 1)
                    act.activation(buf[:, n, :], X[:, n, :], ACT.Square).then_inc(n_sq, 1)

            def new_x(nm):
                return [(x_ready, XR[nm] + n + 1) for n in range(DC)]

            split_hi(0, 0, first=True)
            act.wait_ge(c_loaded, 32)
            bring_root("even")
            fill_scaled(NB, "even_norm_g", [(x_loaded[n * X_PARTS // DC], 16) for n in range(DC)])
            split_hi(0, 1, first=True)
            root("even")
            for j in range(HC):
                split_hi(0, 2 * j + 2)
                split_hi(0, 2 * j + 3)
                act.wait_ge(e_z, 2 * j + 2)
                if j:
                    act.wait_ge(e_glu, j)
                act.activation(SIG[:], ZE[:, 1, :], ACT.Sigmoid, bias=vec("even_b_in", 12 + j)).then_inc(e_sig, 1)

            def gelu(s):
                j = s - 2 * HC
                act.wait_ge(e_z, s + 1)
                dst = V[:, j, :] if j < HC else U[:, j - HC, :]
                act.activation(dst, ZE[:, s % 2, :], ACT.Gelu_apprx_tanh,
                               bias=vec("even_b_in", 4 + j if j < HC else j - HC)).then_inc(e_gelu, 1)

            def y_high(n):
                act.wait_ge(e_y, n + 1)
                act.activation(HH[:, n, :], Y[:, n, :], ACT.Copy).then_inc(h_hi, 1)

            for j in range(HC):
                s = 2 * HC + j
                split_hi(0, s + 2)
                gelu(s)
                for k in range(*DIAG_PARTS[j:j + 2]):
                    ins = act.activation(TAPD[:, k, :], tab("identity"), ACT.Identity, scale=vec("even_conv_w", (HC - 1) * TAPS + k))
                ins.then_inc(e_diag, 1)
            squares(NB, V, range(HC), n_cent, 0)
            split_hi(0, 14)
            gelu(12)
            bring_root("v")
            root("v")
            for n in range(HC):
                act.wait_ge(n_row, ROWS["v"] + n + 1)
                act.activation(V[:, n, :], NB[:, n, :], ACT.Identity, scale=vec("even_v_ln_g", n),
                               bias=vec("even_v_ln_b", n)).then_inc(e_vaff, 1)
            split_hi(0, 15)
            gelu(13)
            split_hi(0, 16)
            gelu(14)
            for t in range(TT):
                act.wait_ge(e_vt, t + 1)
                act.activation(VTOK[:, t, :], PS[:, 2 + t, :], ACT.Copy).then_inc(e_vtok, 1)
            split_hi(0, 17)
            act.wait_ge(e_conv3, 1)
            act.activation(CONV[:, HC - 1, :], PS[:, 7, :], ACT.Identity, bias=vec("even_conv_b", HC - 1)).then_inc(e_kept3, 1)
            gelu(15)
            squares(NB, CONV, range(HC), n_cent, HC)
            bring_root("conv")
            y_high(0)
            y_high(1)
            root("conv")
            y_high(2)
            y_high(3)
            for n in range(HC):
                if n % 2 == 0:
                    split_hi(0, E_OUT + 2 + n // 2)
                act.wait_ge(n_row, ROWS["conv"] + n + 1)
                act.activation(Y[:, HC + n, :], NB[:, n, :], ACT.Silu, scale=vec("even_conv_ln_g", n),
                               bias=vec("even_conv_ln_b", n))
                act.drain()
                act.activation(HH[:, HC + n, :], Y[:, HC + n, :], ACT.Copy).then_inc(h_hi, 1)
            for k in range(4, DC + 1):
                split_hi(0, E_OUT + k)
            act.wait_ge(r_loaded, 32)

            def conv_ffn(l):
                base = F_UP[l] // 2
                cv = f"ffn_conv{l}"
                bring_root(f"f{l}")
                fill_scaled(NBF, f"ffn_norm_g{l}", new_x(f"f{l}"))
                split_hi(base, 1)
                root(f"f{l}")

                def last_tap(i, b, first=False):
                    if b == 0 and not first:
                        act.wait_ge(f_silu, FC * l + i)
                    w = VEC[:, bass.ds(VEC_AT[cv] + 8 * i + 4 * b, 4)]
                    act.wait_ge(f_z, 2 * FC * l + 2 * i + b + 1)
                    act.activation(ACCS[:, b, :], ZF[:, b, :], ACT.Identity, scale=w[:, 2:3], bias=w[:, 3:4]).then_inc(f_acc, 1)

                def gate(i):
                    act.wait_ge(f_conv, 2 * FC * l + 2 * i + 1)
                    act.activation(SG[:], ACCS[:, 0, :], ACT.Silu).then_inc(f_silu, 1)

                def high(i):
                    act.wait_ge(f_mid, FC * l + i + 1)
                    act.activation(MH[:, bass.ds(i, 1), :], MID[:], ACT.Copy).then_inc(f_mhi, 1)

                split_hi(base, 2)
                last_tap(0, 0, first=True)
                split_hi(base, 3)
                last_tap(0, 1)
                gate(0)
                with act.Fori(1, FC) as i:
                    split_hi(base + i, 2)
                    last_tap(i, 0)
                    high(i - 1)
                    split_hi(base + i, 3)
                    last_tap(i, 1)
                    gate(i)
                high(FC - 1)
                down = F_DOWN[l] // 2
                with act.Fori(1, FC // 2) as i:
                    for b in range(2):
                        split_hi(down + i, b)
                split_hi(down + FC // 2, 0)

            conv_ffn(0)

            def exps(u, PB=PB, NEGMAX=NEGMAX, SUM=SUM):
                for q, i in enumerate(ROW_ORDER):
                    for e in range(2):
                        w = (i + 1) * P
                        act.wait_ge(at_max, 8 * u + 2 * q + e + 1)
                        row = PB[:, e, ROW_AT[i]:ROW_AT[i] + w]
                        act.activation(row, row, ACT.Exp, scale=-1.0, bias=NEGMAX[:, 4 * e + i:4 * e + i + 1],
                                       accum_out=SUM[:, 4 * e + i:4 * e + i + 1]).then_inc(at_exp, 1)

            def keep_pt(u, PT=PT):
                for e in range(2):
                    act.wait_ge(at_pt, 2 * u + e + 1)
                    act.activation(PT[:, e, :], head_banks(e)[:, 0:1280], ACT.Copy).then_inc(at_ptc, 1)

            bring_root("odd")
            fill_scaled(NBO, "odd_norm_g", new_x("odd"))

            def raw_q(m, c, b):
                act.wait_ge(tile_done, O_QKV + 6 * m + c + 1)
                act.activation(QRAW[:], PS[:, b, :], ACT.Copy, scale=-SCORE_SCALE).then_inc(o_raw, 1)

            def raw_k(m, c, b):
                act.wait_ge(tile_done, O_QKV + 6 * m + c + 1)
                act.activation(KRAW[:], PS[:, b, :], ACT.Copy).then_inc(o_raw, 1)

            def keep_vt(j):
                act.wait_ge(o_perm, 3 * j + 3)
                act.activation(VT[:], PS[:, 7, :].rearrange("p (a b) -> p a b", a=TT), ACT.Copy).then_inc(o_vt, 1)

            def heads_out(j):
                act.wait_ge(at_o, j + 1)
                act.activation(OH[:, bass.ds(j, 1), :], PS[:, 2, :], ACT.Copy).then_inc(o_hi, 1)

            base = O_QKV // 2
            split_hi(base, 1)
            raw_q(0, 0, 0)
            root("odd")
            split_hi(base, 2)
            raw_k(0, 1, 1)
            split_hi(base, 3)
            keep_vt(0)

            def pair_step(m, r):
                j = 2 * m + r
                c = 3 * (r + 1)
                split_hi(base + 3 * m, c + 1)
                exps(j)
                raw_q(m, c, c % 2)
                keep_pt(j)
                split_hi(base + 3 * m, c + 2)
                raw_k(m, c + 1, (c + 1) % 2)
                heads_out(j)
                split_hi(base + 3 * m, c + 3)
                keep_vt(j + 1)

            with act.Fori(0, PAIRS // 2 - 1) as m:
                for r in range(2):
                    pair_step(m, r)
            pair_step(PAIRS // 2 - 1, 0)
            exps(PAIRS - 1)
            keep_pt(PAIRS - 1)
            heads_out(PAIRS - 1)
            for k in range(DC):
                split_hi(0, O_OUT + k + 1)
            conv_ffn(1)

            bring_root("final")
            squares(NBF, X, range(DC), x_ready, XR["final"])
            split_hi(0, L_IN[0] + 1)
            root("final")
            rows_hi(X, ROWS["final"])

            def layer_norm(nm, fill):
                bring_root(nm)
                squares(NB2, X, range(DC), n_cent, ADD[nm])
                root(nm)
                bias = nm.replace("_", "_b")
                if fill is not None:
                    for n in range(DC):
                        act.wait_ge(n_row, ROWS[nm] + n + 1)
                        act.activation(HH[:, n, :], NB2[:, n, :], ACT.Identity, bias=vec(bias, n)).then_inc(h_hi, 1)
                for n in range(DC):
                    act.wait_ge(n_row, ROWS[nm] + n + 1)
                    act.activation(X[:, n, :], NB2[:, n, :], ACT.Identity, bias=vec(bias, n)).then_inc(x_new, 1)

            def mix_layer(l):
                z0 = L_IN[l]

                def hi(s):
                    split_hi(0, z0 + s)

                def take(s):
                    act.wait_ge(tile_done, z0 + s + 1)
                    ps = PS[:, z_bank(s), :]
                    if s == Z_GATE:
                        ins = act.activation(ZT[:, s, :], ps, ACT.Identity, bias=tab("bias_row"))
                    elif s in Z_PU:
                        act.wait_ge(m_zero, l + 1)
                        ins = act.activation(PU[:, Z_PU.index(s), POOL_PAD:], ps, ACT.Copy)
                    else:
                        ins = act.activation(ZT[:, s, :], ps, ACT.Copy, scale=-SCORE_SCALE if s in Z_Q else 1.0)
                    ins.then_inc(z_kept, 1)

                def gate_logs():
                    act.wait_ge(g_logit, l + 1)
                    ls = LS[:].rearrange("p (a b) c -> p a (b c)", a=2)
                    act.activation(ls, PS[:, 2:4, 0:4 * GK], ACT.Abs)
                    act.drain()
                    act.activation(LS[:], LS[:], ACT.Exp, scale=-1.0)
                    act.drain()
                    act.activation(LS[:], LS[:], ACT.Ln, bias=1.0).then_inc(g_soft, 1)

                def branch_gates():
                    act.wait_ge(g_gate, l + 1)
                    gates = PS[:, 6, :].rearrange("p (a b) -> p a b", a=TT)[:, :, GATE_ROW:GATE_ROW + 6 * NSA_PAIRS]
                    act.activation(GT[:], gates, ACT.Sigmoid).then_inc(g_sig, 1)

                def growth():
                    act.wait_ge(g_cum, l + 1)
                    act.activation(BC[:], PS[0:GK, 4:6, :], ACT.Copy, scale=1.0 / 16)
                    act.drain()
                    act.activation(GA[:], BC[:], ACT.Exp)
                    ends = BC[:].rearrange("p a (c t) -> p a c t", t=GLA_CHUNK)[:, :, :, GLA_CHUNK - 1]
                    act.activation(DEC[:], ends, ACT.Exp).then_inc(g_grow, 1)

                def to_end():
                    act.wait_ge(g_diff, l + 1)
                    act.activation(GB[:], GB[:], ACT.Exp).then_inc(g_end, 1)

                def inverse():
                    act.wait_ge(g_q, l + 1)
                    act.activation(GA[:], BC[:], ACT.Exp, scale=-1.0).then_inc(g_inv, 1)

                def hidden(kv):
                    act.wait_ge(c_hid, 2 * l + kv + 1)
                    act.activation(HID[:, kv, :], PS[:, 2 + kv, 0:N_CMP], ACT.Gelu_apprx_tanh).then_inc(c_gelu, 1)

                def keep_values(b):
                    act.wait_ge(v_turn, 2 * l + b + 1)
                    act.activation(VTS[:, b, :, :], PS[:, (3, 1)[b], :].rearrange("p (a b) -> p a b", a=TT), ACT.Copy).then_inc(v_kept, 1)

                def keep_compressed():
                    act.wait_ge(c_kv, l + 1)
                    act.activation(KCS[:], PS[:, 5, 0:N_CMP], ACT.Copy)
                    act.activation(VCS[:], PS[0:N_CMP, 6, 0:P], ACT.Copy).then_inc(c_kept, 1)

                def cmp_exp(jj):
                    act.wait_ge(c_sm, 2 * (NSA_PAIRS * l + jj) + 2)
                    act.activation(PC[:], PC[:], ACT.Exp, scale=-1.0).then_inc(c_x, 1)

                def cmp_keep(jj):
                    act.wait_ge(c_t, NSA_PAIRS * l + jj + 1)
                    act.activation(PTC, PS[0:N_CMP, 5:7, :], ACT.Copy).then_inc(c_ptc, 1)

                def unit(k):
                    exps(UNIT0[l] + k, PB2, NEGMAX2, SUM2)

                def unit_keep(k):
                    keep_pt(UNIT0[l] + k, PT2)

                def keep_gla_keys():
                    act.wait_ge(g_kt, l + 1)
                    view = KTOK[:].rearrange("p (a b) c -> p a (b c)", a=2)
                    act.activation(view[:, 0, :], PS[:, 4, 0:4 * GK], ACT.Copy)
                    act.activation(view[:, 1, :], PS[:, 7, 0:4 * GK], ACT.Copy).then_inc(g_ktok, 1)

                def keep_gla_values():
                    act.wait_ge(g_vt, l + 1)
                    for n in range(3):
                        ins = act.activation(GVTOK[:, :, n * P:(n + 1) * P],
                                             PS[:, 2 + n, :].rearrange("p (a b) -> p a b", a=TT), ACT.Copy)
                    ins.then_inc(g_vtok, 1)

                def gla_out(n):
                    act.wait_ge(g_o, 3 * l + n + 1)
                    act.activation(ZT[:, Z_GV + n, :], PS[:, 7, :], ACT.Copy)
                    act.activation(ZT[:, SQ[n], :], PS[:, 7, :], ACT.Square).then_inc(g_ok, 1)

                def gla_root(n):
                    act.wait_ge(g_var, 3 * l + n + 1)
                    act.activation(ZT[:, Z_OG + n, :], ZT[:, Z_OG + n, :], ACT.Sqrt).then_inc(g_sd, 1)

                def keep(s):
                    hi(s + 1)
                    take(s)

                def mix_high(c):
                    kind, n = MIX_CHUNKS[c]
                    if kind == "nsa":
                        act.wait_ge(u_acc, UNITS * l + NSA_PAIRS + n + 1)
                        act.wait_ge(c_acc, NSA_PAIRS * l + n + 1)
                    elif kind == "pool":
                        act.wait_ge(p_y, 2 * l + n + 1)
                    else:
                        act.wait_ge(g_y, 3 * l + n + 1)
                    act.activation(HH[:, c, :], mixed(c), ACT.Copy).then_inc(h_hi, 1)

                if l:
                    act.wait_ge(x_new, DC * 2 * l)
                take(0)
                keep(1)
                keep(2)
                hi(4)
                gate_logs()
                branch_gates()
                take(3)
                keep(4)
                growth()
                to_end()
                keep(5)
                hidden(0)
                keep(6)
                inverse()
                keep_gla_keys()
                keep(7)
                hidden(1)
                keep(8)
                keep_compressed()
                keep(9)
                hi(11)
                keep_gla_values()
                take(10)
                keep(11)
                gla_out(0)
                keep(12)
                gla_root(0)
                gla_out(1)
                keep_values(0)
                keep(13)
                gla_root(1)
                gla_out(2)
                gla_root(2)
                hi(15)
                unit(0)
                take(14)
                unit_keep(0)
                hi(16)
                cmp_exp(0)
                unit(1)
                take(15)
                unit_keep(1)
                hi(17)
                cmp_keep(0)
                cmp_exp(1)
                take(16)
                hi(18)
                unit(2)
                take(17)
                unit_keep(2)
                hi(19)
                cmp_keep(1)
                take(18)
                hi(20)
                unit(3)
                keep_values(1)
                take(19)
                unit_keep(3)
                hi(21)
                cmp_exp(2)
                unit(4)
                take(20)
                unit_keep(4)
                hi(22)
                cmp_keep(2)
                unit(5)
                take(21)
                unit_keep(5)
                for c in range(4):
                    mix_high(c)
                hi(23)
                mix_high(4)
                act.wait_ge(z_kept, Z_TILES * (l + 1))
                for n in range(3):
                    og = ZT[:, Z_OG + n, :]
                    ins = act.activation(og, og, ACT.Silu)
                ins.then_inc(g_sil, 1)
                for c in range(5, DC):
                    mix_high(c)
                for k in range(2, DC + 2):
                    hi(Z_TILES + k)

            def square_ffn(l):
                for half in range(2):
                    up = L_IN[l] + Z_TILES + DC + half * 2 * F2H
                    done = F2C * l + F2H * half
                    with act.Fori(0, F2H // 2) as i:
                        for b in range(2):
                            act.wait_ge(tile_done, up + 2 * i + b + 1)
                            act.activation(RB[:, b, :], PS[:, b, :], ACT.Relu).then_inc(q_relu, 1)
                            split_hi(up // 2 + i, b + 2)
                            act.wait_ge(q_sq, done + 2 * i + b + 1)
                            act.activation(MH2[:, bass.ds(2 * i + b, 1), :], SB[:, b, :], ACT.Copy).then_inc(q_hi, 1)
                    last = l == DEPTH2 - 1 and half == 1
                    with act.Fori(1, F2H // 2 + (0 if last else 1)) as i:
                        for b in range(2):
                            split_hi((up + F2H) // 2 + i, b)

            for l in range(DEPTH2):
                mix_layer(l)
                layer_norm(f"ln1_{l}", H_FILL[f"up{l}"])
                square_ffn(l)
                layer_norm(f"ln2_{l}", None if l == DEPTH2 - 1 else H_FILL[f"in{l + 1}"])

        @block.tensor
        def _(pe):
            def project(i, c, bank=None, beside=None):
                b = c % 2
                bank = b if bank is None else bank
                pe.wait_ge(w_lo, 2 * i + c + 1)
                for k in range(DC):
                    w = slice(k * P, (k + 1) * P)
                    pe.matmul(PS[:, bank, :], WH[:, b, w], HH[:, k, :], start=(k == 0), stop=False)
                    pe.matmul(PS[:, bank, :], WH[:, b, w], HL[:, k, :], start=False, stop=False)
                    last = pe.matmul(PS[:, bank, :], WL[:, b, w], HH[:, k, :], start=False, stop=(k == DC - 1))
                    if k == DC - 1:
                        last.then_inc(tile_done, 1)
                    if beside:
                        beside(k)

            def add_rows(i, c, rh, rl, first, final, frees=None, order=ORDER):
                b = c % 2
                pe.wait_ge(w_lo, 2 * i + c + 1)
                for n in order if first else range(DC):
                    if frees and n in frees:
                        pe.wait_ge(*frees[n])
                    w = slice(n * P, (n + 1) * P)
                    pe.matmul(PS[:, n, :], WH[:, b, w], rh, start=first, stop=False)
                    pe.matmul(PS[:, n, :], WH[:, b, w], rl, start=False, stop=False)
                    last = pe.matmul(PS[:, n, :], WL[:, b, w], rh, start=False, stop=final)
                    if final and n != DC - 1:
                        last.then_inc(y_done, 1)
                last.then_inc(tile_done, 1)

            def sum_rows(buf, bank, waits, done):
                for q, (n, *wait) in enumerate(waits):
                    pe.wait_ge(*wait)
                    pe.matmul(PS[:, bank, :], tab("ones"), buf[:, n, :], start=(q == 0),
                              stop=(q == len(waits) - 1)).then_inc(done, 1)

            def sum_squares(buf, n, bank, nm, first, final):
                pe.wait_ge(n_sq, NORM[nm][0] + n + 1)
                pe.matmul(PS[:, bank, :], tab("ones"), buf[:, n, :], start=first, stop=final).then_inc(n_sum, 1)

            def first_tile(i, fill, buf=None, nm=None):
                pe.wait_ge(w_lo, 2 * i + 1)
                for k in range(DC + 2):
                    if k < DC:
                        w = slice(k * P, (k + 1) * P)
                        pe.wait_ge(h_lo, fill + k + 1)
                        pe.matmul(PS[:, 0, :], WH[:, 0, w], HH[:, k, :], start=(k == 0), stop=False)
                        pe.matmul(PS[:, 0, :], WH[:, 0, w], HL[:, k, :], start=False, stop=False)
                        last = pe.matmul(PS[:, 0, :], WL[:, 0, w], HH[:, k, :], start=False, stop=(k == DC - 1))
                        if k == DC - 1:
                            last.then_inc(tile_done, 1)
                    if buf and k >= 2:
                        sum_squares(buf, k - 2, 2, nm, k == 2, k == DC + 1)

            pe.wait_ge(c_loaded, 32)
            first_tile(0, H_FILL["even"], NB, "even")

            def tile(s):
                if s >= 2:
                    pe.wait_ge(e_z, s - 1)
                project(0, s)

            def taps(part):
                if part == 0:
                    pe.wait_ge(e_glu, HC)
                for k in range(*PE_PARTS[part:part + 2]):
                    if k in DIAG_PARTS:
                        pe.wait_ge(e_diag, DIAG_PARTS.index(k) + 1)
                    last = pe.matmul(PS[:, 7, :], TAPD[:, k, :], CB[:, HC - 1, k:k + T], start=(k == 0), stop=(k == TAPS - 1))
                    if k == TAPS - 1:
                        last.then_inc(e_conv3, 1)

            for s in range(1, 12):
                tile(s)
            taps(0)
            sum_rows(V, 2, [(n, e_gelu, n + 1) for n in range(HC)], n_add)
            tile(12)
            for n in range(HC):
                sum_squares(NB, n, 3, "v", n == 0, n == HC - 1)
            tile(13)
            taps(1)
            tile(14)
            for t in range(TT):
                for n in range(HC):
                    pe.wait_ge(e_vaff, n + 1)
                    last = pe.transpose(PS[:, 2 + t, n * P:(n + 1) * P], V[:, n, t * P:(t + 1) * P], tab("identity"))
                last.then_inc(e_vt, 1)
            taps(2)
            tile(15)
            pe.wait_ge(e_mask, 1)
            pe.wait_ge(e_vtok, TT)
            for n in range(HC):
                for t in range(TT):
                    for e in range(2):
                        h = 2 * n + e
                        last = pe.matmul(PS[e * HD:(e + 1) * HD, 2 + n, t * P:(t + 1) * P],
                                         VTOK[:, t, h * HD:(h + 1) * HD], WS[:, h, :], start=True, stop=True)
                last.then_inc(e_mix, 1)
            sum_rows(CONV, 6, [(0, e_conv, 2 * TAPS), (1, e_conv, 2 * TAPS), (3, e_kept3, 1), (2, e_conv, 3 * TAPS)], n_add)
            for n in range(HC):
                sum_squares(NB, n, 7, "conv", n == 0, n == HC - 1)
            frees = {n: (e_y, n - 1) for n in (3, 4, 5)} | {7: (n_var, NORM["conv"][1] + 1), 0: (e_z, 16)}
            for k in range(DC):
                pe.wait_ge(h_lo, H_FILL["even_out"] + k + 1)
                add_rows(0, E_OUT + k, HH[:, k, :], HL[:, k, :], k == 0, k == DC - 1, frees if k == 0 else None,
                         (2, 3, 6, 0, 1, 4, 5, 7))

            def conv_ffn(l):
                base = F_UP[l] // 2
                first_tile(base, H_FILL[f"f{l}"], NBF, f"f{l}")
                project(base, 1)
                with pe.Fori(1, FC) as i:
                    for b in range(2):
                        pe.wait_ge(f_z, 2 * FC * l + 2 * i + b - 1)
                        project(base + i, b)
                down = F_DOWN[l] // 2
                done = 2 * FC * (l + 1)
                for b in range(2):
                    pe.wait_ge(f_mlo, FC * l + b + 1)
                    add_rows(down, b, MH[:, b, :], ML[:, b, :], b == 0, False,
                             {0: (f_z, done - 1), 1: (f_z, done)} if b == 0 else None)
                with pe.Fori(1, FC // 2 - 1) as i:
                    for b in range(2):
                        k = 2 * i + b
                        pe.wait_ge(f_mlo, FC * l + 2 * i + b + 1)
                        add_rows(down + i, b, MH[:, bass.ds(k, 1), :], ML[:, bass.ds(k, 1), :], False, False)
                for b in range(2):
                    k = FC - 2 + b
                    pe.wait_ge(f_mlo, FC * l + k + 1)
                    add_rows(down + FC // 2 - 1, b, MH[:, k, :], ML[:, k, :], False, b == 1)

            conv_ffn(0)

            def scores(q, k, frees):
                for i in ROW_ORDER:
                    w = (i + 1) * P
                    for e in range(2):
                        bank = 2 + 3 * e + ROW_AT[i] // T
                        if i and bank in frees:
                            pe.wait_ge(*frees[bank])
                        last = pe.matmul(head_banks(e)[:, ROW_AT[i]:ROW_AT[i] + w], q[e * HD:(e + 1) * HD, i * P:(i + 1) * P],
                                         k[e * HD:(e + 1) * HD, 0:w], start=True, stop=True)
                        if i != 2:
                            last.then_inc(at_s[e], 1)

            def turn_p(u, PB=PB):
                for e in range(2):
                    pe.wait_ge(at_p, 2 * u + e + 1)
                    for i in range(TT):
                        for k in range(i + 1):
                            at = COL_AT[k] + (i - k) * P
                            last = pe.transpose(head_banks(e)[:, at:at + P],
                                                PB[:, e, ROW_AT[i] + k * P:ROW_AT[i] + (k + 1) * P], tab("identity"))
                    last.then_inc(at_pt, 1)

            def values(u, vt, PT=PT):
                for e in range(2):
                    pe.wait_ge(at_ptc, 2 * u + e + 1)
                    for k in range(TT):
                        last = pe.matmul(PS[e * HD:(e + 1) * HD, 2, k * P:T], vt[:, k, e * HD:(e + 1) * HD],
                                         PT[:, e, COL_AT[k]:COL_AT[k] + (TT - k) * P], start=(k == 0), stop=(k == TT - 1))
                last.then_inc(at_o, 1)

            base = O_QKV // 2
            pe.wait_ge(r_loaded, 32)

            def swap_q(j):
                pe.wait_ge(o_raw, 2 * j + 1)
                pe.matmul(PS[:, 5, :], tab("swap"), QRAW[:], start=True, stop=True).then_inc(o_perm, 1)

            def swap_k(j):
                pe.wait_ge(o_raw, 2 * j + 2)
                pe.matmul(PS[:, 6, :], tab("swap"), KRAW[:], start=True, stop=True).then_inc(o_perm, 1)

            def turn_v(j):
                pe.wait_ge(o_v, j + 1)
                for t in range(TT):
                    last = pe.transpose(PS[:, 7, t * P:(t + 1) * P], VRAW[:, t * P:(t + 1) * P], tab("identity"))
                last.then_inc(o_perm, 1)

            def pair_scores(j):
                pe.wait_ge(o_rope, 2 * j + 2)
                scores(QR, KR, {7: (o_vt, j + 1)})

            first_tile(base, H_FILL["odd"], NBO, "odd")
            project(base, 1)
            swap_q(0)
            swap_k(0)
            pe.wait_ge(o_raw, 1)
            project(base, 2)
            turn_v(0)
            pair_scores(0)

            def pair_step(m, r):
                j = 2 * m + r
                c = 3 * (r + 1)
                pe.wait_ge(o_raw, 2 * j + 2)
                project(base + 3 * m, c)
                turn_p(j)
                pe.wait_ge(o_v, j + 1)
                project(base + 3 * m, c + 1)
                values(j, VT)
                swap_q(j + 1)
                swap_k(j + 1)
                project(base + 3 * m, c + 2)
                turn_v(j + 1)
                pe.wait_ge(o_lo, j + 1)
                pair_scores(j + 1)

            with pe.Fori(0, PAIRS // 2 - 1) as m:
                for r in range(2):
                    pair_step(m, r)
            pair_step(PAIRS // 2 - 1, 0)
            turn_p(PAIRS - 1)
            values(PAIRS - 1, VT)
            for k in range(DC):
                pe.wait_ge(o_lo, k + 1)
                if k == 0:
                    pe.wait_ge(o_lo, DC)
                add_rows(0, O_OUT + k, OH[:, k, :], OL[:, k, :], k == 0, k == DC - 1)
            conv_ffn(1)

            pe.wait_ge(x_ready, XR["final"] + 3)
            for n in range(DC):
                sum_squares(NBF, n, 2, "final", n == 0, n == DC - 1)

            def layer_norm(nm):
                sum_rows(X, 0, [(n, x_ready, XR[nm] + n + 1) for n in range(DC)], n_add)
                for n in range(DC):
                    sum_squares(NB2, n, 3, nm, n == 0, n == DC - 1)

            def mix_layer(l):
                z0 = L_IN[l]

                def tile(s, beside=None):
                    if s == 0:
                        first_tile(z0 // 2, H_FILL[f"in{l}"])
                        return
                    if s == Z_OG:
                        kept(s - 1)
                    elif s == Z_OG + 1:
                        pe.wait_ge(v_kept, 2 * l + 2)
                    elif s >= 2:
                        kept(s - 2)
                    project(0, z0 + s, z_bank(s), beside)

                def kept(s):
                    pe.wait_ge(z_kept, Z_TILES * l + s + 1)

                def gate_logits():
                    kept(Z_GATE)
                    for t in range(TT):
                        last = pe.transpose(PS[:, 6, t * P:(t + 1) * P], ZT[:, Z_GATE, t * P:(t + 1) * P], tab("identity"))
                    last.then_inc(g_gate, 1)
                    pe.wait_ge(m_loaded, 80 * (l + 1))
                    for t in range(TT):
                        last = pe.matmul(PS[:, 2 + t // 2, (t % 2) * 2 * GK:(t % 2 + 1) * 2 * GK],
                                         ZT[0:RANK + 1, Z_GATE, t * P:(t + 1) * P], GW[:], start=True, stop=True)
                    last.then_inc(g_logit, 1)

                def cumulate():
                    pe.wait_ge(g_ls, l + 1)
                    for a in range(2):
                        for t in range(TT):
                            last = pe.matmul(PS[0:GK, 4 + a, t * P:(t + 1) * P], LS[:, t, a * GK:(a + 1) * GK], tab("cumulate"),
                                             start=True, stop=True)
                    last.then_inc(g_cum, 1)

                def swap(q):
                    kept(SWAPS[q][0])
                    if q:
                        pe.wait_ge(r_done, 6 * l + q)
                    pe.matmul(PS[:, SWAPS[q][1], :], tab("swap2"), ZT[:, SWAPS[q][0], :], start=True, stop=True).then_inc(r_swap, 1)

                def hidden(kv):
                    def part(k):
                        if k == 0:
                            pe.wait_ge(c_tb, 2 * l + kv + 1)
                        for t in range(k * CMP_BLOCK // DC, (k + 1) * CMP_BLOCK // DC):
                            for g in range(2):
                                rows = slice(g * HD, (g + 1) * HD)
                                last = pe.matmul(PS[rows, 2 + kv, 0:N_CMP], W1[rows, kv, t, :], TB[rows, t, :], start=(t == 0),
                                                 stop=(t == CMP_BLOCK - 1))
                        if k == DC - 1:
                            last.then_inc(c_hid, 1)
                    return part

                def turn_values(b):
                    kept((Z_VS, Z_VW)[b])
                    for t in range(TT):
                        last = pe.transpose(PS[:, (3, 1)[b], t * P:(t + 1) * P], ZT[:, (Z_VS, Z_VW)[b], t * P:(t + 1) * P],
                                            tab("identity"))
                    last.then_inc(v_turn, 1)

                def compressed():
                    pe.wait_ge(c_gelu, 2 * l + 2)
                    pe.wait_ge(g_grow, l + 1)
                    pe.wait_ge(g_sig, l + 1)
                    pe.matmul(PS[:, 5, 0:N_CMP], W2[:, 0, :], HID[:, 0, :], start=True, stop=True)
                    pe.matmul(PS[0:N_CMP, 6, 0:P], HID[:, 1, :], W2[:, 1, :], start=True, stop=True).then_inc(c_kv, 1)

                def cmp_scores(jj):
                    pe.wait_ge(c_kept, l + 1)
                    pe.wait_ge(r_done, 6 * l + 3 + jj)
                    for e in range(2):
                        rows = slice(e * HD, (e + 1) * HD)
                        for i in range(TT):
                            last = pe.matmul(PS[:, (4, 7)[e], i * N_CMP:(i + 1) * N_CMP],
                                             ZT[rows, Z_Q[jj], i * P:(i + 1) * P], KCS[rows, :],
                                             start=True, stop=True)
                    last.then_inc(c_s, 1)

                def cmp_turn(jj):
                    pe.wait_ge(c_p, NSA_PAIRS * l + jj + 1)
                    for q in range(8):
                        last = pe.transpose(PS[0:N_CMP, 5 + q // TT, (q % TT) * P:(q % TT + 1) * P], PC[:, q, :], tab("identity"))
                    last.then_inc(c_t, 1)

                def cmp_values(jj):
                    pe.wait_ge(c_ptc, NSA_PAIRS * l + jj + 1)
                    for e in range(2):
                        last = pe.matmul(PS[e * HD:(e + 1) * HD, 3, :], VCS[:, e * HD:(e + 1) * HD], PTC[:, e, :],
                                         start=True, stop=True)
                    last.then_inc(c_v, 1)

                def unit_scores(k, frees):
                    b, jj = divmod(k, NSA_PAIRS)
                    scores(ZT[:, Z_Q[jj], :], ZT[:, (Z_KS, Z_KW)[b], :], {2: (u_acc, UNITS * l + k)} | frees)

                def unit_values(k):
                    turn_p(UNIT0[l] + k, PB2)
                    values(UNIT0[l] + k, VTS[:, k // NSA_PAIRS, :, :], PT2)

                def turn_gla_keys():
                    pe.wait_ge(g_ke, l + 1)
                    pe.wait_ge(g_grow, l + 1)
                    pe.wait_ge(r_done, 6 * l + 1)
                    for t in range(TT):
                        for a in range(2):
                            at = (t % 2) * 2 * GK + a * GK
                            last = pe.transpose(PS[:, 4 if t < 2 else 7, at:at + GK], GB[:, a, t * P:(t + 1) * P],
                                                tab("identity")[0:GK, 0:GK])
                    last.then_inc(g_kt, 1)

                def turn_gla_values():
                    kept(Z_GV + 2)
                    pe.wait_ge(c_gelu, 2 * l + 2)
                    pe.wait_ge(g_ktok, l + 1)
                    for n in range(3):
                        for t in range(TT):
                            last = pe.transpose(PS[:, 2 + n, t * P:(t + 1) * P], ZT[:, Z_GV + n, t * P:(t + 1) * P],
                                                tab("identity"))
                    last.then_inc(g_vt, 1)

                def chunk_states():
                    pe.wait_ge(g_ktok, l + 1)
                    pe.wait_ge(g_vtok, l + 1)
                    for a in range(2):
                        for c in range(GLA_CHUNKS - 1):
                            rows = slice((c % 2) * GLA_CHUNK, (c % 2 + 1) * GLA_CHUNK)
                            for h in range(3):
                                k = a * GK + h * GLA_DK
                                v = (3 * a + h) * GLA_DV
                                at = (4 * a + c // 2) * GLA_DV
                                last = pe.matmul(PS[h * GLA_DK:(h + 1) * GLA_DK, 3 + c % 2, at:at + GLA_DV],
                                                 KTOK[rows, c // 2, k:k + GLA_DK], GVTOK[rows, c // 2, v:v + GLA_DV],
                                                 start=True, stop=True)
                    last.then_inc(g_ds, 1)

                def within(n):
                    pe.wait_ge(g_ki, l + 1)
                    pe.wait_ge(c_kept, l + 1)
                    if n:
                        pe.wait_ge(g_am, 3 * l + n)
                    for e in range(2):
                        a, h = divmod(2 * n + e, 3)
                        rows = slice(h * GLA_DK, (h + 1) * GLA_DK)
                        for t in range(TT):
                            cols = slice(t * P, (t + 1) * P)
                            last = pe.matmul(PS[:, 5 + e, cols], ZT[rows, Z_GK + a, cols], ZT[rows, Z_GQ + a, cols],
                                             start=True, stop=True)
                    last.then_inc(g_at, 1)

                def gla_values(n):
                    pe.wait_ge(g_am, 3 * l + n + 1)
                    pe.wait_ge(g_st, l + 1)
                    if n:
                        pe.wait_ge(g_ok, 3 * l + n)
                    for e in range(2):
                        a, h = divmod(2 * n + e, 3)
                        rows = slice(h * GLA_DK, (h + 1) * GLA_DK)
                        v = (2 * n + e) * GLA_DV
                        for t in range(TT):
                            pe.matmul(PS[e * HD:(e + 1) * HD, 7, t * P:(t + 1) * P], GVTOK[:, t, v:v + GLA_DV],
                                      AT[:, e, t * P:(t + 1) * P], start=True, stop=False)
                            for c in (2 * t, 2 * t + 1):
                                if c:
                                    cols = slice(c * GLA_CHUNK, (c + 1) * GLA_CHUNK)
                                    last = pe.matmul(PS[e * HD:(e + 1) * HD, 7, cols], ST[rows, a, c, :], ZT[rows, Z_GQ + a, cols],
                                                     start=False, stop=(c == 2 * t + 1))
                    last.then_inc(g_o, 1)

                def gla_squares(n):
                    pe.wait_ge(g_ok, 3 * l + n + 1)
                    if n:
                        pe.wait_ge(g_var, 3 * l + n)
                    pe.matmul(PS[:, 4, :], tab("head_mean"), ZT[:, SQ[n], :], start=True, stop=True).then_inc(g_ms, 1)

                def pool_mix(n):
                    pe.wait_ge(p_sum, 2 * l + n + 1)
                    pe.matmul(PS[:, (4, 7)[n], :], PW[:, n, :], PU[:, n, POOL_PAD:], start=True, stop=True).then_inc(p_lin, 1)

                tile(0)
                tile(1)
                tile(2)
                gate_logits()
                swap(0)
                tile(3)
                tile(4)
                cumulate()
                tile(5, hidden(0))
                tile(6)
                turn_gla_keys()
                tile(7, hidden(1))
                tile(8)
                compressed()
                tile(9)
                turn_gla_values()
                tile(10)
                within(0)
                chunk_states()
                tile(11)
                gla_values(0)
                within(1)
                swap(1)
                tile(12)
                gla_squares(0)
                gla_values(1)
                within(2)
                turn_values(0)
                swap(2)
                tile(13)
                gla_squares(1)
                gla_values(2)
                swap(3)
                gla_squares(2)
                unit_scores(0, {2: (r_done, 6 * l + 4), 3: (v_kept, 2 * l + 1), 4: (g_var, 3 * l + 3),
                                5: (g_am, 3 * l + 3), 7: (g_ok, 3 * l + 3)})
                tile(14)
                unit_values(0)
                cmp_scores(0)
                unit_scores(1, {4: (c_sm, 6 * l + 1)})
                tile(15)
                unit_values(1)
                cmp_turn(0)
                swap(4)
                cmp_scores(1)
                tile(16)
                pe.wait_ge(r_done, 6 * l + 5)
                unit_scores(2, {4: (c_sm, 6 * l + 3), 5: (c_ptc, 3 * l + 1)})
                tile(17)
                unit_values(2)
                cmp_values(0)
                cmp_turn(1)
                swap(5)
                tile(18)
                pe.wait_ge(r_done, 6 * l + 6)
                unit_scores(3, {3: (c_acc, 3 * l + 1), 5: (c_ptc, 3 * l + 2)})
                turn_values(1)
                tile(19)
                unit_values(3)
                cmp_scores(2)
                cmp_values(1)
                unit_scores(4, {3: (c_acc, 3 * l + 2), 4: (c_sm, 6 * l + 5)})
                tile(20)
                unit_values(4)
                cmp_turn(2)
                pool_mix(0)
                pool_mix(1)
                unit_scores(5, {4: (p_y, 2 * l + 1), 5: (c_ptc, 3 * l + 3), 7: (p_y, 2 * l + 2)})
                tile(21)
                unit_values(5)
                cmp_values(2)
                frees = {0: (z_kept, Z_TILES * (l + 1)), 2: (u_acc, UNITS * (l + 1)), 3: (c_acc, 3 * l + 3)}
                for k in range(DC):
                    pe.wait_ge(h_lo, H_FILL[f"out{l}"] + k + 1)
                    add_rows(0, z0 + Z_TILES + k, HH[:, k, :], HL[:, k, :], k == 0, k == DC - 1, frees if k == 0 else None,
                             (4, 5, 6, 7, 0, 1, 3, 2))

            def square_ffn(l):
                for half in range(2):
                    up = L_IN[l] + Z_TILES + DC + half * 2 * F2H
                    done = F2C * l + F2H * half
                    if half:
                        pe.wait_ge(x_ready, XR[f"half{l}"] + 1)
                        project(up // 2, 0)
                        pe.wait_ge(x_ready, XR[f"half{l}"] + 2)
                    else:
                        first_tile(up // 2, H_FILL[f"up{l}"])
                    project(up // 2, 1)
                    with pe.Fori(1, F2H // 2) as i:
                        for b in range(2):
                            pe.wait_ge(q_relu, done + 2 * i + b - 1)
                            project(up // 2 + i, b)
                    down = (up + F2H) // 2
                    if half:
                        pe.wait_ge(x_ready, XR[f"half{l}"] + DC)
                    for b in range(2):
                        pe.wait_ge(q_lo, done + b + 1)
                        add_rows(down, b, MH2[:, b, :], ML2[:, b, :], b == 0, False,
                                 {0: (q_relu, done + F2H - 1), 1: (q_relu, done + F2H)} if b == 0 else None)
                    with pe.Fori(1, F2H // 2 - 1) as i:
                        for b in range(2):
                            k = 2 * i + b
                            pe.wait_ge(q_lo, done + 2 * i + b + 1)
                            add_rows(down + i, b, MH2[:, bass.ds(k, 1), :], ML2[:, bass.ds(k, 1), :], False, False)
                    for b in range(2):
                        k = F2H - 2 + b
                        pe.wait_ge(q_lo, done + k + 1)
                        add_rows(down + F2H // 2 - 1, b, MH2[:, k, :], ML2[:, k, :], False, b == 1)

            for l in range(DEPTH2):
                mix_layer(l)
                layer_norm(f"ln1_{l}")
                square_ffn(l)
                layer_norm(f"ln2_{l}")

        @block.vector
        def _(dve):
            def split_lo(i, c):
                b = c % 2
                dve.wait_ge(w_hi, 2 * i + c + 1)
                dve.tensor_tensor(WL[:, b, :], RAW[:, b, :], WH[:, b, :].bitcast(F32), ALU.subtract).then_inc(w_lo, 1)

            def mean(bank, width, ready, count):
                dve.wait_ge(ready, count)
                dve.tensor_scalar(MU[:], PS[:, bank, :], 1.0 / width, None, ALU.mult)
                dve.drain()

            def centre(buf, order):
                for n in order:
                    dve.tensor_tensor(buf[:, n, :], buf[:, n, :], MU[:], ALU.subtract).then_inc(n_cent, 1)

            def spread(bank, width, eps, nm, chunks, meanwhile=None, rstd=RSTD):
                base, inst = NORM[nm]
                dve.wait_ge(n_sum, base + chunks)
                dve.tensor_scalar(STD[:], PS[:, bank, :], 1.0 / width, eps, ALU.mult, ALU.add).then_inc(n_var, 1)
                if meanwhile:
                    meanwhile()
                dve.wait_ge(n_std, inst + 1)
                dve.reciprocal(rstd[:], STD[:])
                dve.drain()

            def rows(buf, src, gain, fill):
                for n in range(DC + 1):
                    if n < DC:
                        dve.scalar_tensor_tensor(buf[:, n, :], src[:, n, :], vec(gain, n), RSTD[:], ALU.mult, ALU.mult)\
                           .then_inc(n_row, 1)
                    if n:
                        low(buf, n - 1, fill)

            def low(buf, n, fill):
                dve.wait_ge(h_hi, fill + n + 1)
                dve.tensor_tensor(HL[:, n, :], buf[:, n, :], HH[:, n, :].bitcast(F32), ALU.subtract).then_inc(h_lo, 1)

            def low_scaled(n, gain, fill):
                dve.wait_ge(h_hi, fill + n + 1)
                dve.scalar_tensor_tensor(HL[:, n, :], X[:, n, :], vec(gain, n), HH[:, n, :].bitcast(F32), ALU.mult,
                                         ALU.subtract).then_inc(h_lo, 1)

            def add_out(out_no, last_slot, scale=None, gain=None, fill=None):
                for n in range(DC):
                    if n < DC - 1:
                        dve.wait_ge(y_done, (DC - 1) * out_no + n + 1)
                    else:
                        dve.wait_ge(tile_done, last_slot + 1)
                    if scale is None:
                        dve.tensor_tensor(X[:, n, :], X[:, n, :], PS[:, n, :], ALU.add).then_inc(x_ready, 1)
                    else:
                        dve.scalar_tensor_tensor(X[:, n, :], X[:, n, :], scale, PS[:, n, :], ALU.mult, ALU.add)\
                           .then_inc(x_ready, 1)
                    if gain and n:
                        low_scaled(n - 1, gain, fill)
                if gain:
                    low_scaled(DC - 1, gain, fill)

            split_lo(0, 0)
            dve.wait_ge(c_loaded, 32)
            for n in range(DC):
                low_scaled(n, "even_norm_g", H_FILL["even"])
            split_lo(0, 1)
            spread(2, D, EPS, "even", DC)

            def normed(s):
                dve.wait_ge(tile_done, s + 1)
                if s >= 10:
                    dve.wait_ge(e_gelu, s - 9)
                elif s >= 2:
                    dve.wait_ge(e_glu, s // 2)
                dve.tensor_tensor(ZE[:, s % 2, :], PS[:, s % 2, :], RSTD[:], ALU.mult).then_inc(e_z, 1)

            def glu(j):
                dve.wait_ge(e_sig, j + 1)
                if j == 0:
                    dve.wait_ge(e_pad, 1)
                dve.scalar_tensor_tensor(CB[:, j, PAD:], ZE[:, 0, :], vec("even_b_in", 8 + j), SIG[:], ALU.add, ALU.mult)\
                   .then_inc(e_glu, 1)

            def tap(n, k, before):
                src = CB[:, n, k:k + T]
                w = vec("even_conv_w", n * TAPS + k)
                if k == 0:
                    ins = dve.tensor_scalar(CONV[:, n, :], src, w, vec("even_conv_b", n), ALU.mult, ALU.add)
                else:
                    dve.wait_ge(e_conv, before)
                    ins = dve.scalar_tensor_tensor(CONV[:, n, :], src, w, CONV[:, n, :], ALU.mult, ALU.add)
                ins.then_inc(e_conv, 1)

            def two_chunks(first, last):
                for k in range(first, last):
                    for n in range(2):
                        tap(n, k, 2 * k + n - 1)

            def third_chunk(first, last):
                for k in range(first, last):
                    tap(2, k, 2 * TAPS + k)

            def step(s):
                normed(s)
                split_lo(0, s + 2)

            def mix_y(n):
                dve.wait_ge(e_mix, n + 1)
                dve.tensor_tensor(MIX[:, n % 2, :].rearrange("p (a b) -> p a b", a=TT),
                                  PS[:, 2 + n, :].rearrange("p (a b) -> p a b", a=TT),
                                  BS[:, n:n + 1, :].to_broadcast([P, TT, P]), ALU.add)
                dve.drain()
                dve.wait_ge(e_gelu, HC + n + 1)
                dve.tensor_tensor(Y[:, n, :], MIX[:, n % 2, :], U[:, n, :], ALU.mult).then_inc(e_y, 1)

            done = 0
            for s in range(12):
                step(s)
                if s % 2 and s < 8:
                    glu(s // 2)
                taps = (0, 0, 0, 0, 3, 2, 2, 2, 2, 3, 2, 3)[s]
                two_chunks(done, done + taps)
                done += taps
            two_chunks(done, done + 6)
            mean(2, HALF, n_add, HC)
            centre(V, range(HC))
            two_chunks(done + 6, done + 7)
            step(12)
            two_chunks(done + 7, done + 9)
            spread(3, HALF, EPS, "v", HC, rstd=RSTDV)
            for n in range(HC):
                dve.tensor_tensor(NB[:, n, :], V[:, n, :], RSTDV[:], ALU.mult).then_inc(n_row, 1)
            step(13)
            two_chunks(done + 9, TAPS)
            step(14)
            third_chunk(0, 22)
            step(15)
            third_chunk(22, TAPS)
            dve.wait_ge(s_loaded, 32)
            mean(6, HALF, n_add, 2 * HC)
            centre(CONV, range(HC))
            mix_y(0)
            mix_y(1)
            low(Y, 0, H_FILL["even_out"])
            low(Y, 1, H_FILL["even_out"])

            def other_chunks():
                mix_y(2)
                mix_y(3)
                low(Y, 2, H_FILL["even_out"])
                low(Y, 3, H_FILL["even_out"])

            spread(7, HALF, EPS, "conv", HC, other_chunks, rstd=RSTDV)
            for n in range(HC):
                dve.tensor_tensor(NB[:, n, :], CONV[:, n, :], RSTDV[:], ALU.mult).then_inc(n_row, 1)
            for n in range(HC):
                if n % 2 == 0:
                    split_lo(0, E_OUT + 2 + n // 2)
                low(Y, HC + n, H_FILL["even_out"])
            for k in range(4, DC + 1):
                split_lo(0, E_OUT + k)
            dve.wait_ge(r_loaded, 32)
            add_out(0, E_OUT + DC - 1, gain="ffn_norm_g0", fill=H_FILL["f0"])

            def conv_ffn(l, out_no, gain, fill):
                base = F_UP[l] // 2
                cv = f"ffn_conv{l}"
                split_lo(base, 1)
                spread(2, D, EPS, f"f{l}", DC)

                def normed(i, b, first=False):
                    if not first:
                        dve.wait_ge(f_conv, 2 * FC * l + 2 * i + b - 1)
                    dve.wait_ge(tile_done, 2 * (base + i) + b + 1)
                    dve.tensor_tensor(ZF[:, b, :], PS[:, b, :], RSTD[:], ALU.mult).then_inc(f_z, 1)

                def taps(i, b):
                    w = VEC[:, bass.ds(VEC_AT[cv] + 8 * i + 4 * b, 4)]
                    dve.wait_ge(f_acc, 2 * FC * l + 2 * i + b + 1)
                    for back in (1, 2):
                        acc = ACCS[:, b, back:T]
                        ins = dve.scalar_tensor_tensor(acc, ZF[:, b, 0:T - back], w[:, 2 - back:3 - back], acc, ALU.mult, ALU.add)
                        if back == 1:
                            dve.drain()
                    ins.then_inc(f_conv, 1)

                def gated(i, first=False):
                    if not first:
                        dve.wait_ge(f_mlo, FC * l + i)
                    dve.wait_ge(f_conv, 2 * FC * l + 2 * i + 2)
                    dve.wait_ge(f_silu, FC * l + i + 1)
                    dve.tensor_tensor(MID[:], SG[:], ACCS[:, 1, :], ALU.mult).then_inc(f_mid, 1)

                def gated_low(i):
                    dve.wait_ge(f_mhi, FC * l + i + 1)
                    dve.tensor_tensor(ML[:, bass.ds(i, 1), :], MID[:], MH[:, bass.ds(i, 1), :].bitcast(F32), ALU.subtract)\
                       .then_inc(f_mlo, 1)

                for b in range(2):
                    normed(0, b, first=True)
                    split_lo(base, b + 2)
                    taps(0, b)
                def pair(i, first=False):
                    normed(i, 0)
                    split_lo(base + i, 2)
                    gated(i - 1, first)
                    taps(i, 0)
                    normed(i, 1)
                    split_lo(base + i, 3)
                    taps(i, 1)
                    gated_low(i - 1)

                pair(1, first=True)
                with dve.Fori(2, FC) as i:
                    pair(i)
                gated(FC - 1)
                gated_low(FC - 1)
                down = F_DOWN[l] // 2
                with dve.Fori(1, FC // 2) as i:
                    for b in range(2):
                        split_lo(down + i, b)
                split_lo(down + FC // 2, 0)
                add_out(out_no, F_DOWN[l] + FC - 1, gain=gain, fill=fill)

            conv_ffn(0, 1, "odd_norm_g", H_FILL["odd"])

            def maxima(u, mask, PB=PB, NEGMAX=NEGMAX, SUM=SUM):
                for q, i in enumerate(ROW_ORDER):
                    for e in range(2):
                        w = (i + 1) * P
                        row = slice(ROW_AT[i], ROW_AT[i] + w)
                        if i:
                            dve.wait_ge(at_s[e], 3 * u + q - q // 3 + 1)
                        dve.memset(SUM[:, 4 * e + i:4 * e + i + 1], 0.0)
                        dve.tensor_tensor_reduce(PB[:, e, row], head_banks(e)[:, row], tab(mask)[:, T - w:T], 1.0, 3.0e38,
                                                 ALU.add, ALU.min, NEGMAX[:, 4 * e + i:4 * e + i + 1]).then_inc(at_max, 1)

            def divide(u, gates=None, PB=PB, SUM=SUM, RCP=RCP):
                for e in range(2):
                    dve.wait_ge(at_exp, 8 * u + e + 7)
                    dve.reciprocal(RCP[:, 4 * e:4 * e + 4], SUM[:, 4 * e:4 * e + 4])
                    dve.drain()
                    if gates is not None:
                        dve.tensor_tensor(RCP[:, 4 * e:4 * e + 4], RCP[:, 4 * e:4 * e + 4], gates(e), ALU.mult)
                        dve.drain()
                    for i in range(TT):
                        row = PB[:, e, ROW_AT[i]:ROW_AT[i] + (i + 1) * P]
                        ins = dve.tensor_scalar(row, row, RCP[:, 4 * e + i:4 * e + i + 1], None, ALU.mult)
                    ins.then_inc(at_p, 1)

            base = O_QKV // 2

            def rope(dst, src, bank, side):
                dve.tensor_tensor(dst, src, COSR, ALU.mult)
                dve.tensor_tensor(RT[:, side, :], PS[:, bank, :], SINR, ALU.mult)
                dve.drain()
                return dve.tensor_tensor(dst, dst, RT[:, side, :], ALU.add)

            def ropes(j):
                dve.wait_ge(o_perm, 3 * j + 1)
                rope(QR[:], QRAW[:], 5, 0).then_inc(o_rope, 1)
                dve.wait_ge(o_perm, 3 * j + 2)
                rope(KR[:], KRAW[:], 6, 1).then_inc(o_rope, 1)

            def normed_v(m, c, b):
                dve.wait_ge(tile_done, O_QKV + 6 * m + c + 1)
                dve.tensor_tensor(VRAW[:], PS[:, b, :], RSTD[:], ALU.mult).then_inc(o_v, 1)

            def heads_low(j):
                dve.wait_ge(o_hi, j + 1)
                dve.tensor_tensor(OL[:, bass.ds(j, 1), :], PS[:, 2, :], OH[:, bass.ds(j, 1), :].bitcast(F32), ALU.subtract)\
                   .then_inc(o_lo, 1)

            split_lo(base, 1)
            spread(2, D, EPS, "odd", DC, lambda: split_lo(base, 2))
            dve.tensor_tensor(COSR, tab("cos"), RSTD[:], ALU.mult)
            dve.tensor_tensor(SINR, tab("sin"), RSTD[:], ALU.mult)
            dve.drain()
            ropes(0)
            split_lo(base, 3)
            normed_v(0, 2, 0)

            def pair_step(m, r):
                j = 2 * m + r
                c = 3 * (r + 1)
                split_lo(base + 3 * m, c + 1)
                maxima(j, "dilated")
                divide(j)
                split_lo(base + 3 * m, c + 2)
                heads_low(j)
                ropes(j + 1)
                split_lo(base + 3 * m, c + 3)
                normed_v(m, c + 2, c % 2)

            with dve.Fori(0, PAIRS // 2 - 1) as m:
                for r in range(2):
                    pair_step(m, r)
            pair_step(PAIRS // 2 - 1, 0)
            maxima(PAIRS - 1, "dilated")
            divide(PAIRS - 1)
            heads_low(PAIRS - 1)
            for k in range(DC):
                split_lo(0, O_OUT + k + 1)
            add_out(2, O_OUT + DC - 1, gain="ffn_norm_g1", fill=H_FILL["f1"])
            conv_ffn(1, 3, None, None)

            split_lo(0, L_IN[0] + 1)
            spread(2, D, EPS, "final", DC)
            rows(X, X, "final_norm_g", H_FILL["in0"])

            def layer_norm(nm, fill, slot=None):
                if slot:
                    split_lo(0, slot)
                mean(0, D, n_add, ADD[nm] + DC)
                centre(X, range(DC))
                spread(3, D, LN_EPS, nm, DC)
                gain, bias = nm.replace("_", "_g"), nm.replace("_", "_b")
                for n in range(DC + 1):
                    if n < DC:
                        dve.scalar_tensor_tensor(NB2[:, n, :], X[:, n, :], vec(gain, n), RSTD[:], ALU.mult, ALU.mult)\
                           .then_inc(n_row, 1)
                    if n and fill is not None:
                        dve.wait_ge(h_hi, fill + n)
                        dve.scalar_tensor_tensor(HL[:, n - 1, :], NB2[:, n - 1, :], vec(bias, n - 1), HH[:, n - 1, :].bitcast(F32),
                                                 ALU.add, ALU.subtract).then_inc(h_lo, 1)

            def mix_layer(l):
                z0 = L_IN[l]

                def lo(s):
                    split_lo(0, z0 + s)

                def kept(s):
                    dve.wait_ge(z_kept, Z_TILES * l + s + 1)

                def gate_logs():
                    dve.wait_ge(g_soft, l + 1)
                    ls = LS[:].rearrange("p (a b) c -> p a (b c)", a=2)
                    dve.scalar_tensor_tensor(ls, PS[:, 2:4, 0:4 * GK], 0.0, ls, ALU.min, ALU.subtract).then_inc(g_ls, 1)

                def chunked(x):
                    return x.rearrange("p a (c t) -> p a c t", t=GLA_CHUNK)

                def from_end():
                    dve.wait_ge(g_grow, l + 1)
                    for a in range(2):
                        bc = chunked(BC[:])[:, a]
                        ends = bc[:, :, GLA_CHUNK - 1:GLA_CHUNK].to_broadcast([GK, GLA_CHUNKS, GLA_CHUNK])
                        ins = dve.tensor_tensor(chunked(GB[:])[:, a], ends, bc, ALU.subtract)
                    ins.then_inc(g_diff, 1)

                def decay_queries():
                    kept(Z_GQ + 1)
                    q = ZT[0:GK, Z_GQ:Z_GQ + 2, :]
                    dve.scalar_tensor_tensor(q, q, GLA_DK ** -0.5, GA[:], ALU.mult, ALU.mult).then_inc(g_q, 1)

                def decay_keys():
                    kept(Z_GK + 1)
                    dve.wait_ge(g_end, l + 1)
                    dve.tensor_tensor(GB[:], ZT[0:GK, Z_GK:Z_GK + 2, :], GB[:], ALU.mult).then_inc(g_ke, 1)

                def inverse_keys():
                    dve.wait_ge(g_inv, l + 1)
                    k = ZT[0:GK, Z_GK:Z_GK + 2, :]
                    dve.tensor_tensor(k, k, GA[:], ALU.mult).then_inc(g_ki, 1)

                def turn(q):
                    dve.wait_ge(r_swap, 6 * l + q + 1)
                    z = ZT[:, SWAPS[q][0], :]
                    dve.tensor_tensor(z, z, tab("cos2"), ALU.mult)
                    dve.tensor_tensor(MU[:], PS[:, SWAPS[q][1], :], tab("sin2"), ALU.mult)
                    dve.drain()
                    dve.tensor_tensor(z, z, MU[:], ALU.add).then_inc(r_done, 1)
                    dve.drain()

                def blocks(kv):
                    kept(Z_KC + kv)
                    dve.wait_ge(m_loaded, 80 * (l + 1))
                    if kv:
                        dve.wait_ge(c_hid, 2 * l + 1)
                    z = ZT[:, Z_KC + kv, :].rearrange("p (n s) -> p s n", s=CMP_STRIDE)
                    for part in range(2):
                        js = slice(part * CMP_STRIDE, (part + 1) * CMP_STRIDE)
                        pos = CP[:, kv, js].rearrange("p (s n) -> p s n", n=1).to_broadcast([P, CMP_STRIDE, N_CMP])
                        ins = dve.tensor_tensor(TB[:, js, :], z[:, :, part:part + N_CMP], pos, ALU.add)
                    ins.then_inc(c_tb, 1)

                def cmp_soft(jj):
                    u = NSA_PAIRS * l + jj
                    dve.wait_ge(c_s, u + 1)
                    if jj:
                        dve.wait_ge(c_t, u)
                    for e in range(2):
                        ins = dve.tensor_tensor(PC[:, e * TT:(e + 1) * TT, :].rearrange("p i n -> p (i n)"),
                                                PS[:, (4, 7)[e], 0:TT * N_CMP], tab("cmp_mask"), ALU.add)
                    ins.then_inc(c_sm, 1)
                    dve.drain()
                    dve.tensor_reduce(CM[:], PC[:], AX.X, ALU.min)
                    dve.drain()
                    dve.tensor_scalar(CM[:], CM[:], 1.0e20, None, ALU.min)
                    dve.drain()
                    least = CM[:].rearrange("p (q n) -> p q n", n=1).to_broadcast([P, 8, N_CMP])
                    dve.tensor_tensor(PC[:], PC[:], least, ALU.subtract).then_inc(c_sm, 1)

                def gate(b, jj, e):
                    return GT[:, :, 3 * (NSA_PAIRS * e + jj) + b]

                def cmp_divide(jj):
                    u = NSA_PAIRS * l + jj
                    dve.wait_ge(c_x, u + 1)
                    dve.tensor_reduce(CS[:], PC[:], AX.X, ALU.add)
                    dve.drain()
                    dve.tensor_scalar(CS[:], CS[:], 1.0e-30, None, ALU.max)
                    dve.drain()
                    dve.reciprocal(CS[:], CS[:])
                    dve.drain()
                    dve.wait_ge(g_sig, l + 1)
                    for e in range(2):
                        dve.tensor_tensor(CS[:, TT * e:TT * e + TT], CS[:, TT * e:TT * e + TT], gate(0, jj, e), ALU.mult)
                    dve.drain()
                    share = CS[:].rearrange("p (q n) -> p q n", n=1).to_broadcast([P, 8, N_CMP])
                    dve.tensor_tensor(PC[:], PC[:], share, ALU.mult).then_inc(c_p, 1)

                def cmp_add(jj):
                    dve.wait_ge(c_v, NSA_PAIRS * l + jj + 1)
                    o = ZT[:, NSA_OUT[jj], :]
                    dve.tensor_tensor(o, o, PS[:, 3, :], ALU.add).then_inc(c_acc, 1)
                    dve.drain()

                def unit(k):
                    b, jj = divmod(k, NSA_PAIRS)
                    maxima(UNIT0[l] + k, "causal", PB2, NEGMAX2, SUM2)
                    divide(UNIT0[l] + k, lambda e: gate(1 + b, jj, e), PB2, SUM2, RCP2)

                def unit_add(k):
                    b, jj = divmod(k, NSA_PAIRS)
                    dve.wait_ge(at_o, UNIT0[l] + k + 1)
                    o = ZT[:, NSA_OUT[jj], :]
                    if b == 0:
                        ins = dve.tensor_copy(o, PS[:, 2, :])
                    else:
                        ins = dve.tensor_tensor(o, o, PS[:, 2, :], ALU.add)
                    ins.then_inc(u_acc, 1)
                    dve.drain()

                def states():
                    dve.wait_ge(g_ds, l + 1)
                    for c in range(GLA_CHUNKS - 1):
                        for a in range(2):
                            ds = PS[0:GK, 3 + c % 2, (4 * a + c // 2) * GLA_DV:(4 * a + c // 2 + 1) * GLA_DV]
                            if c == 0:
                                ins = dve.tensor_copy(ST[:, a, 1, :], ds)
                            else:
                                ins = dve.scalar_tensor_tensor(ST[:, a, c + 1, :], ST[:, a, c, :], DEC[:, a, c:c + 1], ds,
                                                               ALU.mult, ALU.add)
                        if c < GLA_CHUNKS - 2:
                            dve.drain()
                    ins.then_inc(g_st, 1)

                def mask_within(n):
                    dve.wait_ge(g_at, 3 * l + n + 1)
                    dve.wait_ge(m_zero, l + 1)
                    if n:
                        dve.wait_ge(g_o, 3 * l + n)
                    mask = tab("gla_mask").bitcast(I32).rearrange("p (a t) -> p a t", a=1).to_broadcast([P, TT, P])
                    for e in range(2):
                        ins = dve.copy_predicated(AT[:, e, :].rearrange("p (a t) -> p a t", a=TT), mask,
                                                  PS[:, 5 + e, :].rearrange("p (a t) -> p a t", a=TT))
                    ins.then_inc(g_am, 1)

                def gla_var(n):
                    dve.wait_ge(g_ms, 3 * l + n + 1)
                    dve.tensor_scalar(ZT[:, Z_OG + n, :], PS[:, 4, :], EPS, None, ALU.add).then_inc(g_var, 1)

                def gla_scale(n):
                    dve.wait_ge(g_sd, 3 * l + n + 1)
                    dve.reciprocal(RSTD[:], ZT[:, Z_OG + n, :])
                    dve.drain()
                    o = ZT[:, Z_GV + n, :]
                    dve.scalar_tensor_tensor(o, o, vec(f"gla_norm_g{l}", n), RSTD[:], ALU.mult, ALU.mult)
                    dve.drain()

                def gla_gate(n):
                    dve.wait_ge(g_sil, l + 1)
                    o = ZT[:, Z_GV + n, :]
                    dve.tensor_tensor(o, o, ZT[:, Z_OG + n, :], ALU.mult).then_inc(g_y, 1)

                def mix_low(c):
                    dve.wait_ge(h_hi, H_FILL[f"out{l}"] + c + 1)
                    dve.tensor_tensor(HL[:, c, :], mixed(c), HH[:, c, :].bitcast(F32), ALU.subtract).then_inc(h_lo, 1)

                def pool_scale(n):
                    dve.wait_ge(p_lin, 2 * l + n + 1)
                    dve.tensor_scalar(PU[:, n, POOL_PAD:], PS[:, (4, 7)[n], :], vec(f"pool_scale{l}", n), None, ALU.mult)\
                       .then_inc(p_y, 1)

                lo(2)
                lo(3)
                turn(0)
                blocks(0)
                lo(4)
                gate_logs()
                lo(5)
                from_end()
                lo(6)
                decay_keys()
                blocks(1)
                lo(7)
                decay_queries()
                inverse_keys()
                lo(8)
                lo(9)
                lo(10)
                lo(11)
                mask_within(0)
                states()
                lo(12)
                mask_within(1)
                turn(1)
                lo(13)
                mask_within(2)
                gla_var(0)
                turn(2)
                lo(14)
                gla_var(1)
                turn(3)
                gla_var(2)
                lo(15)
                unit(0)
                gla_scale(0)
                unit_add(0)
                cmp_soft(0)
                lo(16)
                unit(1)
                cmp_divide(0)
                unit_add(1)
                gla_scale(1)
                turn(4)
                cmp_soft(1)
                lo(17)
                unit(2)
                cmp_divide(1)
                lo(18)
                unit_add(2)
                gla_scale(2)
                cmp_add(0)
                turn(5)
                lo(19)
                unit(3)
                lo(20)
                unit_add(3)
                cmp_soft(2)
                cmp_add(1)
                unit(4)
                cmp_divide(2)
                lo(21)
                unit_add(4)
                pool_scale(0)
                pool_scale(1)
                unit(5)
                lo(22)
                unit_add(5)
                cmp_add(2)
                for c in range(4):
                    mix_low(c)
                lo(23)
                mix_low(4)
                for n in range(3):
                    gla_gate(n)
                for c in range(5, DC):
                    mix_low(c)
                for k in range(2, DC + 1):
                    lo(Z_TILES + k)
                add_out(4 + 3 * l, z0 + Z_TILES + DC - 1, ALPHA)

            def square_ffn(l):
                for half in range(2):
                    up = L_IN[l] + Z_TILES + DC + half * 2 * F2H
                    done = F2C * l + F2H * half
                    with dve.Fori(0, F2H // 2) as i:
                        for b in range(2):
                            dve.wait_ge(q_relu, done + 2 * i + b + 1)
                            dve.tensor_tensor(SB[:, b, :], RB[:, b, :], RB[:, b, :], ALU.mult).then_inc(q_sq, 1)
                            split_lo(up // 2 + i, b + 2)
                            dve.wait_ge(q_hi, done + 2 * i + b + 1)
                            dve.tensor_tensor(ML2[:, bass.ds(2 * i + b, 1), :], SB[:, b, :],
                                              MH2[:, bass.ds(2 * i + b, 1), :].bitcast(F32), ALU.subtract).then_inc(q_lo, 1)
                    last = l == DEPTH2 - 1 and half == 1
                    with dve.Fori(1, F2H // 2) as i:
                        for b in range(2):
                            split_lo((up + F2H) // 2 + i, b)
                    if not last:
                        split_lo((up + F2H) // 2 + F2H // 2, 0)
                    add_out(5 + 3 * l + half, up + 2 * F2H - 1, None if half else ALPHA)
                    if not half:
                        split_lo((up + F2H) // 2 + F2H // 2, 1)

            for l in range(DEPTH2):
                mix_layer(l)
                layer_norm(f"ln1_{l}", H_FILL[f"up{l}"], L_IN[l] + Z_TILES + DC + 1)
                square_ffn(l)
                if l < DEPTH2 - 1:
                    layer_norm(f"ln2_{l}", H_FILL[f"in{l + 1}"], L_IN[l + 1] + 1)
                else:
                    layer_norm(f"ln2_{l}", None)


def _columns(v):
    return np.asarray(v).reshape(-1, P).T


def _by_columns(w):
    k, n = w.shape
    return w.reshape(k // P, P, n // P, P).transpose(2, 1, 0, 3).reshape(-1, D)


def lay_out(a):
    w_in = a["even_w_in"][0]
    za, zb = w_in[:, :D], w_in[:, D:]
    pairs = [np.concatenate([zb[:, n * P:(n + 1) * P], zb[:, HALF + n * P:HALF + (n + 1) * P]], 1) for n in range(HC)]
    stream = [_by_columns(np.concatenate(pairs + [za[:, HALF:], za[:, :HALF]], 1)), a["even_w_out"][0]]

    def ffn(l):
        up = a["ffn_w_up"][l]
        both = np.stack([up[:, :FF].reshape(D, FC, P), up[:, FF:].reshape(D, FC, P)], 2).reshape(D, 2 * FF)
        return [_by_columns(both), a["ffn_w_down"][l]]

    stream += ffn(0)
    qkv = a["odd_w_qkv"][0].reshape(D, 3, PAIRS, P).transpose(0, 2, 1, 3).reshape(D, 3 * D)
    stream += [_by_columns(qkv), a["odd_w_o"][0]]
    stream += ffn(1)
    for l in range(DEPTH2):
        w = a["w_in_2"][l]
        at = np.cumsum([0, 384, 768, 18, 192, 192, 384, 16, 384, 256])
        q, kv, gates, gq, gk, gv, rank, og, pu = (w[:, at[n]:at[n + 1]] for n in range(9))
        none = np.zeros((D, P), np.float32)
        first = np.concatenate([rank, none[:, :GATE_ROW - RANK], gates, none[:, :P - GATE_ROW - gates.shape[1]]], 1)
        kv = kv.reshape(D, 6, P)
        heads = q.reshape(D, 2, NSA_PAIRS, HD).transpose(0, 2, 1, 3).reshape(D, -1)
        threes = [np.concatenate([g[:, n * GK:(n + 1) * GK], none[:, :P - GK]], 1) for g in (gk, gq) for n in range(2)]
        head = [heads[:, n * P:(n + 1) * P] for n in range(NSA_PAIRS)]
        cols = np.concatenate([first, kv[:, 0], kv[:, 1], *threes, gv, kv[:, 2], kv[:, 3], head[0], head[1], pu[:, :P],
                               head[2], pu[:, P:], kv[:, 4], kv[:, 5], og], 1)
        w_out = a["w_out_2"][l]
        nsa = w_out[:384].reshape(2, NSA_PAIRS, HD, D).transpose(1, 0, 2, 3).reshape(-1, D)
        up, down = _by_columns(a["w_up_2"][l]), a["w_down_2"][l]
        half = F2H * P
        gla, pool = w_out[384:768], w_out[768:]
        stream += [_by_columns(cols), nsa[:2 * P], pool, nsa[2 * P:], gla, up[:half], down[:half], up[half:], down[half:]]
    vecs = [_columns(a["even_norm_g"][0]), _columns(a["even_b_in"][0]), _columns(a["even_v_ln_g"][0]),
            _columns(a["even_v_ln_b"][0]),
            a["even_conv_w"][0].reshape(TAPS, HC, P).transpose(2, 1, 0).reshape(P, -1),
            _columns(a["even_conv_b"][0]), _columns(a["even_conv_ln_g"][0]), _columns(a["even_conv_ln_b"][0]),
            _columns(a["odd_norm_g"][0]), _columns(a["final_norm_g"])]
    for l in range(2):
        taps = np.concatenate([a["ffn_conv_w"][l], a["ffn_conv_b"][l][None]], 0)
        vecs += [_columns(a["ffn_norm_g"][l]),
                 taps.reshape(4, 2, FC, P).transpose(3, 2, 1, 0).reshape(P, -1)]
    for l in range(DEPTH2):
        vecs += [_columns(a[n][l]) for n in ("gla_norm_g_2", "pool_scale_2", "ln1_g_2", "ln1_b_2", "ln2_g_2", "ln2_b_2")]
    feeds = {
        "wstream": np.concatenate(stream, 0),
        "xt": a["x"][0].T.reshape(DC, P, T).transpose(1, 0, 2),
        "vecs": np.concatenate(vecs, 1),
        "tables": make_tables(),
        "spatial_w": a["even_w_s"][0].transpose(2, 0, 1),
        "spatial_b": np.repeat(a["even_b_s"][0].reshape(HC, 2, P), HD, 1).transpose(1, 0, 2),
    }
    blocks = np.zeros((DEPTH2, P, 2, P), np.float32)
    second = np.zeros((DEPTH2, P, 2, P), np.float32)
    for g in range(2):
        r = slice(g * HD, (g + 1) * HD)
        for n in range(2):
            blocks[:, r, n, r] = a["pool_w_2"][:, 2 * n + g]
            second[:, r, n, r] = a["cmp_w2_2"][:, n]
    w1 = a["cmp_w1_2"].reshape(DEPTH2, 2, CMP_BLOCK, HD, HD).transpose(0, 3, 1, 2, 4)
    pos = a["cmp_pos_2"].transpose(0, 3, 1, 2)
    feeds |= {
        "gate_w": np.concatenate([a["gla_w_gate2_2"], a["gla_b_gate_2"][:, None]], 1),
        "pool_w": blocks, "cmp_w2": second,
        "cmp_w1": np.concatenate([w1, w1], 1), "cmp_p": np.concatenate([pos, pos], 1),
    }
    return {n: np.ascontiguousarray(v) for n, v in feeds.items()}


def kernel(**inputs):
    import concourse.bacc as bacc
    from concourse.bass_utils import run_bass_kernel_spmd

    feeds = lay_out({n: np.asarray(v) for n, v in inputs.items()})
    nc = bacc.Bacc("TRN2", target_bir_lowering=False, num_devices=1)
    aps = {n: nc.dram_tensor(n, v.shape, F32, kind="ExternalInput").ap() for n, v in feeds.items()}
    out = nc.dram_tensor("out", (P, DC, T), F32, kind="ExternalOutput").ap()
    program(nc, **aps, out=out)
    result = run_bass_kernel_spmd(nc, [feeds], core_ids=[0]).results[0]["out"]
    return result.transpose(1, 0, 2).reshape(D, T).T[None]
```

```python
from contextlib import ExitStack

import numpy as np

import concourse.bass as bass
from concourse import mybir

F32 = mybir.dt.float32
F32R = mybir.dt.float32r
I32 = mybir.dt.int32
ALU = mybir.AluOpType
ACT = mybir.ActivationFunctionType
AX = mybir.AxisListType

P = 128
T = 512
TT = T // P
D = 1024
DC = D // P
X_PARTS = 4
HALF = D // 2
HC = HALF // P
TAPS = 31
PAD = TAPS - 1
DIAG_PARTS = (0, 8, 16, 24, TAPS)
PE_PARTS = (0, 10, 20, TAPS)
FF = 2816
FC = FF // P
FF2 = 4096
F2C = FF2 // P
F2H = F2C // 2
HD = 64
PAIRS = D // P
NSA_PAIRS = 3
N_CMP = 31
CMP_BLOCK, CMP_STRIDE = 32, 16
GLA_CHUNK = 64
GLA_CHUNKS = T // GLA_CHUNK
DEPTH2 = 2
M_LOADS = 5 * 16
EPS = 1e-6
LN_EPS = 1e-5
ALPHA = float((2 * DEPTH2) ** 0.25)
BIG = 1.0e30
SCORE_SCALE = HD ** -0.5

Z_GATE, Z_KC, Z_VC, Z_GK, Z_GQ, Z_GV, Z_KS, Z_VS = 0, 1, 2, 3, 5, 7, 10, 11
Z_Q, Z_PU = (12, 13, 15), (14, 16)
Z_KW, Z_VW, Z_OG = 17, 18, 19
Z_TILES = 22
RANK = 16
GLA_DK, GLA_DV = 32, 64
GK = 3 * GLA_DK
POOL_PAD = 16
GATE_ROW = 32

SWAPS = ((Z_KC, 7), (Z_KS, 2), (Z_Q[0], 2), (Z_Q[1], 2), (Z_Q[2], 3), (Z_KW, 7))

E_IN = 0
E_OUT = E_IN + 16
F_UP = [E_OUT + DC, 0]
F_DOWN = [F_UP[0] + 2 * FC, 0]
O_QKV = F_DOWN[0] + FC
O_OUT = O_QKV + 3 * PAIRS
F_UP[1] = O_OUT + DC
F_DOWN[1] = F_UP[1] + 2 * FC
L_IN = [F_DOWN[1] + FC, 0]
L_SLOTS = Z_TILES + DC + 2 * F2C
L_IN[1] = L_IN[0] + L_SLOTS
SLOTS = L_IN[1] + L_SLOTS

VECS = [("even_norm_g", DC), ("even_b_in", 16), ("even_v_ln_g", HC), ("even_v_ln_b", HC),
        ("even_conv_w", HC * TAPS), ("even_conv_b", HC), ("even_conv_ln_g", HC), ("even_conv_ln_b", HC),
        ("odd_norm_g", DC), ("final_norm_g", DC)]
for _l in range(2):
    VECS += [(f"ffn_norm_g{_l}", DC), (f"ffn_conv{_l}", 2 * FC * 4)]
for _l in range(DEPTH2):
    VECS += [(f"gla_norm_g{_l}", 3), (f"pool_scale{_l}", 2), (f"ln1_g{_l}", DC), (f"ln1_b{_l}", DC),
             (f"ln2_g{_l}", DC), (f"ln2_b{_l}", DC)]
VEC_AT = {}
VEC_COLS = 0
for _n, _w in VECS:
    VEC_AT[_n] = VEC_COLS
    VEC_COLS += _w

VEC_EVEN = VEC_AT["odd_norm_g"]

TABLES = [("identity", P), ("ones", P), ("eps", 2), ("swap2", P), ("cumulate", P), ("head_mean", P),
          ("dilated", T), ("causal", T), ("cos", T), ("sin", T), ("cos2", T), ("sin2", T),
          ("cmp_mask", TT * N_CMP), ("inv_count", 2 * POOL_PAD),
          ("inv_window", 2), ("bias_row", 1), ("gla_mask", P)]
TAB_AT = {}
TAB_COLS = 0
for _n, _w in TABLES:
    TAB_AT[_n] = (TAB_COLS, _w)
    TAB_COLS += _w
TAB_EVEN = TAB_AT["swap2"][0]

UNIT0 = [PAIRS, PAIRS + 2 * NSA_PAIRS]
UNITS = 2 * NSA_PAIRS

FIRST = 5
ADD = {n: 2 * HC + (FIRST + 1) * i for i, n in enumerate(f"ln{a}_{l}" for l in range(DEPTH2) for a in (1, 2))}
ORDER = (2, 3, 4, 5, 6, 7, 0, 1)
CENT = {n: 2 * HC + DC * i for i, n in enumerate(ADD)}
PART = {n: 1 + 2 * i for i, n in enumerate(ADD)}
NORM, _at = {}, 0
for _i, (_n, _w) in enumerate([("even", DC), ("v", HC), ("conv", HC), ("f0", DC), ("odd", DC), ("f1", DC), ("final", DC)]
                              + [(f"ln{a}_{l}", DC) for l in range(DEPTH2) for a in (1, 2)]):
    NORM[_n] = (_at, _i)
    _at += _w
ROWS, _at = {}, 0
for _n, _w in [("v", HC), ("conv", HC), ("final", DC)] + [(f"ln{a}_{l}", DC) for l in range(DEPTH2) for a in (1, 2)]:
    ROWS[_n] = _at
    _at += _w
H_FILL = {n: DC * i for i, n in enumerate(
    ["even", "even_out", "f0", "odd", "f1"] + [f"{a}{l}" for l in range(DEPTH2) for a in ("in", "out", "up")])}
XR = {n: DC * i for i, n in enumerate(
    ["f0", "odd", "f1", "final"] + [f"{a}{l}" for l in range(DEPTH2) for a in ("ln1_", "half", "ln2_")])}


def z_bank(s):
    return (s + (s >= Z_OG)) % 2


def make_tables():
    t = {}
    i = np.arange(P)
    t["identity"] = np.eye(P)
    t["ones"] = np.ones((P, P))
    t["eps"] = np.tile([EPS, LN_EPS], (P, 1))
    swap2 = np.zeros((P, P))
    half, half2 = HD // 2, 8
    for base in (0, HD):
        for d in range(half2):
            swap2[base + half2 + d, base + d] = -1.0
            swap2[base + d, base + half2 + d] = 1.0
    t["swap2"] = swap2
    pos = np.arange(T, dtype=np.float32)
    inv = (np.float32(10000.0) ** (-np.arange(half, dtype=np.float32) / np.float32(half))).astype(np.float32)
    ang = (pos[None, :] * inv[:, None]).astype(np.float32)
    t["cos"] = np.tile(np.cos(ang), (4, 1))
    t["sin"] = np.tile(np.concatenate([-np.sin(ang), np.sin(ang)]), (2, 1))
    inv2 = (np.float32(500000.0) ** (-np.arange(half2, dtype=np.float32) * np.float32(2.0) / np.float32(16))).astype(np.float32)
    ang2 = (pos[None, :] * inv2[:, None]).astype(np.float32)
    cos2, sin2 = np.ones((HD, T)), np.zeros((HD, T))
    cos2[:half2], cos2[half2:2 * half2] = np.cos(ang2), np.cos(ang2)
    sin2[:half2], sin2[half2:2 * half2] = np.sin(ang2), np.sin(ang2)
    t["cos2"], t["sin2"] = np.tile(cos2, (2, 1)), np.tile(sin2, (2, 1))
    same = (i[:, None] // GLA_CHUNK) == (i[None, :] // GLA_CHUNK)
    t["cumulate"] = same & (i[:, None] <= i[None, :])
    t["gla_mask"] = same & (i[:, None] <= i[None, :])
    t["head_mean"] = ((i[:, None] // HD) == (i[None, :] // HD)) / HD
    dist = P * (3 - np.arange(T)[None, :] // P) + i[:, None] - np.arange(T)[None, :] % P
    count = (dist <= 128) * 1 + (dist % 4 == 0) + (dist % 16 == 0)
    count = np.where(dist >= 0, count, 0)
    t["dilated"] = np.where(count > 0, -np.log(np.maximum(count, 1)), BIG)
    t["causal"] = np.where(dist >= 0, 0.0, BIG)
    token = P * np.arange(TT)[None, :, None] + i[:, None, None]
    last = CMP_STRIDE * np.arange(N_CMP)[None, None, :] + CMP_BLOCK - 1
    t["cmp_mask"] = np.where(last <= token, 0.0, BIG).reshape(P, TT * N_CMP)
    count, window = np.zeros((P, 2, POOL_PAD)), np.zeros((P, 2))
    for g, w in enumerate((2, 4, 8, 16)):
        rows = slice(HD * (g % 2), HD * (g % 2) + HD)
        count[rows, g // 2, :] = 1.0 / np.minimum(np.arange(POOL_PAD) + 1, w)
        window[rows, g // 2] = 1.0 / w
    t["inv_count"], t["inv_window"] = count, window
    t["bias_row"] = (i == RANK) * 1.0
    return np.concatenate([np.asarray(t[n], np.float32).reshape(P, w) for n, w in TABLES], axis=1)


def program(nc, wstream, xt, vecs, tables, spatial_w, spatial_b, gate_w, pool_w, cmp_w1, cmp_w2, cmp_p, out):
    with ExitStack() as ctx:
        def sb(name, shape, dt=F32, scope=ctx):
            return scope.enter_context(nc.sbuf_tensor(name, shape, dt))

        def sem(name):
            return ctx.enter_context(nc.semaphore(name))

        PS = ctx.enter_context(nc.psum_tensor("PS", [P, 8, T], F32))
        X = sb("X", [P, DC, T])
        HH = sb("HH", [P, DC, T], F32R)
        HL = sb("HL", [P, DC, T], F32R)
        RAW = sb("RAW", [P, 2, D])
        WH = sb("WH", [P, 2, D], F32R)
        WL = sb("WL", [P, 2, D], F32R)
        VEC = sb("VEC", [P, VEC_COLS])
        TAB = sb("TAB", [P, TAB_COLS])
        MU = sb("MU", [P, T])
        RSTD = sb("RSTD", [P, T])
        STD = sb("STD", [P, T])
        WARM = sb("WARM", [P, len(NORM)])

        def vec(name, j=0):
            return VEC[:, VEC_AT[name] + j:VEC_AT[name] + j + 1]

        def tab(name):
            at, w = TAB_AT[name]
            return TAB[:, at:at + w]

        with ExitStack() as even:
            NB = sb("NB", [P, DC, T], scope=even)
            CB = sb("CB", [P, HC, PAD + T], scope=even)
            CONV = sb("CONV", [P, HC, T], scope=even)
            SIG = sb("SIG", [P, T], scope=even)
            U = sb("U", [P, HC, T], scope=even)
            V = sb("V", [P, HC, T], scope=even)
            VTOK = sb("VTOK", [P, TT, HALF], scope=even)
            WS = sb("WS", [P, 2 * HC, P], scope=even)
            BS = sb("BS", [P, HC, P], scope=even)
            MIX = sb("MIX", [P, 2, T], scope=even)
            Y = sb("Y", [P, DC, T], scope=even)
            ZE = sb("ZE", [P, 2, T], scope=even)
            RSTDV = sb("RSTDV", [P, T], scope=even)
        TAPD = Y[:].rearrange("p a b -> p (a b)")[:, 0:TAPS * P].rearrange("p (k m) -> p k m", m=P)
        with ExitStack() as ffn:
            NBF = sb("NBF", [P, DC, T], scope=ffn)
            MH = sb("MH", [P, FC, T], F32R, scope=ffn)
            ML = sb("ML", [P, FC, T], F32R, scope=ffn)
        ACCS = NBF[:, 0:2, :]
        SG = NBF[:, 2, :]
        MID = NBF[:, 3, :]
        ZF = NBF[:, 4:6, :]
        with ExitStack() as odd:
            NBO = sb("NBO", [P, DC, T], scope=odd)
            COSR, SINR = NBO[:, 0, :], NBO[:, 1, :]
            QRAW = sb("QRAW", [P, T], scope=odd)
            KRAW = sb("KRAW", [P, T], scope=odd)
            VRAW = sb("VRAW", [P, T], scope=odd)
            QR = sb("QR", [P, T], scope=odd)
            KR = sb("KR", [P, T], scope=odd)
            RT = sb("RT", [P, 2, T], scope=odd)
            QS = sb("QS", [P, 2, T], F32R, scope=odd)
            KS = sb("KS", [P, 2, T], F32R, scope=odd)
            KL = sb("KL", [P, T], F32R, scope=odd)
            VT = sb("VT", [P, TT, P], scope=odd)
            PB = sb("PB", [P, 2, 1280], scope=odd)
            PT = sb("PT", [P, 2, 1280], scope=odd)
            NEGMAX = sb("NEGMAX", [P, 8], scope=odd)
            SUM = sb("SUM", [P, 8], scope=odd)
            RCP = sb("RCP", [P, 8], scope=odd)
            OH = sb("OH", [P, PAIRS, T], F32R, scope=odd)
            OL = sb("OL", [P, PAIRS, T], F32R, scope=odd)

        with ExitStack() as mixer:
            ZT = sb("ZT", [P, Z_TILES, T], scope=mixer)
            GVTOK = sb("GVTOK", [P, TT, 6 * GLA_DV], scope=mixer)
            AT = sb("AT", [P, 2, T], scope=mixer)
            GW = sb("GW", [RANK + 1, 2 * GK], scope=mixer)
            PW = sb("PW", [P, 2, P], scope=mixer)
            W2 = sb("W2", [P, 2, P], scope=mixer)
            CP = sb("CP", [P, 2, CMP_BLOCK], scope=mixer)
            GT = sb("GT", [P, TT, 3 * 2 * NSA_PAIRS], scope=mixer)
            VTS = sb("VTS", [P, 2, TT, P], scope=mixer)
            HID = sb("HID", [P, 2, N_CMP], scope=mixer)
            KCS = sb("KCS", [P, N_CMP], scope=mixer)
            VCS = sb("VCS", [N_CMP, P], scope=mixer)
            PC = sb("PC", [P, 8, N_CMP], scope=mixer)
            CM = sb("CM", [P, 8], scope=mixer)
            CS = sb("CS", [P, 8], scope=mixer)
            NEGMAX2 = sb("NEGMAX2", [P, 8], scope=mixer)
            SUM2 = sb("SUM2", [P, 8], scope=mixer)
            RCP2 = sb("RCP2", [P, 8], scope=mixer)
            LS = sb("LS", [P, TT, 2 * GK], scope=mixer)
            BC = sb("BC", [GK, 2, T], scope=mixer)
            GA = sb("GA", [GK, 2, T], scope=mixer)
            GB = sb("GB", [GK, 2, T], scope=mixer)
            DEC = sb("DEC", [GK, 2, GLA_CHUNKS], scope=mixer)
            ST = sb("ST", [GK, 2, GLA_CHUNKS, GLA_DV], scope=mixer)
            PU = sb("PU", [P, 2, POOL_PAD + T], scope=mixer)
            PA = sb("PA", [P, POOL_PAD + T], scope=mixer)
            PD = sb("PD", [P, POOL_PAD + T], scope=mixer)
            with ExitStack() as compress:
                W1 = sb("W1", [P, 2, CMP_BLOCK, HD], scope=compress)
                TB = sb("TB", [P, CMP_BLOCK, N_CMP], scope=compress)
            with ExitStack() as attend:
                PB2 = sb("PB2", [P, 2, 1280], scope=attend)
                PT2 = sb("PT2", [P, 2, 1280], scope=attend)
        KTOK = LS
        SQ = (Z_GATE, *Z_PU)
        PTC = ZT[0:N_CMP, Z_PU[0]:Z_PU[1] + 1:Z_PU[1] - Z_PU[0], :]
        NSA_OUT = (Z_KC, Z_VC, Z_VS)
        with ExitStack() as stacked:
            ZS = sb("ZS", [P, Z_TILES + 5, T], F32R, scope=stacked)
        Z_QS = ((Z_GATE, Z_GK), (Z_GK + 1, Z_GQ), (Z_GQ + 1, Z_TILES))
        Z_KH = ((Z_KW, Z_VW), (Z_TILES + 3, Z_TILES + 4))
        Z_KL = (Z_KS, Z_KW)
        MIX_CHUNKS = [("nsa", 0), ("nsa", 1), ("pool", 0), ("pool", 1), ("nsa", 2), ("gla", 0), ("gla", 1), ("gla", 2)]

        def mixed(c):
            kind, n = MIX_CHUNKS[c]
            return PU[:, n, POOL_PAD:] if kind == "pool" else ZT[:, NSA_OUT[n] if kind == "nsa" else Z_GV + n, :]
        with ExitStack() as ffn2:
            NB2 = sb("NB2", [P, DC, T], scope=ffn2)
            RB = sb("RB", [P, 2, T], scope=ffn2)
            SB = sb("SB", [P, 2, T], scope=ffn2)
            MH2 = sb("MH2", [P, F2H, T], F32R, scope=ffn2)
            ML2 = sb("ML2", [P, F2H, T], F32R, scope=ffn2)

        w_loaded = [sem("w_loaded0"), sem("w_loaded1")]
        w_hi = sem("w_hi")
        w_lo = sem("w_lo")
        tile_done = sem("tile_done")
        x_loaded = [sem(f"x_loaded{n}") for n in range(X_PARTS)]
        c_loaded = sem("c_loaded")
        r_loaded = sem("r_loaded")
        s_loaded = sem("s_loaded")
        out_stored = sem("out_stored")
        y_done = sem("y_done")
        x_ready = sem("x_ready")
        h_hi = sem("h_hi")
        h_lo = sem("h_lo")
        n_sq = sem("n_sq")
        n_part = sem("n_part")
        n_sum = sem("n_sum")
        n_add = sem("n_add")
        n_cent = sem("n_cent")
        n_std = sem("n_std")
        n_row = sem("n_row")
        e_pad = sem("e_pad")
        e_mask = sem("e_mask")
        e_z = sem("e_z")
        e_sig = sem("e_sig")
        e_glu = sem("e_glu")
        e_gelu = sem("e_gelu")
        e_conv = sem("e_conv")
        e_diag = sem("e_diag")
        e_conv3 = sem("e_conv3")
        e_kept3 = sem("e_kept3")
        e_vaff = sem("e_vaff")
        e_vt = sem("e_vt")
        e_vtok = sem("e_vtok")
        e_mix = sem("e_mix")
        e_y = sem("e_y")
        f_z = sem("f_z")
        f_acc = sem("f_acc")
        f_conv = sem("f_conv")
        f_silu = sem("f_silu")
        f_mid = sem("f_mid")
        f_mhi = sem("f_mhi")
        f_mlo = sem("f_mlo")
        o_raw = sem("o_raw")
        o_v = sem("o_v")
        o_rope = sem("o_rope")
        o_high = sem("o_high")
        o_low = sem("o_low")
        o_turn = sem("o_turn")
        o_vt = sem("o_vt")
        o_hi = sem("o_hi")
        o_lo = sem("o_lo")
        at_s = [sem("at_s0"), sem("at_s1")]
        at_max = sem("at_max")
        at_exp = sem("at_exp")
        at_p = sem("at_p")
        at_pt = sem("at_pt")
        at_ptc = sem("at_ptc")
        at_o = sem("at_o")

        m_loaded = sem("m_loaded")
        m_zero = sem("m_zero")
        z_kept = sem("z_kept")
        x_new = sem("x_new")
        g_logit = sem("g_logit")
        g_gate = sem("g_gate")
        g_sig = sem("g_sig")
        g_soft = sem("g_soft")
        g_ls = sem("g_ls")
        g_cum = sem("g_cum")
        g_grow = sem("g_grow")
        g_diff = sem("g_diff")
        g_end = sem("g_end")
        g_q = sem("g_q")
        g_inv = sem("g_inv")
        g_ke = sem("g_ke")
        g_ki = sem("g_ki")
        g_kt = sem("g_kt")
        g_vt = sem("g_vt")
        g_ktok = sem("g_ktok")
        g_vtok = sem("g_vtok")
        g_ds = sem("g_ds")
        g_st = sem("g_st")
        g_at = sem("g_at")
        g_am = sem("g_am")
        g_o = sem("g_o")
        g_ok = sem("g_ok")
        g_ms = sem("g_ms")
        g_var = sem("g_var")
        g_sd = sem("g_sd")
        g_sil = sem("g_sil")
        g_y = sem("g_y")
        r_swap = sem("r_swap")
        r_done = sem("r_done")
        k_own = sem("k_own")
        k_high = sem("k_high")
        k_low = sem("k_low")
        v_turn = sem("v_turn")
        v_kept = sem("v_kept")
        c_tb = sem("c_tb")
        c_hid = sem("c_hid")
        c_gelu = sem("c_gelu")
        c_kv = sem("c_kv")
        c_kept = sem("c_kept")
        c_s = sem("c_s")
        c_sm = sem("c_sm")
        c_x = sem("c_x")
        c_p = sem("c_p")
        c_t = sem("c_t")
        c_ptc = sem("c_ptc")
        c_v = sem("c_v")
        c_acc = sem("c_acc")
        u_acc = sem("u_acc")
        p_sum = sem("p_sum")
        p_lin = sem("p_lin")
        p_y = sem("p_y")
        q_relu = sem("q_relu")
        q_sq = sem("q_sq")
        q_hi = sem("q_hi")
        q_lo = sem("q_lo")

        ROW_AT = {3: 0, 2: 512, 0: 896, 1: 1024}
        ROW_ORDER = (3, 2, 0, 1)
        COL_AT = {0: 0, 1: 512, 3: 896, 2: 1024}

        def head_banks(e):
            return PS[:, 2 + 3 * e:5 + 3 * e, :].rearrange("p a b -> p (a b)")

        block = ctx.enter_context(nc.Block())

        @block.sync
        def _(sp):
            def load_x(n):
                w = DC // X_PARTS
                sp.dma_start(X[:, n * w:(n + 1) * w, :], xt[:, n * w:(n + 1) * w, :]).then_inc(x_loaded[n], 16)

            sp.dma_start(RAW[:, 0, :], wstream[0:P, :]).then_inc(w_loaded[0], 16)
            sp.dma_start(VEC[:, 0:VEC_EVEN], vecs[:, 0:VEC_EVEN]).then_inc(c_loaded, 16)
            load_x(0)
            sp.dma_start(TAB[:, 0:TAB_EVEN], tables[:, 0:TAB_EVEN]).then_inc(c_loaded, 16)
            for n in range(1, X_PARTS):
                load_x(n)
            sp.dma_start(RAW[:, 1, :], wstream[P:2 * P, :]).then_inc(w_loaded[1], 16)
            sp.dma_start(WS[:], spatial_w).then_inc(s_loaded, 16)
            sp.dma_start(BS[:], spatial_b).then_inc(s_loaded, 16)
            sp.dma_start(VEC[:, VEC_EVEN:], vecs[:, VEC_EVEN:]).then_inc(r_loaded, 16)
            sp.dma_start(TAB[:, TAB_EVEN:], tables[:, TAB_EVEN:]).then_inc(r_loaded, 16)
            with sp.Fori(1, SLOTS // 2) as i:
                for b in range(2):
                    sp.wait_ge(w_lo, 2 * i + b - 1)
                    sp.dma_start(RAW[:, b, :], wstream[bass.ds((2 * i + b) * P, P), :]).then_inc(w_loaded[b], 16)
            for n in range(DC):
                sp.wait_ge(x_new, DC * (2 * DEPTH2 - 1) + n + 1)
                sp.dma_start(out[:, n, :], X[:, n, :]).then_inc(out_stored, 16)
            sp.wait_ge(out_stored, 16 * DC)

        @block.gpsimd
        def _(pool):
            pool.memset(CB[:, :, 0:PAD], 0.0).then_inc(e_pad, 1)
            pool.wait_ge(s_loaded, 32)
            pool.affine_select(out=WS[:], in_=WS[:], pattern=[[0, 2 * HC], [1, P]], base=0, channel_multiplier=-1,
                               compare_op=ALU.is_ge, fill=0.0).then_inc(e_mask, 1)

            pool.wait_ge(r_loaded, 32)
            for l in range(DEPTH2):
                pool.wait_ge(tile_done, L_IN[l])
                for dst, src in ((GW, gate_w), (PW, pool_w), (W2, cmp_w2), (CP, cmp_p), (W1, cmp_w1)):
                    pool.dma_start(dst[:], src[l]).then_inc(m_loaded, 16)
                pool.memset(PU[:, :, 0:POOL_PAD], 0.0)
                pool.memset(AT[:], 0.0).then_inc(m_zero, 1)
                for n in range(2):
                    pool.wait_ge(z_kept, Z_TILES * l + Z_PU[n] + 1)
                    if n:
                        pool.drain()
                    src, width = PU[:, n, :], 1
                    for dst in (PA, PD) if n == 0 else (PA, PD, PA, PD):
                        first = 2 * width - 1
                        pool.tensor_tensor(dst[:, first:], src[:, first:], src[:, first - width:POOL_PAD + T - width], ALU.add)
                        pool.drain()
                        src, width = dst, 2 * width
                    for half, win in ((0, PA), (1, PD)):
                        rows = slice(half * HD, (half + 1) * HD)
                        early = tab("inv_count")[rows, n * POOL_PAD:(n + 1) * POOL_PAD]
                        pool.tensor_tensor(win[rows, 0:POOL_PAD], win[rows, POOL_PAD:2 * POOL_PAD], early, ALU.mult)
                        pool.drain()
                        pool.tensor_scalar(win[rows, 2 * POOL_PAD:], win[rows, 2 * POOL_PAD:],
                                           tab("inv_window")[rows, n:n + 1], None, ALU.mult)
                        pool.drain()
                        u = PU[rows, n, :]
                        pool.tensor_tensor(u[:, POOL_PAD:2 * POOL_PAD], win[rows, 0:POOL_PAD], u[:, POOL_PAD:2 * POOL_PAD],
                                           ALU.subtract)
                        last = pool.tensor_tensor(u[:, 2 * POOL_PAD:], win[rows, 2 * POOL_PAD:], u[:, 2 * POOL_PAD:],
                                                  ALU.subtract)
                    last.then_inc(p_sum, 1)

        @block.scalar
        def _(act):
            def split_hi(i, c, first=False):
                b = c % 2
                act.wait_ge(w_loaded[b], 16 * (i + c // 2 + 1))
                if not first:
                    act.wait_ge(tile_done, 2 * i + c - 1)
                act.activation(WH[:, b, :], RAW[:, b, :], ACT.Copy).then_inc(w_hi, 1)

            def squares(buf, src, order, ready, base):
                for q, n in enumerate(order):
                    act.wait_ge(ready, base + q + 1)
                    act.activation(buf[:, n, :], src[:, n, :], ACT.Square).then_inc(n_sq, 1)

            def bring_root(nm):
                n = NORM[nm][1]
                act.activation(WARM[:, n:n + 1], tab("ones")[:, 0:1], ACT.Sqrt)

            def root(nm, bank, width):
                n = NORM[nm][1]
                eps = tab("eps")[:, 1:2] if nm.startswith("ln") else tab("eps")[:, 0:1]
                act.wait_ge(n_sum, n + 1)
                act.activation(STD[:], PS[:, bank, :], ACT.Sqrt, scale=1.0 / width, bias=eps).then_inc(n_std, 1)

            def rows_hi(buf, base):
                for n in range(DC):
                    act.wait_ge(n_row, base + n + 1)
                    act.activation(HH[:, n, :], buf[:, n, :], ACT.Copy).then_inc(h_hi, 1)

            def fill_scaled(buf, gain, waits):
                for n in range(DC):
                    act.wait_ge(*waits[n])
                    act.activation(HH[:, n, :], X[:, n, :], ACT.Identity, scale=vec(gain, n)).then_inc(h_hi, 1)
                    act.activation(buf[:, n, :], X[:, n, :], ACT.Square).then_inc(n_sq, 1)

            def new_x(nm):
                return [(x_ready, XR[nm] + n + 1) for n in range(DC)]

            split_hi(0, 0, first=True)
            act.wait_ge(c_loaded, 32)
            bring_root("even")
            fill_scaled(NB, "even_norm_g", [(x_loaded[n * X_PARTS // DC], 16) for n in range(DC)])
            split_hi(0, 1, first=True)
            root("even", 2, D)
            for j in range(HC):
                split_hi(0, 2 * j + 2)
                split_hi(0, 2 * j + 3)
                act.wait_ge(e_z, 2 * j + 2)
                if j:
                    act.wait_ge(e_glu, j)
                act.activation(SIG[:], ZE[:, 1, :], ACT.Sigmoid, bias=vec("even_b_in", 12 + j)).then_inc(e_sig, 1)

            def gelu(s):
                j = s - 2 * HC
                act.wait_ge(e_z, s + 1)
                dst = V[:, j, :] if j < HC else U[:, j - HC, :]
                act.activation(dst, ZE[:, s % 2, :], ACT.Gelu_apprx_tanh,
                               bias=vec("even_b_in", 4 + j if j < HC else j - HC)).then_inc(e_gelu, 1)

            def y_high(n):
                act.wait_ge(e_y, n + 1)
                act.activation(HH[:, n, :], Y[:, n, :], ACT.Copy).then_inc(h_hi, 1)

            for j in range(HC):
                s = 2 * HC + j
                split_hi(0, s + 2)
                gelu(s)
                for k in range(*DIAG_PARTS[j:j + 2]):
                    ins = act.activation(TAPD[:, k, :], tab("identity"), ACT.Identity,
                                         scale=vec("even_conv_w", (HC - 1) * TAPS + k))
                ins.then_inc(e_diag, 1)
            squares(NB, V, range(HC), n_cent, 0)
            split_hi(0, 14)
            gelu(12)
            bring_root("v")
            root("v", 3, HALF)
            for n in range(HC):
                act.wait_ge(n_row, ROWS["v"] + n + 1)
                act.activation(V[:, n, :], NB[:, n, :], ACT.Identity, scale=vec("even_v_ln_g", n),
                               bias=vec("even_v_ln_b", n)).then_inc(e_vaff, 1)
            split_hi(0, 15)
            gelu(13)
            split_hi(0, 16)
            gelu(14)
            for t in range(TT):
                act.wait_ge(e_vt, t + 1)
                act.activation(VTOK[:, t, :], PS[:, 2 + t, :], ACT.Copy).then_inc(e_vtok, 1)
            split_hi(0, 17)
            act.wait_ge(e_conv3, 1)
            act.activation(CONV[:, HC - 1, :], PS[:, 7, :], ACT.Identity, bias=vec("even_conv_b", HC - 1)).then_inc(e_kept3, 1)
            gelu(15)
            squares(NB, CONV, range(HC), n_cent, HC)
            bring_root("conv")
            y_high(0)
            y_high(1)
            root("conv", 7, HALF)
            y_high(2)
            y_high(3)
            for n in range(HC):
                if n % 2 == 0:
                    split_hi(0, E_OUT + 2 + n // 2)
                act.wait_ge(n_row, ROWS["conv"] + n + 1)
                act.activation(Y[:, HC + n, :], NB[:, n, :], ACT.Silu, scale=vec("even_conv_ln_g", n),
                               bias=vec("even_conv_ln_b", n))
                act.drain()
                act.activation(HH[:, HC + n, :], Y[:, HC + n, :], ACT.Copy).then_inc(h_hi, 1)
            for k in range(4, DC + 1):
                split_hi(0, E_OUT + k)
            act.wait_ge(r_loaded, 32)

            def conv_ffn(l):
                base = F_UP[l] // 2
                cv = f"ffn_conv{l}"
                bring_root(f"f{l}")
                fill_scaled(NBF, f"ffn_norm_g{l}", new_x(f"f{l}"))
                split_hi(base, 1)
                root(f"f{l}", 2, D)

                def last_tap(i, b, first=False):
                    if b == 0 and not first:
                        act.wait_ge(f_silu, FC * l + i)
                    w = VEC[:, bass.ds(VEC_AT[cv] + 8 * i + 4 * b, 4)]
                    act.wait_ge(f_z, 2 * FC * l + 2 * i + b + 1)
                    act.activation(ACCS[:, b, :], ZF[:, b, :], ACT.Identity, scale=w[:, 2:3], bias=w[:, 3:4]).then_inc(f_acc, 1)

                def gate(i):
                    act.wait_ge(f_conv, 2 * FC * l + 2 * i + 1)
                    act.activation(SG[:], ACCS[:, 0, :], ACT.Silu).then_inc(f_silu, 1)

                def high(i):
                    act.wait_ge(f_mid, FC * l + i + 1)
                    act.activation(MH[:, bass.ds(i, 1), :], MID[:], ACT.Copy).then_inc(f_mhi, 1)

                split_hi(base, 2)
                last_tap(0, 0, first=True)
                split_hi(base, 3)
                last_tap(0, 1)
                gate(0)
                with act.Fori(1, FC) as i:
                    split_hi(base + i, 2)
                    last_tap(i, 0)
                    high(i - 1)
                    split_hi(base + i, 3)
                    last_tap(i, 1)
                    gate(i)
                high(FC - 1)
                down = F_DOWN[l] // 2
                with act.Fori(1, FC // 2) as i:
                    for b in range(2):
                        split_hi(down + i, b)
                split_hi(down + FC // 2, 0)

            conv_ffn(0)

            def exps(u, PB=PB, NEGMAX=NEGMAX, SUM=SUM):
                for q, i in enumerate(ROW_ORDER):
                    for e in range(2):
                        w = (i + 1) * P
                        act.wait_ge(at_max, 8 * u + 2 * q + e + 1)
                        row = PB[:, e, ROW_AT[i]:ROW_AT[i] + w]
                        act.activation(row, row, ACT.Exp, scale=-1.0, bias=NEGMAX[:, 4 * e + i:4 * e + i + 1],
                                       accum_out=SUM[:, 4 * e + i:4 * e + i + 1]).then_inc(at_exp, 1)

            def keep_pt(u, PT=PT):
                for e in range(2):
                    act.wait_ge(at_pt, 2 * u + e + 1)
                    act.activation(PT[:, e, :], head_banks(e)[:, 0:1280], ACT.Copy).then_inc(at_ptc, 1)

            bring_root("odd")
            fill_scaled(NBO, "odd_norm_g", new_x("odd"))

            def raw(dst, side, scale, m, c, b):
                act.wait_ge(tile_done, O_QKV + 6 * m + c + 1)
                act.activation(dst, PS[:, b, :], ACT.Copy, scale=scale)
                for head in range(0, P, HD):
                    for to, at in ((head, head + HD // 2), (head + HD // 2, head)):
                        ins = act.activation(RT[to:to + HD // 2, side, :], PS[at:at + HD // 2, b, :], ACT.Copy, scale=scale)
                ins.then_inc(o_raw, 1)

            def raw_k(m, c, b):
                raw(KRAW[:], 0, 1.0, m, c, b)

            def raw_q(m, c, b):
                raw(QRAW[:], 1, -SCORE_SCALE, m, c, b)

            def keep_vt(j, b):
                act.wait_ge(o_turn, j + 1)
                act.activation(VT[:], PS[:, b, :].rearrange("p (a b) -> p a b", a=TT), ACT.Copy).then_inc(o_vt, 1)

            def high_q(j):
                act.wait_ge(o_rope, 2 * j + 2)
                for e in range(2):
                    own = slice(e * HD, (e + 1) * HD)
                    ins = act.activation(QS[own, e, :], QR[own, :], ACT.Copy)
                ins.then_inc(o_high, 1)

            def high_k(j):
                act.wait_ge(o_rope, 2 * j + 1)
                for e in range(2):
                    own, other = slice(e * HD, (e + 1) * HD), slice((1 - e) * HD, (2 - e) * HD)
                    act.activation(KS[own, e, :], KR[own, :], ACT.Copy)
                    ins = act.activation(KS[other, e, :], KR[own, :], ACT.Copy)
                ins.then_inc(o_high, 1)

            def heads_out(j):
                act.wait_ge(at_o, j + 1)
                act.activation(OH[:, bass.ds(j, 1), :], PS[:, 2, :], ACT.Copy).then_inc(o_hi, 1)

            base = O_QKV // 2
            split_hi(base, 1)
            raw_k(0, 0, 0)
            root("odd", 2, D)
            split_hi(base, 2)
            raw_q(0, 1, 1)
            split_hi(base, 3)
            high_k(0)
            high_q(0)

            def pair_step(m, r):
                j = 2 * m + r
                c = 3 * (r + 1)
                exps(j)
                keep_vt(j, (c + 1) % 2)
                split_hi(base + 3 * m, c + 1)
                raw_k(m, c, c % 2)
                keep_pt(j)
                split_hi(base + 3 * m, c + 2)
                high_k(j + 1)
                raw_q(m, c + 1, (c + 1) % 2)
                heads_out(j)
                split_hi(base + 3 * m, c + 3)
                high_q(j + 1)

            with act.Fori(0, PAIRS // 2 - 1) as m:
                for r in range(2):
                    pair_step(m, r)
            pair_step(PAIRS // 2 - 1, 0)
            exps(PAIRS - 1)
            keep_vt(PAIRS - 1, 1)
            keep_pt(PAIRS - 1)
            heads_out(PAIRS - 1)
            for k in range(DC):
                split_hi(0, O_OUT + k + 1)
            conv_ffn(1)

            bring_root("final")
            squares(NBF, X, range(DC), x_ready, XR["final"])
            split_hi(0, L_IN[0] + 1)
            root("final", 2, D)
            rows_hi(X, ROWS["final"])

            def layer_norm(nm, fill):
                bring_root(nm)
                squares(NB2, X, range(DC), n_cent, CENT[nm])
                root(nm, 3, D)
                bias = nm.replace("_", "_b")
                for n in range(DC):
                    act.wait_ge(n_row, ROWS[nm] + n + 1)
                    if fill is not None:
                        act.activation(HH[:, n, :], NB2[:, n, :], ACT.Identity, bias=vec(bias, n)).then_inc(h_hi, 1)
                    act.activation(X[:, n, :], NB2[:, n, :], ACT.Identity, bias=vec(bias, n)).then_inc(x_new, 1)

            def mix_layer(l):
                z0 = L_IN[l]

                def high_queries(jj):
                    act.wait_ge(r_done, 6 * l + 3 + jj)
                    act.wait_ge(*((g_ms, 3 * l + 1), (g_at, 3 * l + 3), (g_o, 3 * l + 3))[jj])
                    act.wait_ge(*((g_at, 3 * l + 2), (g_o, 3 * l + 2), (g_o, 3 * l + 3))[jj])
                    for e in range(2):
                        own = slice(e * HD, (e + 1) * HD)
                        ins = act.activation(ZS[own, Z_QS[jj][e], :], ZT[own, Z_Q[jj], :], ACT.Copy)
                    ins.then_inc(k_high, 1)

                def high_keys(b):
                    act.wait_ge(r_done, 6 * l + (2, 6)[b])
                    if b:
                        act.wait_ge(g_o, 3 * l + 3)
                    for e in range(2):
                        own = slice(e * HD, (e + 1) * HD)
                        ins = act.activation(ZS[own, Z_KH[b][e], :], ZT[own, Z_KL[b], :], ACT.Copy)
                    ins.then_inc(k_own, 1)
                    act.wait_ge(k_own, 2 * l + b + 1)
                    for e in range(2):
                        own, other = slice(e * HD, (e + 1) * HD), slice((1 - e) * HD, (2 - e) * HD)
                        ins = act.activation(ZS[other, Z_KH[b][e], :], ZS[own, Z_KH[b][e], :].bitcast(F32), ACT.Copy)
                    ins.then_inc(k_high, 1)

                def hi(s):
                    split_hi(0, z0 + s)

                def take(s):
                    act.wait_ge(tile_done, z0 + s + 1)
                    ps = PS[:, z_bank(s), :]
                    if s == Z_GATE:
                        ins = act.activation(ZT[:, s, :], ps, ACT.Identity, bias=tab("bias_row"))
                    elif s in Z_PU:
                        act.wait_ge(m_zero, l + 1)
                        ins = act.activation(PU[:, Z_PU.index(s), POOL_PAD:], ps, ACT.Copy)
                    else:
                        ins = act.activation(ZT[:, s, :], ps, ACT.Copy, scale=-SCORE_SCALE if s in Z_Q else 1.0)
                    ins.then_inc(z_kept, 1)

                def gate_logs():
                    act.wait_ge(g_logit, l + 1)
                    ls = LS[:].rearrange("p (a b) c -> p a (b c)", a=2)
                    act.activation(ls, PS[:, 2:4, 0:4 * GK], ACT.Abs)
                    act.drain()
                    act.activation(LS[:], LS[:], ACT.Exp, scale=-1.0)
                    act.drain()
                    act.activation(LS[:], LS[:], ACT.Ln, bias=1.0).then_inc(g_soft, 1)

                def branch_gates():
                    act.wait_ge(g_gate, l + 1)
                    gates = PS[:, 6, :].rearrange("p (a b) -> p a b", a=TT)[:, :, GATE_ROW:GATE_ROW + 6 * NSA_PAIRS]
                    act.activation(GT[:], gates, ACT.Sigmoid).then_inc(g_sig, 1)

                def growth():
                    act.wait_ge(g_cum, l + 1)
                    act.activation(BC[:], PS[0:GK, 4:6, :], ACT.Copy, scale=1.0 / 16)
                    act.drain()
                    act.activation(GA[:], BC[:], ACT.Exp)
                    ends = BC[:].rearrange("p a (c t) -> p a c t", t=GLA_CHUNK)[:, :, :, GLA_CHUNK - 1]
                    act.activation(DEC[:], ends, ACT.Exp).then_inc(g_grow, 1)

                def to_end():
                    act.wait_ge(g_diff, l + 1)
                    act.activation(GB[:], GB[:], ACT.Exp).then_inc(g_end, 1)

                def inverse():
                    act.wait_ge(g_q, l + 1)
                    act.activation(GA[:], BC[:], ACT.Exp, scale=-1.0).then_inc(g_inv, 1)

                def hidden(kv):
                    act.wait_ge(c_hid, 2 * l + kv + 1)
                    act.activation(HID[:, kv, :], PS[:, 2 + kv, 0:N_CMP], ACT.Gelu_apprx_tanh).then_inc(c_gelu, 1)

                def keep_values(b):
                    act.wait_ge(v_turn, 2 * l + b + 1)
                    act.activation(VTS[:, b, :, :], PS[:, (3, 1)[b], :].rearrange("p (a b) -> p a b", a=TT), ACT.Copy)\
                       .then_inc(v_kept, 1)

                def keep_compressed():
                    act.wait_ge(c_kv, l + 1)
                    act.activation(KCS[:], PS[:, 5, 0:N_CMP], ACT.Copy)
                    act.activation(VCS[:], PS[0:N_CMP, 6, 0:P], ACT.Copy).then_inc(c_kept, 1)

                def cmp_exp(jj):
                    act.wait_ge(c_sm, 2 * (NSA_PAIRS * l + jj) + 2)
                    act.activation(PC[:], PC[:], ACT.Exp, scale=-1.0).then_inc(c_x, 1)

                def cmp_keep(jj):
                    act.wait_ge(c_t, NSA_PAIRS * l + jj + 1)
                    act.activation(PTC, PS[0:N_CMP, 5:7, :], ACT.Copy).then_inc(c_ptc, 1)

                def unit(k):
                    exps(UNIT0[l] + k, PB2, NEGMAX2, SUM2)

                def unit_keep(k):
                    keep_pt(UNIT0[l] + k, PT2)

                def keep_gla_keys():
                    act.wait_ge(g_kt, l + 1)
                    view = KTOK[:].rearrange("p (a b) c -> p a (b c)", a=2)
                    act.activation(view[:, 0, :], PS[:, 4, 0:4 * GK], ACT.Copy)
                    act.activation(view[:, 1, :], PS[:, 7, 0:4 * GK], ACT.Copy).then_inc(g_ktok, 1)

                def keep_gla_values():
                    act.wait_ge(g_vt, l + 1)
                    for n in range(3):
                        ins = act.activation(GVTOK[:, :, n * P:(n + 1) * P],
                                             PS[:, 2 + n, :].rearrange("p (a b) -> p a b", a=TT), ACT.Copy)
                    ins.then_inc(g_vtok, 1)

                def gla_out(n):
                    act.wait_ge(g_o, 3 * l + n + 1)
                    act.activation(ZT[:, Z_GV + n, :], PS[:, 7, :], ACT.Copy)
                    act.activation(ZT[:, SQ[n], :], PS[:, 7, :], ACT.Square).then_inc(g_ok, 1)

                def gla_root(n):
                    act.wait_ge(g_var, 3 * l + n + 1)
                    act.activation(ZT[:, Z_OG + n, :], ZT[:, Z_OG + n, :], ACT.Sqrt).then_inc(g_sd, 1)

                def keep(s):
                    hi(s + 1)
                    take(s)

                def mix_high(c):
                    kind, n = MIX_CHUNKS[c]
                    if kind == "nsa":
                        act.wait_ge(u_acc, UNITS * l + NSA_PAIRS + n + 1)
                        act.wait_ge(c_acc, NSA_PAIRS * l + n + 1)
                    elif kind == "pool":
                        act.wait_ge(p_y, 2 * l + n + 1)
                    else:
                        act.wait_ge(g_y, 3 * l + n + 1)
                    act.activation(HH[:, c, :], mixed(c), ACT.Copy).then_inc(h_hi, 1)

                if l:
                    act.wait_ge(x_new, DC * 2 * l)
                take(0)
                keep(1)
                keep(2)
                hi(4)
                gate_logs()
                branch_gates()
                take(3)
                keep(4)
                growth()
                to_end()
                keep(5)
                hidden(0)
                keep(6)
                inverse()
                keep_gla_keys()
                keep(7)
                hidden(1)
                keep(8)
                keep_compressed()
                keep(9)
                hi(11)
                keep_gla_values()
                take(10)
                keep(11)
                gla_out(0)
                hi(13)
                high_keys(0)
                take(12)
                gla_root(0)
                gla_out(1)
                keep_values(0)
                hi(14)
                high_queries(0)
                take(13)
                gla_root(1)
                gla_out(2)
                gla_root(2)
                hi(15)
                unit(0)
                high_queries(1)
                take(14)
                unit_keep(0)
                hi(16)
                cmp_exp(0)
                unit(1)
                take(15)
                unit_keep(1)
                hi(17)
                cmp_keep(0)
                high_queries(2)
                cmp_exp(1)
                take(16)
                hi(18)
                unit(2)
                take(17)
                unit_keep(2)
                hi(19)
                cmp_keep(1)
                high_keys(1)
                take(18)
                hi(20)
                unit(3)
                keep_values(1)
                take(19)
                unit_keep(3)
                hi(21)
                cmp_exp(2)
                unit(4)
                take(20)
                unit_keep(4)
                hi(22)
                cmp_keep(2)
                unit(5)
                take(21)
                unit_keep(5)
                for c in range(4):
                    mix_high(c)
                hi(23)
                mix_high(4)
                act.wait_ge(z_kept, Z_TILES * (l + 1))
                for n in range(3):
                    og = ZT[:, Z_OG + n, :]
                    ins = act.activation(og, og, ACT.Silu)
                ins.then_inc(g_sil, 1)
                for c in range(5, DC):
                    mix_high(c)
                for k in range(2, DC + 2):
                    hi(Z_TILES + k)

            def square_ffn(l):
                for half in range(2):
                    up = L_IN[l] + Z_TILES + DC + half * 2 * F2H
                    done = F2C * l + F2H * half
                    with act.Fori(0, F2H // 2) as i:
                        for b in range(2):
                            act.wait_ge(tile_done, up + 2 * i + b + 1)
                            act.activation(RB[:, b, :], PS[:, b, :], ACT.Relu).then_inc(q_relu, 1)
                            split_hi(up // 2 + i, b + 2)
                            act.wait_ge(q_sq, done + 2 * i + b + 1)
                            act.activation(MH2[:, bass.ds(2 * i + b, 1), :], SB[:, b, :], ACT.Copy).then_inc(q_hi, 1)
                    last = l == DEPTH2 - 1 and half == 1
                    with act.Fori(1, F2H // 2 + (0 if last else 1)) as i:
                        for b in range(2):
                            split_hi((up + F2H) // 2 + i, b)

            for l in range(DEPTH2):
                mix_layer(l)
                layer_norm(f"ln1_{l}", H_FILL[f"up{l}"])
                square_ffn(l)
                layer_norm(f"ln2_{l}", None if l == DEPTH2 - 1 else H_FILL[f"in{l + 1}"])

        @block.tensor
        def _(pe):
            def project(i, c, bank=None, beside=None):
                b = c % 2
                bank = b if bank is None else bank
                pe.wait_ge(w_lo, 2 * i + c + 1)
                for k in range(DC):
                    w = slice(k * P, (k + 1) * P)
                    pe.matmul(PS[:, bank, :], WH[:, b, w], HH[:, k, :], start=(k == 0), stop=False)
                    pe.matmul(PS[:, bank, :], WH[:, b, w], HL[:, k, :], start=False, stop=False)
                    last = pe.matmul(PS[:, bank, :], WL[:, b, w], HH[:, k, :], start=False, stop=(k == DC - 1))
                    if k == DC - 1:
                        last.then_inc(tile_done, 1)
                    if beside:
                        beside(k)

            def add_rows(i, c, rh, rl, first, final, frees=None, order=ORDER):
                b = c % 2
                pe.wait_ge(w_lo, 2 * i + c + 1)
                for n in order if first else range(DC):
                    if frees and n in frees:
                        pe.wait_ge(*frees[n])
                    w = slice(n * P, (n + 1) * P)
                    pe.matmul(PS[:, n, :], WH[:, b, w], rh, start=first, stop=False)
                    pe.matmul(PS[:, n, :], WH[:, b, w], rl, start=False, stop=False)
                    last = pe.matmul(PS[:, n, :], WL[:, b, w], rh, start=False, stop=final)
                    if final and n != DC - 1:
                        last.then_inc(y_done, 1)
                last.then_inc(tile_done, 1)

            def sum_rows(buf, bank, waits, done, part=None):
                for q, (n, *wait) in enumerate(waits):
                    pe.wait_ge(*wait)
                    pe.matmul(PS[:, bank, :], tab("ones"), buf[:, n, :], start=(q == 0),
                              stop=(part is None and q == len(waits) - 1)).then_inc(done, 1)
                if part:
                    pe.wait_ge(*part)
                    pe.matmul(PS[:, bank, :], tab("ones"), MU[:], start=False, stop=True).then_inc(done, 1)

            def sum_squares(buf, n, bank, nm, final, ready=None):
                pe.wait_ge(*(ready or (n_sq, NORM[nm][0] + n + 1)))
                last = pe.matmul(PS[:, bank, :], tab("ones"), buf[:, n, :], start=(n == 0), stop=final)
                if final:
                    last.then_inc(n_sum, 1)

            def first_tiles(i, fill, tiles, buf=None, nm=None):
                pe.wait_ge(w_lo, 2 * i + tiles)
                behind = DC // 2 if tiles == 2 else 2 if buf else 0
                for step in range(DC + behind):
                    for b in range(tiles):
                        k = step - b * behind
                        if not 0 <= k < DC:
                            continue
                        w = slice(k * P, (k + 1) * P)
                        pe.wait_ge(h_lo, fill + k + 1)
                        pe.matmul(PS[:, b, :], WH[:, b, w], HH[:, k, :], start=(k == 0), stop=False)
                        pe.matmul(PS[:, b, :], WH[:, b, w], HL[:, k, :], start=False, stop=False)
                        last = pe.matmul(PS[:, b, :], WL[:, b, w], HH[:, k, :], start=False, stop=(k == DC - 1))
                        if k == DC - 1:
                            last.then_inc(tile_done, 1)
                    if buf and step >= behind:
                        sum_squares(buf, step - behind, 2, nm, step == DC + 1)

            pe.wait_ge(c_loaded, 32)
            first_tiles(0, H_FILL["even"], 1, NB, "even")

            def tile(s):
                if s >= 2:
                    pe.wait_ge(e_z, s - 1)
                project(0, s)

            def taps(part):
                if part == 0:
                    pe.wait_ge(e_glu, HC)
                for k in range(*PE_PARTS[part:part + 2]):
                    if k in DIAG_PARTS:
                        pe.wait_ge(e_diag, DIAG_PARTS.index(k) + 1)
                    last = pe.matmul(PS[:, 7, :], TAPD[:, k, :], CB[:, HC - 1, k:k + T], start=(k == 0), stop=(k == TAPS - 1))
                    if k == TAPS - 1:
                        last.then_inc(e_conv3, 1)

            for s in range(1, 12):
                tile(s)
            taps(0)
            sum_rows(V, 2, [(n, e_gelu, n + 1) for n in range(HC)], n_add)
            tile(12)
            for n in range(HC):
                sum_squares(NB, n, 3, "v", n == HC - 1)
            tile(13)
            taps(1)
            tile(14)
            for t in range(TT):
                for n in range(HC):
                    pe.wait_ge(e_vaff, n + 1)
                    last = pe.transpose(PS[:, 2 + t, n * P:(n + 1) * P], V[:, n, t * P:(t + 1) * P], tab("identity"))
                last.then_inc(e_vt, 1)
            taps(2)
            tile(15)
            pe.wait_ge(e_mask, 1)
            pe.wait_ge(e_vtok, TT)
            for n in range(HC):
                for t in range(TT):
                    for e in range(2):
                        h = 2 * n + e
                        last = pe.matmul(PS[e * HD:(e + 1) * HD, 2 + n, t * P:(t + 1) * P],
                                         VTOK[:, t, h * HD:(h + 1) * HD], WS[:, h, :], start=True, stop=True)
                last.then_inc(e_mix, 1)
            sum_rows(CONV, 6, [(0, e_conv, 2 * TAPS), (1, e_conv, 2 * TAPS), (3, e_kept3, 1), (2, e_conv, 3 * TAPS)], n_add)
            for n in range(HC):
                sum_squares(NB, n, 7, "conv", n == HC - 1)
            frees = {n: (e_y, n - 1) for n in (3, 4, 5)} | {7: (n_std, NORM["conv"][1] + 1), 0: (e_z, 16)}
            for k in range(DC):
                pe.wait_ge(h_lo, H_FILL["even_out"] + k + 1)
                add_rows(0, E_OUT + k, HH[:, k, :], HL[:, k, :], k == 0, k == DC - 1, frees if k == 0 else None,
                         (2, 3, 6, 0, 1, 4, 5, 7))

            def conv_ffn(l):
                base = F_UP[l] // 2
                first_tiles(base, H_FILL[f"f{l}"], 1, NBF, f"f{l}")
                project(base, 1)
                with pe.Fori(1, FC) as i:
                    for b in range(2):
                        pe.wait_ge(f_z, 2 * FC * l + 2 * i + b - 1)
                        project(base + i, b)
                down = F_DOWN[l] // 2
                done = 2 * FC * (l + 1)
                for b in range(2):
                    pe.wait_ge(f_mlo, FC * l + b + 1)
                    add_rows(down, b, MH[:, b, :], ML[:, b, :], b == 0, False,
                             {0: (f_z, done - 1), 1: (f_z, done)} if b == 0 else None)
                with pe.Fori(1, FC // 2 - 1) as i:
                    for b in range(2):
                        k = 2 * i + b
                        pe.wait_ge(f_mlo, FC * l + 2 * i + b + 1)
                        add_rows(down + i, b, MH[:, bass.ds(k, 1), :], ML[:, bass.ds(k, 1), :], False, False)
                for b in range(2):
                    k = FC - 2 + b
                    pe.wait_ge(f_mlo, FC * l + k + 1)
                    add_rows(down + FC // 2 - 1, b, MH[:, k, :], ML[:, k, :], False, b == 1)

            conv_ffn(0)

            def scores(product, frees):
                for i in ROW_ORDER:
                    w = (i + 1) * P
                    for e in range(2):
                        bank = 2 + 3 * e + ROW_AT[i] // T
                        if i and bank in frees:
                            pe.wait_ge(*frees[bank])
                        last = product(head_banks(e)[:, ROW_AT[i]:ROW_AT[i] + w], e, slice(i * P, w), slice(0, w))
                        if i != 2:
                            last.then_inc(at_s[e], 1)

            def turn_p(u, PB=PB):
                for e in range(2):
                    pe.wait_ge(at_p, 2 * u + e + 1)
                    for i in range(TT):
                        for k in range(i + 1):
                            at = COL_AT[k] + (i - k) * P
                            last = pe.transpose(head_banks(e)[:, at:at + P],
                                                PB[:, e, ROW_AT[i] + k * P:ROW_AT[i] + (k + 1) * P], tab("identity"))
                    last.then_inc(at_pt, 1)

            def values(u, vt, PT=PT):
                for e in range(2):
                    pe.wait_ge(at_ptc, 2 * u + e + 1)
                    for k in range(TT):
                        last = pe.matmul(PS[e * HD:(e + 1) * HD, 2, k * P:T], vt[:, k, e * HD:(e + 1) * HD],
                                         PT[:, e, COL_AT[k]:COL_AT[k] + (TT - k) * P], start=(k == 0), stop=(k == TT - 1))
                last.then_inc(at_o, 1)

            base = O_QKV // 2
            def turn_v(j, b):
                pe.wait_ge(o_v, j + 1)
                for t in range(TT):
                    last = pe.transpose(PS[:, b, t * P:(t + 1) * P], VRAW[:, t * P:(t + 1) * P], tab("identity"))
                last.then_inc(o_turn, 1)

            def pair_scores(j):
                def product(out, e, qs, ks):
                    own = slice(e * HD, (e + 1) * HD)
                    pe.matmul(out, QS[:, e, qs], KS[:, e, ks], start=True, stop=False)
                    return pe.matmul(out, QS[own, e, qs], KL[own, ks], start=False, stop=True)

                pe.wait_ge(o_low, 2 * j + 2)
                scores(product, {})

            first_tiles(base, H_FILL["odd"], 1, NBO, "odd")
            project(base, 1)
            pe.wait_ge(o_raw, 1)
            project(base, 2)
            pair_scores(0)
            turn_v(0, 0)

            def pair_step(m, r):
                j = 2 * m + r
                c = 3 * (r + 1)
                pe.wait_ge(o_raw, 2 * j + 2)
                project(base + 3 * m, c)
                turn_p(j)
                pe.wait_ge(o_vt, j + 1)
                project(base + 3 * m, c + 1)
                values(j, VT)
                pe.wait_ge(o_raw, 2 * j + 3)
                project(base + 3 * m, c + 2)
                pe.wait_ge(o_lo, j + 1)
                pair_scores(j + 1)
                turn_v(j + 1, c % 2)

            with pe.Fori(0, PAIRS // 2 - 1) as m:
                for r in range(2):
                    pair_step(m, r)
            pair_step(PAIRS // 2 - 1, 0)
            turn_p(PAIRS - 1)
            values(PAIRS - 1, VT)
            for k in range(DC):
                pe.wait_ge(o_lo, k + 1)
                if k == 0:
                    pe.wait_ge(o_lo, DC)
                add_rows(0, O_OUT + k, OH[:, k, :], OL[:, k, :], k == 0, k == DC - 1)
            conv_ffn(1)

            pe.wait_ge(x_ready, XR["final"] + 3)
            for n in range(FIRST):
                sum_squares(NBF, n, 2, "final", False)
            sum_squares(NBF, FIRST, 2, "final", True, (n_part, 1))

            def layer_norm(nm):
                sum_rows(X, 0, [(n, x_ready, XR[nm] + n + 1) for n in range(FIRST)], n_add, (n_part, PART[nm] + 1))
                for n in range(FIRST):
                    sum_squares(NB2, n, 3, nm, False)
                sum_squares(NB2, FIRST, 3, nm, True, (n_part, PART[nm] + 2))

            def mix_layer(l):
                z0 = L_IN[l]

                def tile(s, beside=None):
                    if s == Z_OG:
                        kept(s - 1)
                    elif s == Z_OG + 1:
                        pe.wait_ge(v_kept, 2 * l + 2)
                    elif s >= 2:
                        kept(s - 2)
                    project(0, z0 + s, z_bank(s), beside)

                def kept(s):
                    pe.wait_ge(z_kept, Z_TILES * l + s + 1)

                def gate_logits():
                    kept(Z_GATE)
                    for t in range(TT):
                        last = pe.transpose(PS[:, 6, t * P:(t + 1) * P], ZT[:, Z_GATE, t * P:(t + 1) * P], tab("identity"))
                    last.then_inc(g_gate, 1)
                    pe.wait_ge(m_loaded, M_LOADS * (l + 1))
                    for t in range(TT):
                        last = pe.matmul(PS[:, 2 + t // 2, (t % 2) * 2 * GK:(t % 2 + 1) * 2 * GK],
                                         ZT[0:RANK + 1, Z_GATE, t * P:(t + 1) * P], GW[:], start=True, stop=True)
                    last.then_inc(g_logit, 1)

                def cumulate():
                    pe.wait_ge(g_ls, l + 1)
                    for a in range(2):
                        for t in range(TT):
                            last = pe.matmul(PS[0:GK, 4 + a, t * P:(t + 1) * P], LS[:, t, a * GK:(a + 1) * GK], tab("cumulate"),
                                             start=True, stop=True)
                    last.then_inc(g_cum, 1)

                def swap(q):
                    kept(SWAPS[q][0])
                    if q:
                        pe.wait_ge(r_done, 6 * l + q)
                    pe.matmul(PS[:, SWAPS[q][1], :], tab("swap2"), ZT[:, SWAPS[q][0], :], start=True, stop=True)\
                      .then_inc(r_swap, 1)

                def hidden(kv):
                    def part(k):
                        if k == 0:
                            pe.wait_ge(c_tb, 2 * l + kv + 1)
                        for t in range(k * CMP_BLOCK // DC, (k + 1) * CMP_BLOCK // DC):
                            for g in range(2):
                                rows = slice(g * HD, (g + 1) * HD)
                                last = pe.matmul(PS[rows, 2 + kv, 0:N_CMP], W1[rows, kv, t, :], TB[rows, t, :], start=(t == 0),
                                                 stop=(t == CMP_BLOCK - 1))
                        if k == DC - 1:
                            last.then_inc(c_hid, 1)
                    return part

                def turn_values(b):
                    kept((Z_VS, Z_VW)[b])
                    for t in range(TT):
                        last = pe.transpose(PS[:, (3, 1)[b], t * P:(t + 1) * P], ZT[:, (Z_VS, Z_VW)[b], t * P:(t + 1) * P],
                                            tab("identity"))
                    last.then_inc(v_turn, 1)

                def compressed():
                    pe.wait_ge(c_gelu, 2 * l + 2)
                    pe.wait_ge(g_grow, l + 1)
                    pe.wait_ge(g_sig, l + 1)
                    pe.matmul(PS[:, 5, 0:N_CMP], W2[:, 0, :], HID[:, 0, :], start=True, stop=True)
                    pe.matmul(PS[0:N_CMP, 6, 0:P], HID[:, 1, :], W2[:, 1, :], start=True, stop=True).then_inc(c_kv, 1)

                def cmp_scores(jj):
                    pe.wait_ge(c_kept, l + 1)
                    pe.wait_ge(r_done, 6 * l + 3 + jj)
                    for e in range(2):
                        rows = slice(e * HD, (e + 1) * HD)
                        for i in range(TT):
                            last = pe.matmul(PS[:, (4, 7)[e], i * N_CMP:(i + 1) * N_CMP],
                                             ZT[rows, Z_Q[jj], i * P:(i + 1) * P], KCS[rows, :],
                                             start=True, stop=True)
                    last.then_inc(c_s, 1)

                def cmp_turn(jj):
                    pe.wait_ge(c_p, NSA_PAIRS * l + jj + 1)
                    for q in range(8):
                        last = pe.transpose(PS[0:N_CMP, 5 + q // TT, (q % TT) * P:(q % TT + 1) * P], PC[:, q, :], tab("identity"))
                    last.then_inc(c_t, 1)

                def cmp_values(jj):
                    pe.wait_ge(c_ptc, NSA_PAIRS * l + jj + 1)
                    for e in range(2):
                        last = pe.matmul(PS[e * HD:(e + 1) * HD, 3, :], VCS[:, e * HD:(e + 1) * HD], PTC[:, e, :],
                                         start=True, stop=True)
                    last.then_inc(c_v, 1)

                def unit_scores(k, frees):
                    b, jj = divmod(k, NSA_PAIRS)

                    def product(out, e, qs, ks):
                        own = slice(e * HD, (e + 1) * HD)
                        pe.matmul(out, ZS[:, Z_QS[jj][e], qs], ZS[:, Z_KH[b][e], ks], start=True, stop=False)
                        return pe.matmul(out, ZS[own, Z_QS[jj][e], qs], ZS[own, Z_KL[b], ks], start=False, stop=True)

                    pe.wait_ge(k_low, 5 * l + (2, 3, 4, 5, 5, 5)[k])
                    pe.wait_ge(k_high, 5 * l + (2, 3, 4, 5, 5, 5)[k])
                    scores(product, {2: (u_acc, UNITS * l + k)} | frees)

                def unit_values(k):
                    turn_p(UNIT0[l] + k, PB2)
                    values(UNIT0[l] + k, VTS[:, k // NSA_PAIRS, :, :], PT2)

                def turn_gla_keys():
                    pe.wait_ge(g_ke, l + 1)
                    pe.wait_ge(g_grow, l + 1)
                    pe.wait_ge(r_done, 6 * l + 1)
                    for t in range(TT):
                        for a in range(2):
                            at = (t % 2) * 2 * GK + a * GK
                            last = pe.transpose(PS[:, 4 if t < 2 else 7, at:at + GK], GB[:, a, t * P:(t + 1) * P],
                                                tab("identity")[0:GK, 0:GK])
                    last.then_inc(g_kt, 1)

                def turn_gla_values():
                    kept(Z_GV + 2)
                    pe.wait_ge(c_gelu, 2 * l + 2)
                    pe.wait_ge(g_ktok, l + 1)
                    for n in range(3):
                        for t in range(TT):
                            last = pe.transpose(PS[:, 2 + n, t * P:(t + 1) * P], ZT[:, Z_GV + n, t * P:(t + 1) * P],
                                                tab("identity"))
                    last.then_inc(g_vt, 1)

                def chunk_states():
                    pe.wait_ge(g_ktok, l + 1)
                    pe.wait_ge(g_vtok, l + 1)
                    for a in range(2):
                        for c in range(GLA_CHUNKS - 1):
                            rows = slice((c % 2) * GLA_CHUNK, (c % 2 + 1) * GLA_CHUNK)
                            for h in range(3):
                                k = a * GK + h * GLA_DK
                                v = (3 * a + h) * GLA_DV
                                at = (4 * a + c // 2) * GLA_DV
                                last = pe.matmul(PS[h * GLA_DK:(h + 1) * GLA_DK, 3 + c % 2, at:at + GLA_DV],
                                                 KTOK[rows, c // 2, k:k + GLA_DK], GVTOK[rows, c // 2, v:v + GLA_DV],
                                                 start=True, stop=True)
                    last.then_inc(g_ds, 1)

                def within(n):
                    pe.wait_ge(g_ki, l + 1)
                    pe.wait_ge(c_kept, l + 1)
                    if n:
                        pe.wait_ge(g_am, 3 * l + n)
                    for e in range(2):
                        a, h = divmod(2 * n + e, 3)
                        rows = slice(h * GLA_DK, (h + 1) * GLA_DK)
                        for t in range(TT):
                            cols = slice(t * P, (t + 1) * P)
                            last = pe.matmul(PS[:, 5 + e, cols], ZT[rows, Z_GK + a, cols], ZT[rows, Z_GQ + a, cols],
                                             start=True, stop=True)
                    last.then_inc(g_at, 1)

                def gla_values(n):
                    pe.wait_ge(g_am, 3 * l + n + 1)
                    pe.wait_ge(g_st, l + 1)
                    if n:
                        pe.wait_ge(g_ok, 3 * l + n)
                    for e in range(2):
                        a, h = divmod(2 * n + e, 3)
                        rows = slice(h * GLA_DK, (h + 1) * GLA_DK)
                        v = (2 * n + e) * GLA_DV
                        for t in range(TT):
                            pe.matmul(PS[e * HD:(e + 1) * HD, 7, t * P:(t + 1) * P], GVTOK[:, t, v:v + GLA_DV],
                                      AT[:, e, t * P:(t + 1) * P], start=True, stop=False)
                            for c in (2 * t, 2 * t + 1):
                                if c:
                                    cols = slice(c * GLA_CHUNK, (c + 1) * GLA_CHUNK)
                                    last = pe.matmul(PS[e * HD:(e + 1) * HD, 7, cols], ST[rows, a, c, :], ZT[rows, Z_GQ + a, cols],
                                                     start=False, stop=(c == 2 * t + 1))
                    last.then_inc(g_o, 1)

                def gla_squares(n):
                    pe.wait_ge(g_ok, 3 * l + n + 1)
                    if n:
                        pe.wait_ge(g_var, 3 * l + n)
                    pe.matmul(PS[:, 4, :], tab("head_mean"), ZT[:, SQ[n], :], start=True, stop=True).then_inc(g_ms, 1)

                def pool_mix(n):
                    pe.wait_ge(p_sum, 2 * l + n + 1)
                    pe.matmul(PS[:, (4, 7)[n], :], PW[:, n, :], PU[:, n, POOL_PAD:], start=True, stop=True).then_inc(p_lin, 1)

                first_tiles(z0 // 2, H_FILL[f"in{l}"], 2)
                tile(2)
                gate_logits()
                swap(0)
                tile(3)
                tile(4)
                cumulate()
                tile(5, hidden(0))
                tile(6)
                turn_gla_keys()
                tile(7, hidden(1))
                tile(8)
                compressed()
                tile(9)
                turn_gla_values()
                tile(10)
                within(0)
                chunk_states()
                tile(11)
                gla_values(0)
                within(1)
                swap(1)
                tile(12)
                gla_squares(0)
                gla_values(1)
                within(2)
                turn_values(0)
                swap(2)
                tile(13)
                gla_squares(1)
                gla_values(2)
                swap(3)
                gla_squares(2)
                unit_scores(0, {2: (r_done, 6 * l + 4), 3: (v_kept, 2 * l + 1), 4: (g_var, 3 * l + 3),
                                5: (g_am, 3 * l + 3), 7: (g_ok, 3 * l + 3)})
                tile(14)
                unit_values(0)
                cmp_scores(0)
                unit_scores(1, {4: (c_sm, 6 * l + 1)})
                tile(15)
                unit_values(1)
                swap(4)
                cmp_turn(0)
                cmp_scores(1)
                tile(16)
                unit_scores(2, {4: (c_sm, 6 * l + 3), 5: (c_ptc, 3 * l + 1)})
                tile(17)
                unit_values(2)
                swap(5)
                cmp_values(0)
                cmp_turn(1)
                tile(18)
                unit_scores(3, {3: (c_acc, 3 * l + 1), 5: (c_ptc, 3 * l + 2)})
                turn_values(1)
                tile(19)
                unit_values(3)
                cmp_scores(2)
                cmp_values(1)
                unit_scores(4, {3: (c_acc, 3 * l + 2), 4: (c_sm, 6 * l + 5)})
                tile(20)
                unit_values(4)
                cmp_turn(2)
                pool_mix(0)
                pool_mix(1)
                unit_scores(5, {4: (p_y, 2 * l + 1), 5: (c_ptc, 3 * l + 3), 7: (p_y, 2 * l + 2)})
                tile(21)
                unit_values(5)
                cmp_values(2)
                frees = {0: (z_kept, Z_TILES * (l + 1)), 2: (u_acc, UNITS * (l + 1)), 3: (c_acc, 3 * l + 3)}
                for k in range(DC):
                    pe.wait_ge(h_lo, H_FILL[f"out{l}"] + k + 1)
                    add_rows(0, z0 + Z_TILES + k, HH[:, k, :], HL[:, k, :], k == 0, k == DC - 1, frees if k == 0 else None,
                             (4, 5, 6, 7, 0, 1, 3, 2))

            def square_ffn(l):
                for half in range(2):
                    up = L_IN[l] + Z_TILES + DC + half * 2 * F2H
                    done = F2C * l + F2H * half
                    if half:
                        pe.wait_ge(x_ready, XR[f"half{l}"] + 1)
                        project(up // 2, 0)
                        pe.wait_ge(x_ready, XR[f"half{l}"] + 2)
                        project(up // 2, 1)
                    else:
                        first_tiles(up // 2, H_FILL[f"up{l}"], 2)
                    with pe.Fori(1, F2H // 2) as i:
                        for b in range(2):
                            pe.wait_ge(q_relu, done + 2 * i + b - 1)
                            project(up // 2 + i, b)
                    down = (up + F2H) // 2
                    if half:
                        pe.wait_ge(x_ready, XR[f"half{l}"] + DC)
                    for b in range(2):
                        pe.wait_ge(q_lo, done + b + 1)
                        add_rows(down, b, MH2[:, b, :], ML2[:, b, :], b == 0, False,
                                 {0: (q_relu, done + F2H - 1), 1: (q_relu, done + F2H)} if b == 0 else None)
                    with pe.Fori(1, F2H // 2 - 1) as i:
                        for b in range(2):
                            k = 2 * i + b
                            pe.wait_ge(q_lo, done + 2 * i + b + 1)
                            add_rows(down + i, b, MH2[:, bass.ds(k, 1), :], ML2[:, bass.ds(k, 1), :], False, False)
                    for b in range(2):
                        k = F2H - 2 + b
                        pe.wait_ge(q_lo, done + k + 1)
                        add_rows(down + F2H // 2 - 1, b, MH2[:, k, :], ML2[:, k, :], False, b == 1)

            for l in range(DEPTH2):
                mix_layer(l)
                layer_norm(f"ln1_{l}")
                square_ffn(l)
                layer_norm(f"ln2_{l}")

        @block.vector
        def _(dve):
            def split_lo(i, c):
                b = c % 2
                dve.wait_ge(w_hi, 2 * i + c + 1)
                dve.tensor_tensor(WL[:, b, :], RAW[:, b, :], WH[:, b, :].bitcast(F32), ALU.subtract).then_inc(w_lo, 1)

            def mean(bank, width, ready, count):
                dve.wait_ge(ready, count)
                dve.tensor_scalar(MU[:], PS[:, bank, :], 1.0 / width, None, ALU.mult)
                dve.drain()

            def squares_part(buf, first, nm):
                for n in range(first + 1, DC):
                    dve.wait_ge(n_sq, NORM[nm][0] + n + 1)
                    ins = dve.tensor_tensor(buf[:, first, :], buf[:, first, :], buf[:, n, :], ALU.add)
                    if n < DC - 1:
                        dve.drain()
                ins.then_inc(n_part, 1)

            def centre(buf, order):
                for n in order:
                    dve.tensor_tensor(buf[:, n, :], buf[:, n, :], MU[:], ALU.subtract).then_inc(n_cent, 1)

            def spread(nm, rstd=RSTD):
                dve.wait_ge(n_std, NORM[nm][1] + 1)
                dve.reciprocal(rstd[:], STD[:])
                dve.drain()

            def rows(buf, src, gain, fill):
                for n in range(DC + 1):
                    if n < DC:
                        dve.scalar_tensor_tensor(buf[:, n, :], src[:, n, :], vec(gain, n), RSTD[:], ALU.mult, ALU.mult)\
                           .then_inc(n_row, 1)
                    if n:
                        low(buf, n - 1, fill)

            def low(buf, n, fill):
                dve.wait_ge(h_hi, fill + n + 1)
                dve.tensor_tensor(HL[:, n, :], buf[:, n, :], HH[:, n, :].bitcast(F32), ALU.subtract).then_inc(h_lo, 1)

            def low_scaled(n, gain, fill):
                dve.wait_ge(h_hi, fill + n + 1)
                dve.scalar_tensor_tensor(HL[:, n, :], X[:, n, :], vec(gain, n), HH[:, n, :].bitcast(F32), ALU.mult,
                                         ALU.subtract).then_inc(h_lo, 1)

            def add_out(out_no, last_slot, scale=None, gain=None, fill=None):
                for n in range(DC):
                    if n < DC - 1:
                        dve.wait_ge(y_done, (DC - 1) * out_no + n + 1)
                    else:
                        dve.wait_ge(tile_done, last_slot + 1)
                    if scale is None:
                        dve.tensor_tensor(X[:, n, :], X[:, n, :], PS[:, n, :], ALU.add).then_inc(x_ready, 1)
                    else:
                        dve.scalar_tensor_tensor(X[:, n, :], X[:, n, :], scale, PS[:, n, :], ALU.mult, ALU.add)\
                           .then_inc(x_ready, 1)
                    if gain and n:
                        low_scaled(n - 1, gain, fill)
                if gain:
                    low_scaled(DC - 1, gain, fill)

            split_lo(0, 0)
            dve.wait_ge(c_loaded, 32)
            for n in range(DC):
                low_scaled(n, "even_norm_g", H_FILL["even"])
            split_lo(0, 1)
            spread("even")

            def normed(s):
                dve.wait_ge(tile_done, s + 1)
                if s >= 10:
                    dve.wait_ge(e_gelu, s - 9)
                elif s >= 2:
                    dve.wait_ge(e_glu, s // 2)
                dve.tensor_tensor(ZE[:, s % 2, :], PS[:, s % 2, :], RSTD[:], ALU.mult).then_inc(e_z, 1)

            def glu(j):
                dve.wait_ge(e_sig, j + 1)
                if j == 0:
                    dve.wait_ge(e_pad, 1)
                dve.scalar_tensor_tensor(CB[:, j, PAD:], ZE[:, 0, :], vec("even_b_in", 8 + j), SIG[:], ALU.add, ALU.mult)\
                   .then_inc(e_glu, 1)

            def tap(n, k, before):
                src = CB[:, n, k:k + T]
                w = vec("even_conv_w", n * TAPS + k)
                if k == 0:
                    ins = dve.tensor_scalar(CONV[:, n, :], src, w, vec("even_conv_b", n), ALU.mult, ALU.add)
                else:
                    dve.wait_ge(e_conv, before)
                    ins = dve.scalar_tensor_tensor(CONV[:, n, :], src, w, CONV[:, n, :], ALU.mult, ALU.add)
                ins.then_inc(e_conv, 1)

            def two_chunks(first, last):
                for k in range(first, last):
                    for n in range(2):
                        tap(n, k, 2 * k + n - 1)

            def third_chunk(first, last):
                for k in range(first, last):
                    tap(2, k, 2 * TAPS + k)

            def step(s):
                normed(s)
                split_lo(0, s + 2)

            def mix_y(n):
                dve.wait_ge(e_mix, n + 1)
                dve.tensor_tensor(MIX[:, n % 2, :].rearrange("p (a b) -> p a b", a=TT),
                                  PS[:, 2 + n, :].rearrange("p (a b) -> p a b", a=TT),
                                  BS[:, n:n + 1, :].to_broadcast([P, TT, P]), ALU.add)
                dve.drain()
                dve.wait_ge(e_gelu, HC + n + 1)
                dve.tensor_tensor(Y[:, n, :], MIX[:, n % 2, :], U[:, n, :], ALU.mult).then_inc(e_y, 1)

            done = 0
            for s in range(12):
                step(s)
                if s % 2 and s < 8:
                    glu(s // 2)
                taps = (0, 0, 0, 0, 3, 2, 2, 2, 2, 3, 2, 3)[s]
                two_chunks(done, done + taps)
                done += taps
            two_chunks(done, done + 6)
            mean(2, HALF, n_add, HC)
            centre(V, range(HC))
            two_chunks(done + 6, done + 7)
            step(12)
            two_chunks(done + 7, done + 9)
            spread("v", RSTDV)
            for n in range(HC):
                dve.tensor_tensor(NB[:, n, :], V[:, n, :], RSTDV[:], ALU.mult).then_inc(n_row, 1)
            step(13)
            two_chunks(done + 9, TAPS)
            step(14)
            third_chunk(0, 22)
            step(15)
            third_chunk(22, TAPS)
            dve.wait_ge(s_loaded, 32)
            mean(6, HALF, n_add, 2 * HC)
            centre(CONV, range(HC))
            mix_y(0)
            mix_y(1)
            low(Y, 0, H_FILL["even_out"])
            low(Y, 1, H_FILL["even_out"])

            for n in (2, 3):
                mix_y(n)
            for n in (2, 3):
                low(Y, n, H_FILL["even_out"])
            spread("conv", RSTDV)
            for n in range(HC):
                dve.tensor_tensor(NB[:, n, :], CONV[:, n, :], RSTDV[:], ALU.mult).then_inc(n_row, 1)
            for n in range(HC):
                if n % 2 == 0:
                    split_lo(0, E_OUT + 2 + n // 2)
                low(Y, HC + n, H_FILL["even_out"])
            for k in range(4, DC + 1):
                split_lo(0, E_OUT + k)
            dve.wait_ge(r_loaded, 32)
            add_out(0, E_OUT + DC - 1, gain="ffn_norm_g0", fill=H_FILL["f0"])

            def conv_ffn(l, out_no, gain, fill):
                base = F_UP[l] // 2
                cv = f"ffn_conv{l}"
                split_lo(base, 1)
                spread(f"f{l}")

                def normed(i, b, first=False):
                    if not first:
                        dve.wait_ge(f_conv, 2 * FC * l + 2 * i + b - 1)
                    dve.wait_ge(tile_done, 2 * (base + i) + b + 1)
                    dve.tensor_tensor(ZF[:, b, :], PS[:, b, :], RSTD[:], ALU.mult).then_inc(f_z, 1)

                def taps(i, b):
                    w = VEC[:, bass.ds(VEC_AT[cv] + 8 * i + 4 * b, 4)]
                    dve.wait_ge(f_acc, 2 * FC * l + 2 * i + b + 1)
                    for back in (1, 2):
                        acc = ACCS[:, b, back:T]
                        ins = dve.scalar_tensor_tensor(acc, ZF[:, b, 0:T - back], w[:, 2 - back:3 - back], acc, ALU.mult, ALU.add)
                        if back == 1:
                            dve.drain()
                    ins.then_inc(f_conv, 1)

                def gated(i, first=False):
                    if not first:
                        dve.wait_ge(f_mlo, FC * l + i)
                    dve.wait_ge(f_conv, 2 * FC * l + 2 * i + 2)
                    dve.wait_ge(f_silu, FC * l + i + 1)
                    dve.tensor_tensor(MID[:], SG[:], ACCS[:, 1, :], ALU.mult).then_inc(f_mid, 1)

                def gated_low(i):
                    dve.wait_ge(f_mhi, FC * l + i + 1)
                    dve.tensor_tensor(ML[:, bass.ds(i, 1), :], MID[:], MH[:, bass.ds(i, 1), :].bitcast(F32), ALU.subtract)\
                       .then_inc(f_mlo, 1)

                for b in range(2):
                    normed(0, b, first=True)
                    split_lo(base, b + 2)
                    taps(0, b)
                def pair(i, first=False):
                    normed(i, 0)
                    split_lo(base + i, 2)
                    gated(i - 1, first)
                    taps(i, 0)
                    normed(i, 1)
                    split_lo(base + i, 3)
                    taps(i, 1)
                    gated_low(i - 1)

                pair(1, first=True)
                with dve.Fori(2, FC) as i:
                    pair(i)
                gated(FC - 1)
                gated_low(FC - 1)
                down = F_DOWN[l] // 2
                with dve.Fori(1, FC // 2) as i:
                    for b in range(2):
                        split_lo(down + i, b)
                split_lo(down + FC // 2, 0)
                add_out(out_no, F_DOWN[l] + FC - 1, gain=gain, fill=fill)

            conv_ffn(0, 1, "odd_norm_g", H_FILL["odd"])

            def maxima(u, mask, PB=PB, NEGMAX=NEGMAX, SUM=SUM):
                for q, i in enumerate(ROW_ORDER):
                    for e in range(2):
                        w = (i + 1) * P
                        row = slice(ROW_AT[i], ROW_AT[i] + w)
                        if i:
                            dve.wait_ge(at_s[e], 3 * u + q - q // 3 + 1)
                        dve.memset(SUM[:, 4 * e + i:4 * e + i + 1], 0.0)
                        dve.tensor_tensor_reduce(PB[:, e, row], head_banks(e)[:, row], tab(mask)[:, T - w:T], 1.0, 3.0e38,
                                                 ALU.add, ALU.min, NEGMAX[:, 4 * e + i:4 * e + i + 1]).then_inc(at_max, 1)

            def divide(u, gates=None, PB=PB, SUM=SUM, RCP=RCP):
                for e in range(2):
                    dve.wait_ge(at_exp, 8 * u + e + 7)
                    dve.reciprocal(RCP[:, 4 * e:4 * e + 4], SUM[:, 4 * e:4 * e + 4])
                    dve.drain()
                    if gates is not None:
                        dve.tensor_tensor(RCP[:, 4 * e:4 * e + 4], RCP[:, 4 * e:4 * e + 4], gates(e), ALU.mult)
                        dve.drain()
                    for i in range(TT):
                        row = PB[:, e, ROW_AT[i]:ROW_AT[i] + (i + 1) * P]
                        ins = dve.tensor_scalar(row, row, RCP[:, 4 * e + i:4 * e + i + 1], None, ALU.mult)
                    ins.then_inc(at_p, 1)

            base = O_QKV // 2

            def rope(raw, dst, side, j):
                dve.wait_ge(o_raw, 2 * j + side + 1)
                dve.tensor_tensor(dst, raw, COSR, ALU.mult)
                dve.tensor_tensor(RT[:, side, :], RT[:, side, :], SINR, ALU.mult)
                dve.drain()
                dve.tensor_tensor(dst, dst, RT[:, side, :], ALU.add).then_inc(o_rope, 1)

            def rope_q(j):
                rope(QRAW[:], QR[:], 1, j)

            def rope_k(j):
                rope(KRAW[:], KR[:], 0, j)

            def low_q(j):
                dve.wait_ge(o_high, 2 * j + 2)
                for e in range(2):
                    own, other = slice(e * HD, (e + 1) * HD), slice((1 - e) * HD, (2 - e) * HD)
                    ins = dve.tensor_tensor(QS[other, e, :], QR[own, :], QS[own, e, :].bitcast(F32), ALU.subtract)
                ins.then_inc(o_low, 1)

            def low_k(j):
                dve.wait_ge(o_high, 2 * j + 1)
                for e in range(2):
                    own = slice(e * HD, (e + 1) * HD)
                    ins = dve.tensor_tensor(KL[own, :], KR[own, :], KS[own, e, :].bitcast(F32), ALU.subtract)
                ins.then_inc(o_low, 1)

            def normed_v(m, c, b):
                dve.wait_ge(tile_done, O_QKV + 6 * m + c + 1)
                dve.tensor_tensor(VRAW[:], PS[:, b, :], RSTD[:], ALU.mult).then_inc(o_v, 1)

            def heads_low(j):
                dve.wait_ge(o_hi, j + 1)
                dve.tensor_tensor(OL[:, bass.ds(j, 1), :], PS[:, 2, :], OH[:, bass.ds(j, 1), :].bitcast(F32), ALU.subtract)\
                   .then_inc(o_lo, 1)

            split_lo(base, 1)
            split_lo(base, 2)
            spread("odd")
            dve.tensor_tensor(COSR, tab("cos"), RSTD[:], ALU.mult)
            dve.tensor_tensor(SINR, tab("sin"), RSTD[:], ALU.mult)
            dve.drain()
            rope_k(0)
            rope_q(0)
            split_lo(base, 3)
            low_k(0)
            low_q(0)
            normed_v(0, 2, 0)

            def pair_step(m, r):
                j = 2 * m + r
                c = 3 * (r + 1)
                maxima(j, "dilated")
                divide(j)
                split_lo(base + 3 * m, c + 1)
                rope_k(j + 1)
                split_lo(base + 3 * m, c + 2)
                low_k(j + 1)
                rope_q(j + 1)
                heads_low(j)
                split_lo(base + 3 * m, c + 3)
                low_q(j + 1)
                normed_v(m, c + 2, c % 2)

            with dve.Fori(0, PAIRS // 2 - 1) as m:
                for r in range(2):
                    pair_step(m, r)
            pair_step(PAIRS // 2 - 1, 0)
            maxima(PAIRS - 1, "dilated")
            divide(PAIRS - 1)
            heads_low(PAIRS - 1)
            for k in range(DC):
                split_lo(0, O_OUT + k + 1)
            add_out(2, O_OUT + DC - 1, gain="ffn_norm_g1", fill=H_FILL["f1"])
            conv_ffn(1, 3, None, None)

            squares_part(NBF, FIRST, "final")
            split_lo(0, L_IN[0] + 1)
            spread("final")
            rows(X, X, "final_norm_g", H_FILL["in0"])

            def layer_norm(nm, fill, slot=None):
                for n in range(FIRST + 1, DC):
                    dve.wait_ge(x_ready, XR[nm] + n + 1)
                    if n > FIRST + 1:
                        dve.drain()
                    ins = dve.tensor_tensor(MU[:], X[:, FIRST, :] if n == FIRST + 1 else MU[:], X[:, n, :], ALU.add)
                ins.then_inc(n_part, 1)
                if slot:
                    split_lo(0, slot)
                mean(0, D, n_add, ADD[nm] + FIRST + 1)
                centre(X, range(DC))
                squares_part(NB2, FIRST, nm)
                spread(nm)
                gain, bias = nm.replace("_", "_g"), nm.replace("_", "_b")
                for n in range(DC + 1):
                    if n < DC:
                        dve.scalar_tensor_tensor(NB2[:, n, :], X[:, n, :], vec(gain, n), RSTD[:], ALU.mult, ALU.mult)\
                           .then_inc(n_row, 1)
                    if n and fill is not None:
                        dve.wait_ge(h_hi, fill + n)
                        dve.scalar_tensor_tensor(HL[:, n - 1, :], NB2[:, n - 1, :], vec(bias, n - 1), HH[:, n - 1, :].bitcast(F32),
                                                 ALU.add, ALU.subtract).then_inc(h_lo, 1)

            def mix_layer(l):
                z0 = L_IN[l]

                def lo(s):
                    split_lo(0, z0 + s)

                def kept(s):
                    dve.wait_ge(z_kept, Z_TILES * l + s + 1)

                def gate_logs():
                    dve.wait_ge(g_soft, l + 1)
                    ls = LS[:].rearrange("p (a b) c -> p a (b c)", a=2)
                    dve.scalar_tensor_tensor(ls, PS[:, 2:4, 0:4 * GK], 0.0, ls, ALU.min, ALU.subtract).then_inc(g_ls, 1)

                def chunked(x):
                    return x.rearrange("p a (c t) -> p a c t", t=GLA_CHUNK)

                def from_end():
                    dve.wait_ge(g_grow, l + 1)
                    for a in range(2):
                        bc = chunked(BC[:])[:, a]
                        ends = bc[:, :, GLA_CHUNK - 1:GLA_CHUNK].to_broadcast([GK, GLA_CHUNKS, GLA_CHUNK])
                        ins = dve.tensor_tensor(chunked(GB[:])[:, a], ends, bc, ALU.subtract)
                    ins.then_inc(g_diff, 1)

                def decay_queries():
                    kept(Z_GQ + 1)
                    q = ZT[0:GK, Z_GQ:Z_GQ + 2, :]
                    dve.scalar_tensor_tensor(q, q, GLA_DK ** -0.5, GA[:], ALU.mult, ALU.mult).then_inc(g_q, 1)

                def decay_keys():
                    kept(Z_GK + 1)
                    dve.wait_ge(g_end, l + 1)
                    dve.tensor_tensor(GB[:], ZT[0:GK, Z_GK:Z_GK + 2, :], GB[:], ALU.mult).then_inc(g_ke, 1)

                def inverse_keys():
                    dve.wait_ge(g_inv, l + 1)
                    k = ZT[0:GK, Z_GK:Z_GK + 2, :]
                    dve.tensor_tensor(k, k, GA[:], ALU.mult).then_inc(g_ki, 1)

                def turn(q):
                    dve.wait_ge(r_swap, 6 * l + q + 1)
                    z = ZT[:, SWAPS[q][0], :]
                    dve.tensor_tensor(z, z, tab("cos2"), ALU.mult)
                    dve.tensor_tensor(MU[:], PS[:, SWAPS[q][1], :], tab("sin2"), ALU.mult)
                    dve.drain()
                    dve.tensor_tensor(z, z, MU[:], ALU.add).then_inc(r_done, 1)
                    dve.drain()

                def low_queries(jj):
                    dve.wait_ge(k_high, 5 * l + 2 + jj)
                    for e in range(2):
                        own, other = slice(e * HD, (e + 1) * HD), slice((1 - e) * HD, (2 - e) * HD)
                        ins = dve.tensor_tensor(ZS[other, Z_QS[jj][e], :], ZT[own, Z_Q[jj], :],
                                                ZS[own, Z_QS[jj][e], :].bitcast(F32), ALU.subtract)
                    ins.then_inc(k_low, 1)

                def low_keys(b):
                    dve.wait_ge(k_own, 2 * l + b + 1)
                    for e in range(2):
                        own = slice(e * HD, (e + 1) * HD)
                        ins = dve.tensor_tensor(ZS[own, Z_KL[b], :], ZT[own, Z_KL[b], :],
                                                ZS[own, Z_KH[b][e], :].bitcast(F32), ALU.subtract)
                    ins.then_inc(k_low, 1)

                def blocks(kv):
                    kept(Z_KC + kv)
                    dve.wait_ge(m_loaded, M_LOADS * (l + 1))
                    if kv:
                        dve.wait_ge(c_hid, 2 * l + 1)
                    z = ZT[:, Z_KC + kv, :].rearrange("p (n s) -> p s n", s=CMP_STRIDE)
                    for part in range(2):
                        js = slice(part * CMP_STRIDE, (part + 1) * CMP_STRIDE)
                        pos = CP[:, kv, js].rearrange("p (s n) -> p s n", n=1).to_broadcast([P, CMP_STRIDE, N_CMP])
                        ins = dve.tensor_tensor(TB[:, js, :], z[:, :, part:part + N_CMP], pos, ALU.add)
                    ins.then_inc(c_tb, 1)

                def cmp_soft(jj):
                    u = NSA_PAIRS * l + jj
                    dve.wait_ge(c_s, u + 1)
                    if jj:
                        dve.wait_ge(c_t, u)
                    for e in range(2):
                        ins = dve.tensor_tensor(PC[:, e * TT:(e + 1) * TT, :].rearrange("p i n -> p (i n)"),
                                                PS[:, (4, 7)[e], 0:TT * N_CMP], tab("cmp_mask"), ALU.add)
                    ins.then_inc(c_sm, 1)
                    dve.drain()
                    dve.tensor_reduce(CM[:], PC[:], AX.X, ALU.min)
                    dve.drain()
                    dve.tensor_scalar(CM[:], CM[:], 1.0e20, None, ALU.min)
                    dve.drain()
                    least = CM[:].rearrange("p (q n) -> p q n", n=1).to_broadcast([P, 8, N_CMP])
                    dve.tensor_tensor(PC[:], PC[:], least, ALU.subtract).then_inc(c_sm, 1)

                def gate(b, jj, e):
                    return GT[:, :, 3 * (NSA_PAIRS * e + jj) + b]

                def cmp_divide(jj):
                    u = NSA_PAIRS * l + jj
                    dve.wait_ge(c_x, u + 1)
                    dve.tensor_reduce(CS[:], PC[:], AX.X, ALU.add)
                    dve.drain()
                    dve.tensor_scalar(CS[:], CS[:], 1.0e-30, None, ALU.max)
                    dve.drain()
                    dve.reciprocal(CS[:], CS[:])
                    dve.drain()
                    dve.wait_ge(g_sig, l + 1)
                    for e in range(2):
                        dve.tensor_tensor(CS[:, TT * e:TT * e + TT], CS[:, TT * e:TT * e + TT], gate(0, jj, e), ALU.mult)
                    dve.drain()
                    share = CS[:].rearrange("p (q n) -> p q n", n=1).to_broadcast([P, 8, N_CMP])
                    dve.tensor_tensor(PC[:], PC[:], share, ALU.mult).then_inc(c_p, 1)

                def cmp_add(jj):
                    dve.wait_ge(c_v, NSA_PAIRS * l + jj + 1)
                    o = ZT[:, NSA_OUT[jj], :]
                    dve.tensor_tensor(o, o, PS[:, 3, :], ALU.add).then_inc(c_acc, 1)
                    dve.drain()

                def unit(k, slot=None):
                    b, jj = divmod(k, NSA_PAIRS)
                    maxima(UNIT0[l] + k, "causal", PB2, NEGMAX2, SUM2)
                    if slot:
                        lo(slot)
                    divide(UNIT0[l] + k, lambda e: gate(1 + b, jj, e), PB2, SUM2, RCP2)

                def unit_add(k):
                    b, jj = divmod(k, NSA_PAIRS)
                    dve.wait_ge(at_o, UNIT0[l] + k + 1)
                    o = ZT[:, NSA_OUT[jj], :]
                    if b == 0:
                        ins = dve.tensor_copy(o, PS[:, 2, :])
                    else:
                        ins = dve.tensor_tensor(o, o, PS[:, 2, :], ALU.add)
                    ins.then_inc(u_acc, 1)
                    dve.drain()

                def states():
                    dve.wait_ge(g_ds, l + 1)
                    for c in range(GLA_CHUNKS - 1):
                        for a in range(2):
                            ds = PS[0:GK, 3 + c % 2, (4 * a + c // 2) * GLA_DV:(4 * a + c // 2 + 1) * GLA_DV]
                            if c == 0:
                                ins = dve.tensor_copy(ST[:, a, 1, :], ds)
                            else:
                                ins = dve.scalar_tensor_tensor(ST[:, a, c + 1, :], ST[:, a, c, :], DEC[:, a, c:c + 1], ds,
                                                               ALU.mult, ALU.add)
                        if c < GLA_CHUNKS - 2:
                            dve.drain()
                    ins.then_inc(g_st, 1)

                def mask_within(n):
                    dve.wait_ge(g_at, 3 * l + n + 1)
                    dve.wait_ge(m_zero, l + 1)
                    if n:
                        dve.wait_ge(g_o, 3 * l + n)
                    mask = tab("gla_mask").bitcast(I32).rearrange("p (a t) -> p a t", a=1).to_broadcast([P, TT, P])
                    for e in range(2):
                        ins = dve.copy_predicated(AT[:, e, :].rearrange("p (a t) -> p a t", a=TT), mask,
                                                  PS[:, 5 + e, :].rearrange("p (a t) -> p a t", a=TT))
                    ins.then_inc(g_am, 1)

                def gla_var(n):
                    dve.wait_ge(g_ms, 3 * l + n + 1)
                    dve.tensor_scalar(ZT[:, Z_OG + n, :], PS[:, 4, :], EPS, None, ALU.add).then_inc(g_var, 1)

                def gla_scale(n):
                    dve.wait_ge(g_sd, 3 * l + n + 1)
                    dve.reciprocal(RSTD[:], ZT[:, Z_OG + n, :])
                    dve.drain()
                    o = ZT[:, Z_GV + n, :]
                    dve.scalar_tensor_tensor(o, o, vec(f"gla_norm_g{l}", n), RSTD[:], ALU.mult, ALU.mult)
                    dve.drain()

                def gla_gate(n):
                    dve.wait_ge(g_sil, l + 1)
                    o = ZT[:, Z_GV + n, :]
                    dve.tensor_tensor(o, o, ZT[:, Z_OG + n, :], ALU.mult).then_inc(g_y, 1)

                def mix_low(c):
                    dve.wait_ge(h_hi, H_FILL[f"out{l}"] + c + 1)
                    dve.tensor_tensor(HL[:, c, :], mixed(c), HH[:, c, :].bitcast(F32), ALU.subtract).then_inc(h_lo, 1)

                def pool_scale(n):
                    dve.wait_ge(p_lin, 2 * l + n + 1)
                    dve.tensor_scalar(PU[:, n, POOL_PAD:], PS[:, (4, 7)[n], :], vec(f"pool_scale{l}", n), None, ALU.mult)\
                       .then_inc(p_y, 1)

                lo(2)
                lo(3)
                turn(0)
                blocks(0)
                lo(4)
                gate_logs()
                lo(5)
                from_end()
                lo(6)
                decay_keys()
                blocks(1)
                lo(7)
                decay_queries()
                inverse_keys()
                lo(8)
                lo(9)
                lo(10)
                lo(11)
                mask_within(0)
                states()
                lo(12)
                mask_within(1)
                turn(1)
                lo(13)
                low_keys(0)
                mask_within(2)
                gla_var(0)
                turn(2)
                lo(14)
                low_queries(0)
                gla_var(1)
                turn(3)
                gla_var(2)
                unit(0, 15)
                low_queries(1)
                gla_scale(0)
                unit_add(0)
                cmp_soft(0)
                unit(1, 16)
                cmp_divide(0)
                unit_add(1)
                turn(4)
                cmp_soft(1)
                low_queries(2)
                lo(17)
                unit(2, 18)
                cmp_divide(1)
                unit_add(2)
                cmp_add(0)
                turn(5)
                lo(19)
                low_keys(1)
                unit(3, 20)
                gla_scale(1)
                unit_add(3)
                cmp_soft(2)
                cmp_add(1)
                unit(4, 21)
                cmp_divide(2)
                gla_scale(2)
                unit_add(4)
                pool_scale(0)
                pool_scale(1)
                unit(5, 22)
                unit_add(5)
                cmp_add(2)
                for c in range(4):
                    mix_low(c)
                lo(23)
                mix_low(4)
                for n in range(3):
                    gla_gate(n)
                for c in range(5, DC):
                    mix_low(c)
                for k in range(2, DC + 1):
                    lo(Z_TILES + k)
                add_out(4 + 3 * l, z0 + Z_TILES + DC - 1, ALPHA)

            def square_ffn(l):
                for half in range(2):
                    up = L_IN[l] + Z_TILES + DC + half * 2 * F2H
                    done = F2C * l + F2H * half
                    with dve.Fori(0, F2H // 2) as i:
                        for b in range(2):
                            dve.wait_ge(q_relu, done + 2 * i + b + 1)
                            dve.tensor_tensor(SB[:, b, :], RB[:, b, :], RB[:, b, :], ALU.mult).then_inc(q_sq, 1)
                            split_lo(up // 2 + i, b + 2)
                            dve.wait_ge(q_hi, done + 2 * i + b + 1)
                            dve.tensor_tensor(ML2[:, bass.ds(2 * i + b, 1), :], SB[:, b, :],
                                              MH2[:, bass.ds(2 * i + b, 1), :].bitcast(F32), ALU.subtract).then_inc(q_lo, 1)
                    last = l == DEPTH2 - 1 and half == 1
                    with dve.Fori(1, F2H // 2) as i:
                        for b in range(2):
                            split_lo((up + F2H) // 2 + i, b)
                    if not last:
                        split_lo((up + F2H) // 2 + F2H // 2, 0)
                    add_out(5 + 3 * l + half, up + 2 * F2H - 1, None if half else ALPHA)
                    if not half:
                        split_lo((up + F2H) // 2 + F2H // 2, 1)

            for l in range(DEPTH2):
                mix_layer(l)
                layer_norm(f"ln1_{l}", H_FILL[f"up{l}"], L_IN[l] + Z_TILES + DC + 1)
                square_ffn(l)
                if l < DEPTH2 - 1:
                    layer_norm(f"ln2_{l}", H_FILL[f"in{l + 1}"], L_IN[l + 1] + 1)
                else:
                    layer_norm(f"ln2_{l}", None)


def _columns(v):
    return np.asarray(v).reshape(-1, P).T


def _by_columns(w):
    k, n = w.shape
    return w.reshape(k // P, P, n // P, P).transpose(2, 1, 0, 3).reshape(-1, D)


def lay_out(a):
    w_in = a["even_w_in"][0]
    za, zb = w_in[:, :D], w_in[:, D:]
    pairs = [np.concatenate([zb[:, n * P:(n + 1) * P], zb[:, HALF + n * P:HALF + (n + 1) * P]], 1) for n in range(HC)]
    stream = [_by_columns(np.concatenate(pairs + [za[:, HALF:], za[:, :HALF]], 1)), a["even_w_out"][0]]

    def ffn(l):
        up = a["ffn_w_up"][l]
        both = np.stack([up[:, :FF].reshape(D, FC, P), up[:, FF:].reshape(D, FC, P)], 2).reshape(D, 2 * FF)
        return [_by_columns(both), a["ffn_w_down"][l]]

    stream += ffn(0)
    qkv = a["odd_w_qkv"][0].reshape(D, 3, PAIRS, P)[:, [1, 0, 2]].transpose(0, 2, 1, 3).reshape(D, 3 * D)
    stream += [_by_columns(qkv), a["odd_w_o"][0]]
    stream += ffn(1)
    for l in range(DEPTH2):
        w = a["w_in_2"][l]
        at = np.cumsum([0, 384, 768, 18, 192, 192, 384, 16, 384, 256])
        q, kv, gates, gq, gk, gv, rank, og, pu = (w[:, at[n]:at[n + 1]] for n in range(9))
        none = np.zeros((D, P), np.float32)
        first = np.concatenate([rank, none[:, :GATE_ROW - RANK], gates, none[:, :P - GATE_ROW - gates.shape[1]]], 1)
        kv = kv.reshape(D, 6, P)
        heads = q.reshape(D, 2, NSA_PAIRS, HD).transpose(0, 2, 1, 3).reshape(D, -1)
        threes = [np.concatenate([g[:, n * GK:(n + 1) * GK], none[:, :P - GK]], 1) for g in (gk, gq) for n in range(2)]
        head = [heads[:, n * P:(n + 1) * P] for n in range(NSA_PAIRS)]
        cols = np.concatenate([first, kv[:, 0], kv[:, 1], *threes, gv, kv[:, 2], kv[:, 3], head[0], head[1], pu[:, :P],
                               head[2], pu[:, P:], kv[:, 4], kv[:, 5], og], 1)
        w_out = a["w_out_2"][l]
        nsa = w_out[:384].reshape(2, NSA_PAIRS, HD, D).transpose(1, 0, 2, 3).reshape(-1, D)
        up, down = _by_columns(a["w_up_2"][l]), a["w_down_2"][l]
        half = F2H * P
        gla, pool = w_out[384:768], w_out[768:]
        stream += [_by_columns(cols), nsa[:2 * P], pool, nsa[2 * P:], gla, up[:half], down[:half], up[half:], down[half:]]
    vecs = [_columns(a["even_norm_g"][0]), _columns(a["even_b_in"][0]), _columns(a["even_v_ln_g"][0]),
            _columns(a["even_v_ln_b"][0]),
            a["even_conv_w"][0].reshape(TAPS, HC, P).transpose(2, 1, 0).reshape(P, -1),
            _columns(a["even_conv_b"][0]), _columns(a["even_conv_ln_g"][0]), _columns(a["even_conv_ln_b"][0]),
            _columns(a["odd_norm_g"][0]), _columns(a["final_norm_g"])]
    for l in range(2):
        taps = np.concatenate([a["ffn_conv_w"][l], a["ffn_conv_b"][l][None]], 0)
        vecs += [_columns(a["ffn_norm_g"][l]),
                 taps.reshape(4, 2, FC, P).transpose(3, 2, 1, 0).reshape(P, -1)]
    for l in range(DEPTH2):
        vecs += [_columns(a[n][l]) for n in ("gla_norm_g_2", "pool_scale_2", "ln1_g_2", "ln1_b_2", "ln2_g_2", "ln2_b_2")]
    feeds = {
        "wstream": np.concatenate(stream, 0),
        "xt": a["x"][0].T.reshape(DC, P, T).transpose(1, 0, 2),
        "vecs": np.concatenate(vecs, 1),
        "tables": make_tables(),
        "spatial_w": a["even_w_s"][0].transpose(2, 0, 1),
        "spatial_b": np.repeat(a["even_b_s"][0].reshape(HC, 2, P), HD, 1).transpose(1, 0, 2),
    }
    blocks = np.zeros((DEPTH2, P, 2, P), np.float32)
    second = np.zeros((DEPTH2, P, 2, P), np.float32)
    for g in range(2):
        r = slice(g * HD, (g + 1) * HD)
        for n in range(2):
            blocks[:, r, n, r] = a["pool_w_2"][:, 2 * n + g]
            second[:, r, n, r] = a["cmp_w2_2"][:, n]
    w1 = a["cmp_w1_2"].reshape(DEPTH2, 2, CMP_BLOCK, HD, HD).transpose(0, 3, 1, 2, 4)
    pos = a["cmp_pos_2"].transpose(0, 3, 1, 2)
    feeds |= {
        "gate_w": np.concatenate([a["gla_w_gate2_2"], a["gla_b_gate_2"][:, None]], 1),
        "pool_w": blocks, "cmp_w2": second,
        "cmp_w1": np.concatenate([w1, w1], 1), "cmp_p": np.concatenate([pos, pos], 1),
    }
    return {n: np.ascontiguousarray(v) for n, v in feeds.items()}


def kernel(**inputs):
    import concourse.bacc as bacc
    from concourse.bass_utils import run_bass_kernel_spmd

    feeds = lay_out({n: np.asarray(v) for n, v in inputs.items()})
    nc = bacc.Bacc("TRN2", target_bir_lowering=False, num_devices=1)
    aps = {n: nc.dram_tensor(n, v.shape, F32, kind="ExternalInput").ap() for n, v in feeds.items()}
    out = nc.dram_tensor("out", (P, DC, T), F32, kind="ExternalOutput").ap()
    program(nc, **aps, out=out)
    result = run_bass_kernel_spmd(nc, [feeds], core_ids=[0]).results[0]["out"]
    return result.transpose(1, 0, 2).reshape(D, T).T[None]
```
